# Optimizing a Trainium2 kernel written in Bass

```python
import jax, jax.numpy as jnp
from jax import lax
import numpy as np

D_MODEL = 1024
BATCH = 1
SEQ = 512
DEPTH = 2

CHUNK = 64
N_MIXERS = 4
GROUP_W = D_MODEL // N_MIXERS
ATT_HEAD_DIM = 64
ATT_HEADS = GROUP_W // ATT_HEAD_DIM
ROPE_DIM = ATT_HEAD_DIM // 4
ROPE_THETA = 500000.0
IDX_HEADS = 4
IDX_DIM = 32
IDX_ROPE_DIM = IDX_DIM // 4
TOPK_MAX = 256
Q_BLOCK = 128
CONV_WIDTH = 31
CONV_GROUPS = 4
POOL_WINDOWS = (2, 4, 8, 16)
POOL_CH = GROUP_W // 4
SGU_CHUNK = 128
SGU_HEADS = 4
SGU_HEAD_W = GROUP_W // SGU_HEADS
N_EXP_GROUPS = 4
EXP_PER_GROUP = 8
N_EXPERTS = N_EXP_GROUPS * EXP_PER_GROUP
EXPERT_FF = 512
MOE_TOPK = 2
MOE_BLOCK = 128
EPS = 1e-6
IN_SPLITS = (GROUP_W, GROUP_W, GROUP_W, IDX_HEADS * IDX_DIM, IDX_DIM, IDX_HEADS, 2 * GROUP_W, GROUP_W, 2 * GROUP_W)
D_IN = 8 * GROUP_W + IDX_HEADS * IDX_DIM + IDX_DIM + IDX_HEADS

kernel_name = "hybrid_chunk_causal_parallel_heads_hmoe"

def _rms(x, g):
    xf = x.astype(jnp.float32)
    y = xf * lax.rsqrt(jnp.mean(xf * xf, axis=-1, keepdims=True) + EPS)
    return y.astype(x.dtype) * g

def _ln(x, g, b):
    xf = x.astype(jnp.float32)
    mu = jnp.mean(xf, axis=-1, keepdims=True)
    var = jnp.mean(jnp.square(xf - mu), axis=-1, keepdims=True)
    return ((xf - mu) * lax.rsqrt(var + EPS)).astype(x.dtype) * g + b

def _rope_tables(positions, rot_dim, dtype):
    half = rot_dim // 2
    inv = jnp.power(jnp.float32(ROPE_THETA), -2.0 * jnp.arange(half, dtype=jnp.float32) / rot_dim)
    ang = positions.astype(jnp.float32)[..., None] * inv
    return jnp.cos(ang).astype(dtype)[:, :, None, :], jnp.sin(ang).astype(dtype)[:, :, None, :]

def _partial_rope(x, cos, sin):
    half = cos.shape[-1]
    x1, x2, rest = x[..., :half], x[..., half:2 * half], x[..., 2 * half:]
    return jnp.concatenate([x1 * cos - x2 * sin, x2 * cos + x1 * sin, rest], axis=-1)

def _dsa_mixer(q, k, v, iq, ik, iw, cos_a, sin_a, cos_i, sin_i, q_norm, k_norm):
    B, S = q.shape[:2]
    q = _partial_rope(_rms(q.reshape(B, S, ATT_HEADS, ATT_HEAD_DIM), q_norm), cos_a, sin_a)
    k = _partial_rope(_rms(k.reshape(B, S, ATT_HEADS, ATT_HEAD_DIM), k_norm), cos_a, sin_a)
    v = v.reshape(B, S, ATT_HEADS, ATT_HEAD_DIM)
    iq = _partial_rope(iq.reshape(B, S, IDX_HEADS, IDX_DIM), cos_i, sin_i)
    ik = _partial_rope(ik[:, :, None, :], cos_i, sin_i)[:, :, 0, :]
    iw = iw * (IDX_HEADS ** -0.5)
    topk = min(TOPK_MAX, S // 4)
    n_blk = S // Q_BLOCK
    key_pos = jnp.arange(S)

    def to_blocks(a):
        return a.reshape(B, n_blk, Q_BLOCK, *a.shape[2:]).swapaxes(0, 1)

    def block(args):
        qb, iqb, iwb, bi = args
        q_pos = bi * Q_BLOCK + jnp.arange(Q_BLOCK)
        key_end = (q_pos // CHUNK + 1) * CHUNK
        admissible = key_pos[None, :] < key_end[:, None]
        dots = jnp.einsum('bqhd,bsd->bqhs', iqb, ik) * (IDX_DIM ** -0.5)
        score = jnp.einsum('bqhs,bqh->bqs', jax.nn.relu(dots), iwb).astype(jnp.float32)
        score = jnp.where(admissible[None], score, -jnp.inf)
        top_val, top_idx = lax.top_k(score, topk)
        valid = jnp.isfinite(top_val)
        k_sel = jax.vmap(lambda kb, ib: kb[ib])(k, top_idx)
        v_sel = jax.vmap(lambda vb, ib: vb[ib])(v, top_idx)
        logits = jnp.einsum('bqhd,bqkhd->bqhk', qb, k_sel).astype(jnp.float32) * (ATT_HEAD_DIM ** -0.5)
        logits = jnp.where(valid[:, :, None, :], logits, -jnp.inf)
        p = jax.nn.softmax(logits, axis=-1).astype(v.dtype)
        o = jnp.einsum('bqhk,bqkhd->bqhd', p, v_sel)
        return o.reshape(B, Q_BLOCK, GROUP_W)

    out = lax.map(block, (to_blocks(q), to_blocks(iq), to_blocks(iw), jnp.arange(n_blk)))
    return out.swapaxes(0, 1).reshape(B, S, GROUP_W)

def _conv_module(a, gate, conv_w, conv_b, ln_g, ln_b, pw_w, pw_b):
    B, S, C = a.shape
    y = a * jax.nn.sigmoid(gate)
    y = jnp.pad(y, ((0, 0), (CONV_WIDTH - 1, 0), (0, 0)))
    y = lax.conv_general_dilated(y, conv_w[:, None, :], window_strides=(1,), padding='VALID',
                                 dimension_numbers=('NWC', 'WIO', 'NWC'), feature_group_count=C) + conv_b
    y = _ln(y.reshape(B, S, CONV_GROUPS, C // CONV_GROUPS),
            ln_g.reshape(CONV_GROUPS, -1), ln_b.reshape(CONV_GROUPS, -1)).reshape(B, S, C)
    return jax.nn.silu(y) @ pw_w + pw_b

def _pool_mixer(p, pool_w, pool_b, pool_scale):
    B, S, C = p.shape
    pg = p.reshape(B, S, len(POOL_WINDOWS), POOL_CH)
    cs = lax.cumsum(pg.astype(jnp.float32), axis=1)
    count = jnp.arange(1, S + 1, dtype=jnp.float32)
    means = []
    for i, w in enumerate(POOL_WINDOWS):
        c_i = cs[:, :, i]
        prev = jnp.pad(c_i, ((0, 0), (w, 0), (0, 0)))[:, :S]
        means.append((c_i - prev) / jnp.minimum(count, w)[None, :, None])
    pooled = jnp.stack(means, axis=2).astype(p.dtype) - pg
    y = jnp.einsum('bsgc,gcd->bsgd', pooled, pool_w) + pool_b
    return y.reshape(B, S, C) * pool_scale

def _sgu_mixer(u, v, ln_g, ln_b, sgu_w, sgu_b):
    B, S, C = u.shape
    n = S // SGU_CHUNK
    vc = _ln(v, ln_g, ln_b).reshape(B, n, SGU_CHUNK, SGU_HEADS, SGU_HEAD_W)
    causal = jnp.tril(jnp.ones((SGU_CHUNK, SGU_CHUNK), dtype=bool))
    w = jnp.where(causal[None], sgu_w, 0)
    mixed = jnp.einsum('hts,bnshc->bnthc', w, vc) + sgu_b.T[None, None, :, :, None]
    return u * mixed.reshape(B, S, C)

def _hier_moe(h, w_rg, b_rg, w_re, b_re, w_gate, w_up, w_down):
    N, D = h.shape
    p_grp = jax.nn.softmax((h @ w_rg + b_rg).astype(jnp.float32), axis=-1)
    g_idx = jnp.argmax(p_grp, axis=-1).astype(jnp.int32)
    p_sel = jnp.take_along_axis(p_grp, g_idx[:, None], axis=1)
    e_logits = jnp.einsum('nd,dge->nge', h, w_re) + b_re
    e_logits = jnp.take_along_axis(e_logits, g_idx[:, None, None], axis=1)[:, 0].astype(jnp.float32)
    top_val, top_j = lax.top_k(e_logits, MOE_TOPK)
    gates = (p_sel * jax.nn.softmax(top_val, axis=-1)).astype(h.dtype)
    expert = g_idx[:, None] * EXP_PER_GROUP + top_j.astype(jnp.int32)
    M = N * MOE_TOPK
    e_flat = expert.reshape(-1)
    tok_flat = jnp.repeat(jnp.arange(N, dtype=jnp.int32), MOE_TOPK)
    g_flat = gates.reshape(-1)
    order = jnp.argsort(e_flat)
    e_s, tok_s, g_s = e_flat[order], tok_flat[order], g_flat[order]
    counts = jnp.zeros(N_EXPERTS, jnp.int32).at[e_flat].add(1)
    padded = (counts + MOE_BLOCK - 1) // MOE_BLOCK * MOE_BLOCK
    pad_end = jnp.cumsum(padded)
    pad_start = pad_end - padded
    start = jnp.cumsum(counts) - counts
    dest = pad_start[e_s] + jnp.arange(M, dtype=jnp.int32) - start[e_s]
    n_blocks = (M + N_EXPERTS * (MOE_BLOCK - 1) + MOE_BLOCK - 1) // MOE_BLOCK
    rows = n_blocks * MOE_BLOCK
    row_tok = jnp.zeros(rows, jnp.int32).at[dest].set(tok_s)
    row_gate = jnp.zeros(rows, h.dtype).at[dest].set(g_s)
    block_expert = jnp.minimum(
        jnp.searchsorted(pad_end, jnp.arange(n_blocks, dtype=jnp.int32) * MOE_BLOCK, side='right'),
        N_EXPERTS - 1)

    def expert_block(args):
        toks, gts, e = args
        xb = h[toks]
        hid = jax.nn.silu(xb @ w_gate[e]) * (xb @ w_up[e])
        return (hid @ w_down[e]) * gts[:, None]

    y_rows = lax.map(expert_block, (row_tok.reshape(n_blocks, MOE_BLOCK),
                                    row_gate.reshape(n_blocks, MOE_BLOCK), block_expert))
    return jnp.zeros_like(h).at[row_tok].add(y_rows.reshape(rows, D))

def setup_inputs(seed: int = 0) -> dict:
    key = jax.random.key(seed)
    it = iter(jax.random.split(key, 32))
    L, D, G, F = DEPTH, D_MODEL, GROUP_W, EXPERT_FF

    def nrm(shape, scale):
        return jax.random.normal(next(it), shape, jnp.float32) * scale

    def gain(shape):
        return 1.0 + 0.02 * jax.random.normal(next(it), shape, jnp.float32)

    x = nrm((BATCH, SEQ, D), 1.0)
    c = nrm((BATCH, D), 1.0)
    offset = jax.random.randint(next(it), (BATCH, 1), 0, 1024, dtype=jnp.int32)
    positions = (jnp.arange(SEQ, dtype=jnp.int32)[None, :] + offset).astype(jnp.int32)
    return {
        "x": x, "c": c, "positions": positions,
        "w_ada": nrm((L, D, 6 * D), D ** -0.5), "b_ada": nrm((L, 6 * D), 0.01),
        "norm1": gain((L, D)), "w_in": nrm((L, D, D_IN), D ** -0.5),
        "q_norm": gain((L, ATT_HEAD_DIM)), "k_norm": gain((L, ATT_HEAD_DIM)),
        "conv_w": nrm((L, CONV_WIDTH, G), CONV_WIDTH ** -0.5), "conv_b": nrm((L, G), 0.01),
        "conv_ln_g": gain((L, G)), "conv_ln_b": nrm((L, G), 0.01),
        "conv_pw_w": nrm((L, G, G), G ** -0.5), "conv_pw_b": nrm((L, G), 0.01),
        "pool_w": nrm((L, len(POOL_WINDOWS), POOL_CH, POOL_CH), POOL_CH ** -0.5),
        "pool_b": nrm((L, len(POOL_WINDOWS), POOL_CH), 0.01), "pool_scale": gain((L, G)),
        "sgu_ln_g": gain((L, G)), "sgu_ln_b": nrm((L, G), 0.01),
        "sgu_w": nrm((L, SGU_HEADS, SGU_CHUNK, SGU_CHUNK), SGU_CHUNK ** -0.5),
        "sgu_b": gain((L, SGU_HEADS, SGU_CHUNK)),
        "out_norm": gain((L, D)), "w_out": nrm((L, D, D), D ** -0.5),
        "norm2": gain((L, D)),
        "w_rg": nrm((L, D, N_EXP_GROUPS), D ** -0.5), "b_rg": nrm((L, N_EXP_GROUPS), 0.01),
        "w_re": nrm((L, D, N_EXP_GROUPS, EXP_PER_GROUP), D ** -0.5),
        "b_re": nrm((L, N_EXP_GROUPS, EXP_PER_GROUP), 0.01),
        "w_gate": nrm((L, N_EXPERTS, D, F), D ** -0.5), "w_up": nrm((L, N_EXPERTS, D, F), D ** -0.5),
        "w_down": nrm((L, N_EXPERTS, F, D), F ** -0.5),
    }

def reference(x, c, positions, w_ada, b_ada, norm1, w_in, q_norm, k_norm, conv_w, conv_b,
              conv_ln_g, conv_ln_b, conv_pw_w, conv_pw_b, pool_w, pool_b, pool_scale,
              sgu_ln_g, sgu_ln_b, sgu_w, sgu_b, out_norm, w_out, norm2, w_rg, b_rg, w_re, b_re,
              w_gate, w_up, w_down):
    B, S, D = x.shape
    split_points = np.cumsum(IN_SPLITS)[:-1].tolist()
    cos_a, sin_a = _rope_tables(positions, ROPE_DIM, x.dtype)
    cos_i, sin_i = _rope_tables(positions, IDX_ROPE_DIM, x.dtype)
    c_act = jax.nn.silu(c)
    for l in range(DEPTH):
        mod = c_act @ w_ada[l] + b_ada[l]
        shift1, scale1, gate1, shift2, scale2, gate2 = [m[:, None, :] for m in jnp.split(mod, 6, axis=-1)]
        h = _rms(x, norm1[l]) * (1 + scale1) + shift1
        proj = h @ w_in[l]
        qa, ka, va, iqa, ika, iwa, b_in, c_in, d_in = jnp.split(proj, split_points, axis=-1)
        b_a, b_g = jnp.split(b_in, 2, axis=-1)
        d_u, d_v = jnp.split(d_in, 2, axis=-1)
        o_a = _dsa_mixer(qa, ka, va, iqa, ika, iwa, cos_a, sin_a, cos_i, sin_i, q_norm[l], k_norm[l])
        o_b = _conv_module(b_a, b_g, conv_w[l], conv_b[l], conv_ln_g[l], conv_ln_b[l], conv_pw_w[l], conv_pw_b[l])
        o_c = _pool_mixer(c_in, pool_w[l], pool_b[l], pool_scale[l])
        o_d = _sgu_mixer(d_u, d_v, sgu_ln_g[l], sgu_ln_b[l], sgu_w[l], sgu_b[l])
        mix = jnp.concatenate([o_a, o_b, o_c, o_d], axis=-1).reshape(B, S, N_MIXERS, GROUP_W)
        mix = _rms(mix, out_norm[l].reshape(N_MIXERS, GROUP_W)).reshape(B, S, D)
        x = x + gate1 * (mix @ w_out[l])
        h2 = _rms(x, norm2[l]) * (1 + scale2) + shift2
        y = _hier_moe(h2.reshape(B * S, D), w_rg[l], b_rg[l], w_re[l], b_re[l], w_gate[l], w_up[l], w_down[l])
        x = x + gate2 * y.reshape(B, S, D)
    return x


_drawn_inputs = setup_inputs


def setup_inputs(seed=0):
    import zlib

    import numpy as np

    out = dict(_drawn_inputs(seed))
    spreads = {}
    factors = {'q_norm': 7.542, 'k_norm': 4.451, 'conv_ln_b': 4.254, 'sgu_ln_g': 3.103, 'sgu_ln_b': 7.388}
    for name, (base, spread) in spreads.items():
        noise = np.random.default_rng([zlib.crc32(name.encode()), seed]).standard_normal(out[name].shape)
        drawn = base * np.exp(spread * noise) if base else spread * noise
        out[name] = __import__('jax').numpy.asarray(drawn.astype(out[name].dtype))
    for name, factor in factors.items():
        out[name] = (out[name] * factor).astype(out[name].dtype)
    return out
```

```python
from contextlib import ExitStack

import numpy as np

import concourse.bass as bass
from concourse import mybir

F32 = mybir.dt.float32
I32 = mybir.dt.int32
U32 = mybir.dt.uint32
ALU = mybir.AluOpType
ACT = mybir.ActivationFunctionType
AX = mybir.AxisListType

P = 128
D = 1024
S = 512
DEPTH = 2
T = S // P
K = D // P
G = D // 4
HEADS, HD = 4, 64
ROT = HD // 8
IH, ID = 4, 32
IROT = ID // 8
CHUNK = 64
TOPK = min(256, S // 4)
TAPS = 31
SGU_H = 4
NG, EPG = 4, 8
E = NG * EPG
FF = 512
EPS = 1e-6
THETA = 500000.0
D_IN = 8 * G + IH * ID + ID + IH

C_Q, C_V, C_CONV = 0, 2 * G, 3 * G + IH * ID + ID + IH
C_POOL, C_SGU = C_CONV + 2 * G, C_CONV + 3 * G
NA = C_CONV - C_V

R_MOD, R_N1, R_N2, R_ON, R_CB, R_LG, R_LB, R_PB, R_QB, R_QS = 0, 48, 56, 64, 72, 74, 76, 78, 80, 82
NROW = 84
SHIFT1, SCALE1, GATE1, SHIFT2, SCALE2, GATE2 = range(6)

RING = 6
ADA_COLS = 512
ADA_CHUNKS = 6 * D // ADA_COLS
N_IN, N_OUT = 5, 2
N_PRE = N_IN + N_OUT
N_CHUNKS = N_PRE + 3 * E

OVER_BLOCKS = 7
ROWS = 2 * S + P
NEG = -3.0e38
GONE = -3.4e38
MASK = -1.0e30
MAGIC = 12582912.0
TWO_PI = 2 * np.pi
PI1 = 6.28125
PI2 = float(np.float32(TWO_PI - PI1) - np.float32(TWO_PI - PI1) % np.float32(2.0 ** -20))
PI3 = float(TWO_PI - PI1 - PI2)


def constants():
    p = np.arange(P)[:, None]
    j = np.arange(P)[None, :]
    parts = {
        "ident": (p == j),
        "mean256": np.full((P, P), 1.0 / G),
        "mean64": (p // 64 == j // 64) / 64.0,
        "upto": (p <= j),
        "before": (p < j),
        "ones": np.ones((P, P)),
        "mask0": np.where((p < CHUNK) & (j >= CHUNK), MASK, 0.0),
        "iota": np.broadcast_to(np.arange(E), (P, E)),
        "invf": np.broadcast_to(np.concatenate([
            np.power(np.float32(THETA), (-2.0 * np.arange(ROT, dtype=np.float32) / np.float32(2 * ROT))),
            np.power(np.float32(THETA), (-2.0 * np.arange(IROT, dtype=np.float32) / np.float32(2 * IROT))),
        ]), (P, ROT + IROT)),
        "eps": np.full((P, 1), EPS),
    }
    win = np.array([2, 4, 8, 16])
    own = np.stack([win[0 + (p[:, 0] // 64)], win[2 + (p[:, 0] // 64)]], 1)
    parts["invw"] = 1.0 / own
    first = np.minimum(np.arange(1, 17)[None, None, :], own[:, :, None])
    parts["invc"] = (1.0 / first).reshape(P, 32)
    parts["blk"] = np.broadcast_to(np.arange(OVER_BLOCKS), (P, OVER_BLOCKS))
    where, at = {}, 0
    for name, a in parts.items():
        where[name] = (at, at + a.shape[1])
        at += a.shape[1]
    return np.concatenate([np.asarray(a, np.float32) for a in parts.values()], 1), where


def build(nc, A, out, debug=None):
    ctx = ExitStack()
    cw = constants()[1]
    NCONST = max(b for _, b in cw.values())

    def sb(name, shape, dt=F32):
        return ctx.enter_context(nc.sbuf_tensor(name, shape, dt))

    sems = []

    def sem(name, cleared=True):
        q = ctx.enter_context(nc.semaphore(name))
        if cleared:
            sems.append(q)
        return q

    mod_dram = nc.dram_tensor("mod_scratch", [DEPTH * 48, P], F32, kind="Internal").ap()
    xs_dram = nc.dram_tensor("sorted_tokens", [ROWS, D], F32, kind="Internal").ap()
    ys_dram = nc.dram_tensor("sorted_outputs", [ROWS, D], F32, kind="Internal").ap()
    x_tok = A["x"].rearrange("b (t p) d -> p (b t) d", p=P)
    out_tok = out.rearrange("b (t p) d -> p (b t) d", p=P)
    ada_v = A["w_ada"].rearrange("l (k p) n -> l p k n", p=P)
    win_v = A["w_in"].rearrange("l (k p) n -> l p k n", p=P)
    wout_v = A["w_out"].rearrange("l (k p) n -> l p k n", p=P)
    wg_v = A["w_gate"].rearrange("l e (k p) n -> l e p k n", p=P)
    wu_v = A["w_up"].rearrange("l e (k p) n -> l e p k n", p=P)
    wd_v = A["w_down"].rearrange("l e (k p) n -> l e p k n", p=P)

    with ctx:
        cst = sb("cst", [P, NCONST])

        def c(name):
            a, b = cw[name]
            return cst[:, a:b]

        ident = c("ident")
        x = sb("x_resident", [P, T, D])
        ring = sb("ring", [P, RING, 4096])
        work = sb("work", [P, 2 * 4096 + 4752])
        hT = work[:, 0:4096].rearrange("p (k s) -> p k s", k=K)
        mixT = work[:, 4096:8192].rearrange("p (k s) -> p k s", k=K)
        xn = work[:, 4096:8192].rearrange("p (t d) -> p t d", t=T)
        tokA = work[:, 8192:8192 + T * NA].rearrange("p (t n) -> p t n", t=T)
        tokB = work[:, 8192 + T * NA:8192 + T * (NA + 512)].rearrange("p (t n) -> p t n", t=T)
        dv = work[:, 8192 + T * (NA + 512):].rearrange("p (t n) -> p t n", t=T)
        prob = work[:, 0:2048].rearrange("p (h n) -> p h n", h=HEADS)
        probT = work[:, 2048:3072].rearrange("p (b n) -> p b n", b=2)
        xT = [work[:, i * 1024:(i + 1) * 1024].rearrange("p (k s) -> p k s", k=K) for i in range(2)]
        sgate = work[:, 2048:2560]
        hid = work[:, 2560:3072]
        hidT = work[:, 3072:3584].rearrange("p (k s) -> p k s", k=4)
        xs = [work[:, 4096 + i * 1024:5120 + i * 1024] for i in range(2)]
        ybuf = [work[:, 6144 + i * 1024:7168 + i * 1024] for i in range(2)]
        got = [[work[:, 8192 + (2 * b + j) * 1024:9216 + (2 * b + j) * 1024] for j in range(2)] for b in range(2)]
        mrow = work[0:1, 0:DEPTH * 6 * D]
        score = sb("score", [P, 1152])
        modt = score[0:DEPTH * 48, 0:2 * P].rearrange("r (i p) -> r i p", i=2)
        crow = score[0:K, 2 * P:3 * P]
        ccol = sb("ccol", [P, K])
        posi = sb("posi", [P, T], I32)
        posf = sb("posf", [P, T])
        ang = sb("ang", [P, T, ROT + IROT])
        turn = sb("turn", [P, T, ROT + IROT])
        sn = sb("sn", [P, T, ROT + IROT])
        cs = sb("cs", [P, T, ROT + IROT])
        prow = sb("prow", [NROW, P])
        cwrow = sb("cwrow", [2 * TAPS, P])
        pcol = sb("pcol", [P, NROW])
        cwcol = sb("cwcol", [P, 2 * TAPS])
        scl = sb("scl", [P, 2, K])
        qkn = sb("qkn", [P, 2, HD])
        sgn = sb("sgn", [P, 2, G])
        sgb = sb("sgb", [P, 2, P])
        sgw = sb("sgw", [P, SGU_H, P])
        sgwT = sb("sgwT", [P, SGU_H, P])
        pww = sb("pww", [P, 2, G])
        plw = sb("plw", [P, 2, P])
        wr = sb("wr", [P, K, NG + E])
        rb = sb("rb", [P, NG + E])
        convin = sb("convin", [P, 2, TAPS - 1 + S])
        acc = mixT[:, 2:4, :]
        uT = mixT[:, 6:8, :]
        sig = uT
        poolin = sb("poolin", [P, 2, 16 + S])
        qT = work[:, 3072:4096].rearrange("p (h n) -> p h n", h=2)
        kT = tokB[:, :, 0:2 * P]
        sums_tile = sb("window_sums", [P, 2 * 2 * (16 + S)])
        wsum = [sums_tile[:, i * 2 * (16 + S):(i + 1) * 2 * (16 + S)].rearrange("p (h n) -> p h n", h=2)
                for i in range(2)]
        iqT, ikT = wsum[0][:, 0, 0:S], wsum[0][:, 1, 0:S]
        tokB_flat = work[:, 8192 + T * NA:8192 + T * (NA + 512)]
        ik4 = tokB_flat[:, 0:S].rearrange("p (t n) -> p t n", t=T)
        sq = sb("sq", [P, 2, S])
        relu = [tokB_flat[:, (1 + i) * S:(2 + i) * S] for i in range(2)]
        SC = [0, 0, 256, 640]
        g1b = convin[:, :, :].rearrange("p h n -> p (h n)")[:, 0:D]
        g2b = work[:, 0:D]
        small = sb("small", [P, 256])
        ss = small[:, 0:4]
        rs = small[:, 4:8]
        ssq = small[:, 8:40]
        rsq = small[:, 40:72]
        m8 = small[:, 72:80]
        mx = small[:, 80:84]
        nmx = small[:, 84:88]
        sums = small[:, 88:92]
        rsum = small[:, 92:96]
        bst = small[:, 96:120].rearrange("p (t n) -> p t n", t=T)
        bag = small[:, 120:128].rearrange("p (t n) -> p t n", t=T)
        rdv = small[:, 128:132]
        gidx = small[:, 132:136]
        gmax = small[:, 136:140]
        psel = small[:, 140:144]
        gates = small[:, 144:152].rearrange("p (j t) -> p j t", j=2)
        posr = small[:, 152:160].rearrange("p (j t) -> p j t", j=2)
        top8 = small[:, 160:192].rearrange("p (t n) -> p t n", t=T)
        topf = small[:, 192:224].rearrange("p (t n) -> p t n", t=T)
        ediff = small[:, 224:228]
        ropet = sq[:, :, :].rearrange("p h n -> p (h n)").rearrange("p (i t h r) -> p i t h r", i=4, t=T, h=8)
        sq_flat = sq[:, :, :].rearrange("p h n -> p (h n)")
        taken = [0]

        def late(*shape):
            n = int(np.prod(shape))
            a = taken[0]
            taken[0] += n
            assert taken[0] <= 4 * (16 + S)
            flat = sums_tile[:, a:a + n]
            if len(shape) == 2:
                return flat.rearrange("p (a b) -> p a b", a=shape[0])
            return flat.rearrange("p (a b c) -> p a b c", a=shape[0], b=shape[1])

        lg = late(T, NG + E)
        r4 = late(3, T, NG)
        el = late(T, E)
        oh = late(3, T, E)
        rank = late(T, E)
        rtmp = late(T, E)
        cnt = late(9, E)
        exc = late(4, E)
        ovm = late(3, OVER_BLOCKS, E)
        topi = sb("topi", [P, T, 8], U32)
        ovf = sb("ovf", [P, 2, OVER_BLOCKS])
        posu = sb("posu", [P, 2, T], U32)
        starti = sb("starti", [1, E], I32)
        ovi = sb("ovi", [1, 16], I32)

        bank = [ctx.enter_context(nc.psum_tensor(f"bank{i}", [P, 512], F32)) for i in range(8)]

        GB, UB, HB = bank[0], bank[1], bank[2]
        YB, XP = bank[3:5], bank[5:7]
        mix_sq_buf = [sq[:, :, :], wsum[1][:, :, 16:]]

        slot = [sem(f"slot{i}_loaded") for i in range(RING)]
        pe_done = sem("pe_done")
        act_evac = sem("act_evac")
        dve_evac = sem("dve_evac")
        act_step = sem("act_step")
        dve_step = sem("dve_step")
        pool_step = sem("pool_step")
        xs_in = [sem(f"xs_in{i}") for i in range(2)]
        zeroed = sem("zeroed", cleared=False)
        scattered = sem("scattered", cleared=False)
        got_in = [sem(f"got_in{i}", cleared=False) for i in range(2)]
        s = {name: sem(name) for name in (
            "consts_in", "x_in", "c_in", "pos_in", "bada_in", "mod_out", "mod_back", "rows_in", "taps_in",
            "norms_in", "sgu_in", "pw_in", "router_in", "gate1_in", "gate2_in", "y_written", "stored",
            "mod_done", "mod_evac", "c_silu", "turns_ready", "mod_sum",
            "rstd_done", "xn_done", "scl_ready", "conv_in", "idx_roped", "relu_free", "conv_done",
            "qk_ss", "qk_rstd", "qk_roped", "sgu_var", "sgu_rstd", "sgu_normed", "pool_in", "pooled", "exp_in",
            "exp_done", "prob_ready", "centered", "centered_sq", "conv_sd", "conv_normed", "swished", "mix_ready",
            "mix_sq", "mix_sd", "mix_normed", "x_added", "copied",
            "gexp_in", "gexp_out", "oh_ready", "routed",
            "gate_mm", "up_mm", "hid_tr", "down_mm", "xs_tr", "xt_ready", "silu_done", "hid_ready", "hidt_ready",
            "y_ready", "scaled", "combined")}

        def clear_semaphores():
            nums = sorted(q.num for q in sems)
            kept = [q.num for q in (zeroed, scattered, *got_in)]
            nc.all_engine_barrier()
            nc.gpsimd.sem_clear(range(nums[0], kept[0]))
            nc.gpsimd.sem_clear(range(kept[-1] + 1, nums[-1] + 1))
            nc.all_engine_barrier()

        def stepper(eng, done):
            n = [0]

            def step(ins):
                n[0] += 1
                ins.then_inc(done, 1)
                eng.wait_ge(done, n[0])
            return step

        HALF = ADA_CHUNKS // RING
        with nc.Block() as block:
            @block.sync
            def _(sp):
                sp.dma_start(cst[:, :], A["constants"]).then_inc(s["consts_in"], 16)
                with sp.Fori(0, DEPTH) as l:
                    with sp.Fori(0, HALF) as i:
                        for j in range(RING):
                            src = ada_v[l, :, :, bass.ds((i * RING + j) * ADA_COLS, ADA_COLS)]
                            dst = ring[:, j, :].rearrange("p (k n) -> p k n", k=K)
                            sp.wait_ge(s["mod_done"], (l * HALF + i) * RING + j + 1)
                            sp.dma_start(dst, src).then_inc(slot[j], 16)
                sp.dma_start(x[:, :, :], x_tok).then_inc(s["x_in"], 16)
                sp.wait_ge(s["x_in"], 16)

            @block.scalar
            def _(act):
                act.sem_inc(s["mod_evac"], RING)
                act.dma_start(crow[:, :], A["c"].rearrange("b (k p) -> (b k) p", p=P)).then_inc(s["c_in"], 16)
                act.dma_start(posi[:, :], A["positions"].rearrange("b (t p) -> p (b t)", p=P),
                              allow_slow_non_contiguous=True).then_inc(s["pos_in"], 16)
                act.dma_start(modt[:, 1, :], A["b_ada"].rearrange("l (r p) -> (l r) p", p=P))\
                   .then_inc(s["bada_in"], 16)
                act.wait_ge(s["c_in"], 16)
                act.activation(crow[:, :], crow[:, :], ACT.Silu).then_inc(s["c_silu"], 1)
                with act.Fori(0, DEPTH) as l:
                    with act.Fori(0, HALF) as i:
                        for j in range(RING):
                            at = act.snap(((l * HALF + i) * RING + j) * ADA_COLS)
                            act.wait_ge(s["mod_done"], (l * HALF + i) * RING + j + 1 + RING)
                            act.activation(mrow[:, bass.ds(at, ADA_COLS)], bank[j][0:1, :], ACT.Copy)\
                               .then_inc(s["mod_evac"], 1)
                act.wait_ge(s["mod_evac"], RING + DEPTH * ADA_CHUNKS)
                act.dma_start(mod_dram.rearrange("(a r) p -> a (r p)", a=1), mrow).then_inc(s["mod_out"], 16)
                act.wait_ge(s["mod_out"], 16)
                act.dma_start(modt[:, 0, :], mod_dram).then_inc(s["mod_back"], 16)
                act.wait_ge(s["mod_sum"], 1)
                act.dma_start(mod_dram, modt[:, 0, :]).then_inc(s["mod_out"], 16)
                act.wait_ge(s["turns_ready"], 1)
                act.activation(sn[:, :, :], ang[:, :, :], ACT.Sin)
                act.activation(cs[:, :, :], turn[:, :, :], ACT.Sin)
                act.wait_ge(s["mod_out"], 32)

            @block.vector
            def _(v):
                step = stepper(v, dve_step)
                v.memset(poolin[:, :, 0:16], 0.0)
                v.memset(plw[:, :, :], 0.0)
                v.wait_ge(s["consts_in"], 16)
                v.wait_ge(s["pos_in"], 16)
                nf = ROT + IROT
                step(v.tensor_copy(posf[:, :], posi[:, :]))
                step(v.tensor_tensor(ang[:, :, :], posf[:, :].unsqueeze(2).to_broadcast([P, T, nf]),
                                     c("invf").unsqueeze(1).to_broadcast([P, T, nf]), ALU.mult))
                step(v.tensor_scalar(turn[:, :, :], ang[:, :, :], 1.0 / TWO_PI, MAGIC, ALU.mult, ALU.add))
                step(v.tensor_scalar(turn[:, :, :], turn[:, :, :], MAGIC, None, ALU.subtract))
                for part in (PI1, PI2, PI3):
                    step(v.scalar_tensor_tensor(ang[:, :, :], turn[:, :, :], -part, ang[:, :, :],
                                                ALU.mult, ALU.add))
                step(v.tensor_scalar(ang[:, :, :], ang[:, :, :], 3.1415925, -3.1415925, ALU.min, ALU.max))
                step(v.tensor_scalar(turn[:, :, :], ang[:, :, :], -1.0, None, ALU.mult))
                step(v.tensor_tensor(turn[:, :, :], turn[:, :, :], ang[:, :, :], ALU.min))
                v.tensor_scalar(turn[:, :, :], turn[:, :, :], float(np.pi / 2), None, ALU.add)\
                    .then_inc(s["turns_ready"], 1)
                v.wait_ge(pe_done, 1)
                v.tensor_copy(ccol[:, :], bank[7][:, 0:K]).then_inc(dve_evac, 1)
                v.wait_ge(s["bada_in"], 16)
                v.wait_ge(s["mod_back"], 16)
                v.tensor_tensor(modt[:, 0, :], modt[:, 0, :], modt[:, 1, :], ALU.add).then_inc(s["mod_sum"], 1)

            @block.gpsimd
            def _(pool):
                pool.memset(sq[:, :, :], 0.0).then_inc(pool_step, 1)
                pool.wait_ge(pool_step, 1)
                zero = sq[:, :, :].rearrange("p h n -> p (h n)")
                for b in range((ROWS - 2 * S) // P):
                    for scratch in (xs_dram, ys_dram):
                        pool.dma_start(scratch[2 * S + b * P:2 * S + (b + 1) * P, :], zero)\
                            .then_inc(zeroed, 16)
                pool.wait_ge(zeroed, 2 * 16 * ((ROWS - 2 * S) // P))

            @block.tensor
            def _(pe):
                pe.sem_inc(s["mod_done"], RING)
                pe.wait_ge(s["consts_in"], 16)
                pe.wait_ge(s["c_silu"], 1)
                pe.transpose(bank[7][:, 0:K], crow[:, :], ident[0:K, 0:K]).then_inc(pe_done, 1)
                pe.wait_ge(dve_evac, 1)
                with pe.Fori(0, DEPTH) as l:
                    with pe.Fori(0, HALF) as i:
                        for j in range(RING):
                            w = ring[:, j, :].rearrange("p (k n) -> p k n", k=K)
                            pe.wait_ge(slot[j], (l * HALF + i + 1) * 16)
                            pe.wait_ge(s["mod_evac"], (l * HALF + i) * RING + j + 1)
                            for k in range(K):
                                mm = pe.matmul(bank[j][0:1, :], ccol[:, k:k + 1], w[:, k, :],
                                               start=(k == 0), stop=(k == K - 1))
                            mm.then_inc(s["mod_done"], 1)
        clear_semaphores()

        jobs = [("params", "dve"), ("taps", "dve")]
        jobs += [(f"h{k}", "act") for k in range(K)]
        jobs += [(f"A{t}", "act") for t in range(T)]
        jobs += [("cg0", "act"), ("ca0", "dve"), ("cg1", "act"), ("ca1", "dve"), ("iqT", "act"), ("ikT", "act")]
        jobs += [(f"idx{b}{h}", "act") for b in range(1, T) for h in range(IH)]
        jobs += [(f"B{t}", "act") for t in range(T)]
        jobs += [("pool0", "act"), ("pool1", "act"), ("u0", "act"), ("u1", "act")]
        jobs += [(f"E{t}", "act") for t in range(T)]
        jobs += [("qT0", "act"), ("qT1", "act"), ("kT0", "act"), ("kT1", "act")]

        def attention_jobs(b):
            out_ = [(f"logit{b}{h}", "dve") for h in range(HEADS)]
            for pair in range(2):
                out_ += [(f"probT{b}{2 * pair}", "act"), (f"probT{b}{2 * pair + 1}", "act"), (f"pv{b}{pair}", "act")]
            return out_

        jobs += attention_jobs(0)
        jobs += [("sgw", "dve"), ("sgu0", "dve"), ("sgu1", "dve"), ("pl0", "dve"), ("pl1", "dve")]
        jobs += attention_jobs(1)
        jobs += [("cmean0", "dve"), ("cvar0", "act"), ("cmean1", "dve"), ("cvar1", "act")]
        jobs += attention_jobs(2)
        jobs += [("pw0", "dve"), ("pw1", "dve")]
        jobs += [("rms2", "act"), ("rms3", "act")]
        jobs += attention_jobs(3)
        jobs += [("rms1", "act"), ("rms0", "act")]
        jobs += [(f"out{n}{t}", "dve") for n in range(N_OUT) for t in range(T)]
        jobs += [(f"m{k}", "act") for k in range(K)]
        jobs += [("route", "dve"), ("rank", "dve")]
        index = {name: i for i, (name, _) in enumerate(jobs)}

        def done(name):
            return index[name] + 1

        def emptied(name):
            i = index[name]
            return sum(1 for _, e in jobs[:i + 1] if e == jobs[i][1])

        def bank_of(name):
            return bank[index[name] % 8]

        def await_bank(pe, name):
            i = index[name] - 8
            if i >= 0:
                pe.wait_ge(act_evac if jobs[i][1] == "act" else dve_evac, emptied(jobs[i][0]))

        IN_COLS = [(C_V, NA), (C_CONV, 2 * G), (C_Q, 2 * G), (C_POOL, 2 * G), (C_SGU + G, G)]
        IN_LAST = ["A3", "ca1", "B3", "u1", "E3", "out03", "out13"]

        def chunk_view(n, width):
            return ring[:, n % RING, 0:K * width].rearrange("p (k n) -> p k n", k=K)

        def loaded(n):
            return slot[n % RING], 16 * (n // RING + 1)

        with nc.Fori(0, DEPTH) as l:
            with nc.Block() as block:
                @block.sync
                def _(sp):
                    def expert_chunk(n, kind, e):
                        src = {"g": wg_v, "u": wu_v, "d": wd_v}[kind][l, e]
                        k = K if kind in "gu" else FF // P
                        sp.dma_start(ring[:, n % RING, :].rearrange("p (k n) -> p k n", k=k), src)\
                            .then_inc(slot[n % RING], 16)

                    def static_wait(n):
                        if n >= RING:
                            sp.wait_ge(pe_done, done(IN_LAST[n - RING]))

                    for n, (a, w) in enumerate(IN_COLS):
                        sp.dma_start(chunk_view(n, w), win_v[l, :, :, a:a + w]).then_inc(slot[n], 16)
                    for j in range(N_OUT):
                        n = N_IN + j
                        static_wait(n)
                        sp.dma_start(chunk_view(n, 512), wout_v[l, :, :, j * 512:(j + 1) * 512])\
                            .then_inc(slot[n % RING], 16)
                    for n, (kind, e) in enumerate([("g", 0), ("u", 0), ("g", 1), ("u", 1), ("d", 0), ("g", 2)], N_PRE):
                        static_wait(n)
                        expert_chunk(n, kind, e)
                    sp.sem_inc(s["y_written"], 16)
                    sp.wait_ge(s["routed"], 1)

                    def write_y(e):
                        row = sp.value_load(starti[0:1, bass.ds(e, 1)], min_val=0, max_val=2 * S)
                        dst = ys_dram[bass.ds(row, P), :]
                        return dst

                    def step_pair(i, first=False, last=False):
                        n = 13
                        sp.wait_ge(s["gate_mm"] if first else s["up_mm"], 1 if first else 2 * i + 1)
                        expert_chunk(n, "u", 2 * i + 2)
                        if first:
                            sp.wait_ge(s["up_mm"], 1)
                        else:
                            sp.wait_ge(s["down_mm"], 2 * i)
                        expert_chunk(n + 1, "d", 2 * i + 1)
                        if not first:
                            dst = write_y(2 * i - 1)
                            sp.wait_ge(s["y_ready"], 2 * i + 1)
                            sp.dma_start(dst, ybuf[1]).then_inc(s["y_written"], 16)
                        sp.wait_ge(s["gate_mm"], 2 * i + 2)
                        expert_chunk(n + 2, "g", 2 * i + 3)
                        sp.wait_ge(s["up_mm"], 2 * i + 2)
                        expert_chunk(n + 3, "u", 2 * i + 3)
                        sp.wait_ge(s["down_mm"], 2 * i + 1)
                        expert_chunk(n + 4, "d", 2 * i + 2)
                        dst = write_y(2 * i)
                        sp.wait_ge(s["y_ready"], 2 * i + 2)
                        sp.dma_start(dst, ybuf[0]).then_inc(s["y_written"], 16)
                        sp.wait_ge(s["gate_mm"], 2 * i + 3)
                        if last:
                            expert_chunk(n + 5, "d", E - 1)
                        else:
                            expert_chunk(n + 5, "g", 2 * i + 4)

                    step_pair(0, first=True)
                    with sp.Fori(1, E // 2 - 2) as i:
                        step_pair(i)
                    step_pair(E // 2 - 2, last=True)
                    for e in range(E - 3, E):
                        dst = write_y(e)
                        sp.wait_ge(s["y_ready"], e + 2)
                        sp.dma_start(dst, ybuf[e % 2]).then_inc(s["y_written"], 16)
                    sp.wait_ge(s["y_written"], 16 * (E + 1))

                @block.scalar
                def _(act):
                    step = stepper(act, act_step)
                    act.dma_start(prow[R_MOD:R_MOD + 48, :], mod_dram[bass.ds(l * 48, 48), :])\
                       .then_inc(s["rows_in"], 16)
                    for r, name, n in ((R_N1, "norm1", K), (R_N2, "norm2", K), (R_ON, "out_norm", K),
                                       (R_CB, "conv_b", 2), (R_LG, "conv_ln_g", 2), (R_LB, "conv_ln_b", 2),
                                       (R_PB, "conv_pw_b", 2), (R_QS, "pool_scale", 2)):
                        act.dma_start(prow[r:r + n, :], A[name][l].rearrange("(r p) -> r p", p=P))\
                           .then_inc(s["rows_in"], 16)
                    act.dma_start(prow[R_QB:R_QB + 2, :], A["pool_b"][l].rearrange("(r a) c -> r (a c)", a=2))\
                       .then_inc(s["rows_in"], 16)
                    act.dma_start(cwrow[:, :], A["conv_w"][l].rearrange("w (h p) -> (w h) p", p=P))\
                       .then_inc(s["taps_in"], 16)
                    for t in range(T):
                        step(act.activation(sq[:, :, :].rearrange("p h n -> p (h n)"), x[:, t, :], ACT.Square,
                                            accum_out=ss[:, t:t + 1]))
                    act.activation(rs, ss, ACT.Sqrt, bias=c("eps"), scale=1.0 / D).then_inc(s["rstd_done"], 1)
                    for j, name in enumerate(("q_norm", "k_norm")):
                        act.dma_start(qkn[:, j, :], A[name][l].partition_broadcast(P)).then_inc(s["norms_in"], 16)
                    for j, name in enumerate(("sgu_ln_g", "sgu_ln_b")):
                        act.dma_start(sgn[:, j, :], A[name][l].partition_broadcast(P)).then_inc(s["sgu_in"], 16)
                    for h in range(SGU_H):
                        act.dma_start(sgb[64 * (h % 2):64 * (h % 2) + 64, h // 2, :],
                                      A["sgu_b"][l, h].partition_broadcast(64)).then_inc(s["sgu_in"], 16)
                    act.dma_start(sgw[:, :, :], A["sgu_w"][l].rearrange("h t s -> t h s")).then_inc(s["sgu_in"], 16)
                    act.dma_start(pww[:, :, :], A["conv_pw_w"][l].rearrange("(i p) n -> p i n", p=P))\
                       .then_inc(s["pw_in"], 16)
                    for g in range(4):
                        o = 64 * (g % 2)
                        act.dma_start(plw[o:o + 64, g // 2, o:o + 64], A["pool_w"][l, g]).then_inc(s["pw_in"], 16)
                    act.dma_start(wr[:, :, 0:NG], A["w_rg"][l].rearrange("(k p) g -> p k g", p=P))\
                       .then_inc(s["router_in"], 16)
                    act.dma_start(wr[:, :, NG:], A["w_re"][l].rearrange("(k p) g e -> p k (g e)", p=P))\
                       .then_inc(s["router_in"], 16)
                    act.dma_start(rb[:, 0:NG], A["b_rg"][l].partition_broadcast(P)).then_inc(s["router_in"], 16)
                    act.dma_start(rb[:, NG:], A["b_re"][l].rearrange("g e -> (g e)").partition_broadcast(P))\
                       .then_inc(s["router_in"], 16)

                    act.wait_ge(s["scl_ready"], 1)
                    for k in range(K):
                        act.wait_ge(pe_done, done(f"h{k}"))
                        act.activation(hT[:, k, :], bank_of(f"h{k}")[:, :], ACT.Identity,
                                       bias=pcol[:, SHIFT1 * K + k:SHIFT1 * K + k + 1], scale=scl[:, 0, k:k + 1])\
                           .then_inc(act_evac, 1)
                    for t in range(T):
                        act.wait_ge(pe_done, done(f"A{t}"))
                        act.activation(tokA[:, t, :], bank_of(f"A{t}")[:, 0:NA], ACT.Copy).then_inc(act_evac, 1)
                    for h in range(2):
                        act.wait_ge(pe_done, done(f"cg{h}"))
                        act.activation(sig[:, h, :], bank_of(f"cg{h}")[:, :], ACT.Sigmoid).then_inc(act_evac, 1)
                    for name, dst in (("iqT", iqT), ("ikT", ikT)):
                        act.wait_ge(pe_done, done(name))
                        act.activation(dst[:, :], bank_of(name)[:, :], ACT.Copy).then_inc(act_evac, 1)
                    n_relu = 0
                    for b in range(1, T):
                        for h in range(IH):
                            act.wait_ge(pe_done, done(f"idx{b}{h}"))
                            if n_relu >= 2:
                                act.wait_ge(s["relu_free"], n_relu - 1)
                            w = (b + 1) * P
                            act.activation(relu[n_relu % 2][:, 0:w], bank_of(f"idx{b}{h}")[:, 0:w], ACT.Relu,
                                           scale=float(ID ** -0.5 * IH ** -0.5)).then_inc(act_evac, 1)
                            n_relu += 1
                    act.wait_ge(s["relu_free"], n_relu)
                    for t in range(T):
                        act.wait_ge(pe_done, done(f"B{t}"))
                        act.activation(tokB[:, t, :], bank_of(f"B{t}")[:, :], ACT.Copy).then_inc(act_evac, 1)
                    for h in range(2):
                        act.wait_ge(pe_done, done(f"pool{h}"))
                        act.activation(poolin[:, h, 16:], bank_of(f"pool{h}")[:, :], ACT.Copy).then_inc(act_evac, 1)
                    act.wait_ge(s["conv_in"], 2)
                    for h in range(2):
                        act.wait_ge(pe_done, done(f"u{h}"))
                        act.activation(uT[:, h, :], bank_of(f"u{h}")[:, :], ACT.Copy).then_inc(act_evac, 1)
                    for t in range(T):
                        act.wait_ge(pe_done, done(f"E{t}"))
                        act.activation(dv[:, t, :], bank_of(f"E{t}")[:, 0:G], ACT.Copy).then_inc(act_evac, 1)
                    act.wait_ge(s["qk_ss"], 1)
                    act.activation(rsq, ssq, ACT.Sqrt, bias=c("eps"), scale=1.0 / HD).then_inc(s["qk_rstd"], 1)
                    for name, dst in (("qT0", qT[:, 0]), ("qT1", qT[:, 1]), ("kT0", kT[:, :, 0:P]), ("kT1", kT[:, :, P:2 * P])):
                        act.wait_ge(pe_done, done(name))
                        src = bank_of(name)[:, :]
                        if name[0] == "k":
                            src = src.rearrange("p (t n) -> p t n", t=T)
                        act.activation(dst, src, ACT.Copy).then_inc(act_evac, 1)

                    def attention(b):
                        w = (b + 1) * P
                        act.wait_ge(s["exp_in"], b + 1)
                        for h in range(HEADS):
                            ins = act.activation(prob[:, h, 0:w], prob[:, h, 0:w], ACT.Exp,
                                                 bias=nmx[:, h:h + 1], scale=float(HD ** -0.5),
                                                 accum_out=sums[:, h:h + 1])
                        ins.then_inc(s["exp_done"], 1)
                        for pair in range(2):
                            before = f"pv{b}0" if pair else (f"pv{b - 1}1" if b else None)
                            if before:
                                act.wait_ge(pe_done, done(before))
                            for h in (2 * pair, 2 * pair + 1):
                                act.wait_ge(pe_done, done(f"probT{b}{h}"))
                                act.activation(probT[:, h % 2, 0:w], bank_of(f"probT{b}{h}")[:, 0:w], ACT.Copy)\
                                   .then_inc(act_evac, 1)
                            act.wait_ge(pe_done, done(f"pv{b}{pair}"))
                            act.activation(mixT[:, pair, b * P:(b + 1) * P], bank_of(f"pv{b}{pair}")[:, 0:P],
                                           ACT.Copy).then_inc(act_evac, 1)

                    def squares(g, n):
                        buf = mix_sq_buf[n % 2]
                        if n >= 2:
                            act.wait_ge(s["mix_normed"], n - 1)
                        act.activation(buf, mixT[:, 2 * g:2 * g + 2, :], ACT.Square).then_inc(s["mix_sq"], 1)

                    def deviation(g, n):
                        act.wait_ge(pe_done, done(f"rms{g}"))
                        act.activation(mix_sq_buf[n % 2][:, 0, :], bank_of(f"rms{g}")[:, :], ACT.Sqrt,
                                       bias=c("eps")).then_inc(act_evac, 1)

                    act.wait_ge(s["sgu_var"], 1)
                    act.activation(rdv, bag[:, :, 1], ACT.Sqrt, bias=c("eps")).then_inc(s["sgu_rstd"], 1)
                    attention(0)
                    attention(1)
                    for h in range(2):
                        act.wait_ge(s["centered"], h + 1)
                        act.activation(sq[:, h, :], acc[:, h, :], ACT.Square).then_inc(s["centered_sq"], 1)
                        act.wait_ge(pe_done, done(f"cvar{h}"))
                        act.activation(sq[:, h, :], bank_of(f"cvar{h}")[:, :], ACT.Sqrt, bias=c("eps"))\
                           .then_inc(act_evac, 1)
                    attention(2)
                    act.wait_ge(s["conv_normed"], 1)
                    for h in range(2):
                        act.activation(acc[:, h, :], acc[:, h, :], ACT.Silu,
                                       bias=pcol[:, R_LB + h:R_LB + h + 1], scale=pcol[:, R_LG + h:R_LG + h + 1])\
                           .then_inc(s["swished"], 1)
                    act.wait_ge(s["conv_done"], 2)
                    act.dma_start(g1b, mod_dram.rearrange("(m r) p -> m (r p)", r=K)
                                  [bass.ds(l * 6 + GATE1, 1), :].partition_broadcast(P)).then_inc(s["gate1_in"], 16)
                    act.wait_ge(s["mix_ready"], 1)
                    squares(2, 0)
                    squares(3, 1)
                    deviation(2, 0)
                    deviation(3, 1)
                    attention(3)
                    act.wait_ge(s["mix_ready"], 2)
                    squares(1, 2)
                    act.wait_ge(act_evac, emptied("pv31"))
                    squares(0, 3)
                    deviation(1, 2)
                    deviation(0, 3)
                    act.wait_ge(s["x_added"], 1)
                    for t in range(T):
                        step(act.activation(sq[:, :, :].rearrange("p h n -> p (h n)"), x[:, t, :], ACT.Square,
                                            accum_out=ss[:, t:t + 1]))
                    act.activation(rs, ss, ACT.Sqrt, bias=c("eps"), scale=1.0 / D).then_inc(s["rstd_done"], 1)
                    for k in range(K):
                        act.wait_ge(pe_done, done(f"m{k}"))
                        act.activation(hT[:, k, :], bank_of(f"m{k}")[:, :], ACT.Identity,
                                       bias=pcol[:, SHIFT2 * K + k:SHIFT2 * K + k + 1], scale=scl[:, 1, k:k + 1])\
                           .then_inc(act_evac, 1)
                    act.wait_ge(s["gexp_in"], 1)
                    act.activation(r4[:, 0], r4[:, 0], ACT.Exp)
                    act.activation(ediff, ediff, ACT.Exp).then_inc(s["gexp_out"], 1)

                    act.wait_ge(s["routed"], 1)
                    act.wait_ge(scattered, (l + 1) * (16 * 2 * T))
                    act.sem_inc(act_step, 1)

                    def load_rows(e, b):
                        row = act.value_load(starti[0:1, bass.ds(e, 1)], min_val=0, max_val=2 * S)
                        act.dma_start(xs[b], xs_dram[bass.ds(row, P), :]).then_inc(xs_in[b], 16)

                    def evacuate_rows(count, b):
                        act.wait_ge(s["xs_tr"], count + 1)
                        for k in range(K):
                            ins = act.activation(xT[b][:, k, :], XP[k // 4][:, (k % 4) * P:(k % 4 + 1) * P],
                                                 ACT.Identity, scale=scl[:, 1, k:k + 1],
                                                 bias=pcol[:, SHIFT2 * K + k:SHIFT2 * K + k + 1])
                        ins.then_inc(s["xt_ready"], 1)

                    def silu(e):
                        act.wait_ge(s["gate_mm"], e + 1)
                        act.activation(sgate, GB[:, :], ACT.Silu).then_inc(s["silu_done"], 1)

                    def evacuate_hidden(e):
                        act.wait_ge(s["hid_tr"], e + 1)
                        act.activation(hidT, HB[:, :].rearrange("p (k s) -> p k s", k=4), ACT.Copy)\
                           .then_inc(s["hidt_ready"], 1)

                    load_rows(0, 0)
                    load_rows(1, 1)
                    evacuate_rows(0, 0)
                    load_rows(2, 0)
                    silu(0)
                    evacuate_rows(1, 1)
                    load_rows(3, 1)

                    def step_expert(e, b, more=True, rows=True):
                        act.wait_ge(s["hid_ready"], e)
                        silu(e)
                        evacuate_hidden(e - 1)
                        if rows:
                            evacuate_rows(e + 1, 1 - b)
                        if more:
                            load_rows(e + 3, 1 - b)

                    with act.Fori(0, E // 2 - 2) as i:
                        step_expert(2 * i + 1, 1)
                        step_expert(2 * i + 2, 0)
                    step_expert(E - 3, 1, more=False)
                    step_expert(E - 2, 0, more=False)
                    step_expert(E - 1, 1, more=False, rows=False)
                    evacuate_hidden(E - 1)

                @block.gpsimd
                def _(pool):
                    step = stepper(pool, pool_step)

                    pool.wait_ge(s["conv_in"], 2)
                    step(pool.tensor_scalar(acc[:, 1, :], convin[:, 1, 0:S], cwcol[:, 1:2],
                                            pcol[:, R_CB + 1:R_CB + 2], ALU.mult, ALU.add))
                    for w in range(1, TAPS):
                        product = wsum[1][:, w % 2, 0:S]
                        step(pool.tensor_scalar(product, convin[:, 1, w:w + S], cwcol[:, 2 * w + 1:2 * w + 2],
                                                None, ALU.mult))
                        step(pool.tensor_tensor(acc[:, 1, :], acc[:, 1, :], product, ALU.add))
                    pool.sem_inc(s["conv_done"], 1)
                    pool.wait_ge(act_evac, emptied("pool1"))
                    a, b = wsum
                    step(pool.tensor_tensor(a[:, :, 1:], poolin[:, :, 1:], poolin[:, :, 0:15 + S], ALU.add))
                    step(pool.tensor_tensor(b[:, :, 3:], a[:, :, 3:], a[:, :, 1:14 + S], ALU.add))
                    step(pool.tensor_tensor(a[:, 1, 7:], b[:, 1, 7:], b[:, 1, 3:12 + S], ALU.add))
                    step(pool.tensor_tensor(b[64:, 1, 15:], a[64:, 1, 15:], a[64:, 1, 7:8 + S], ALU.add))
                    invw, invc = c("invw"), c("invc").rearrange("p (h n) -> p h n", h=2)
                    for lo, src in ((0, a), (64, b)):
                        r = slice(lo, lo + 64)
                        step(pool.tensor_tensor(a[r, :, 16:32], src[r, :, 16:32], invc[r, :, :], ALU.mult))
                        step(pool.tensor_tensor(a[r, :, 16:32], a[r, :, 16:32], poolin[r, :, 16:32], ALU.subtract))
                        for h in range(2):
                            step(pool.tensor_scalar(a[r, h, 32:], src[r, h, 32:], invw[r, h:h + 1], None, ALU.mult))
                            step(pool.tensor_tensor(a[r, h, 32:], a[r, h, 32:], poolin[r, h, 32:], ALU.subtract))
                    pool.sem_inc(s["pooled"], 1)
                    pool.wait_ge(s["routed"], 1)
                    for t in range(T):
                        for j in range(2):
                            pool.indirect_dma_start(
                                xs_dram, bass.IndirectOffsetOnAxis(ap=posu[:, j, t:t + 1], axis=0),
                                xn[:, t, :], None, bounds_check=ROWS - 1, oob_is_err=True)\
                                .then_inc(scattered, 16)

                @block.vector
                def _(v):
                    step = stepper(v, dve_step)
                    v.wait_ge(pe_done, done("params"))
                    step(v.tensor_copy(pcol[:, :], bank_of("params")[:, 0:NROW]))
                    v.sem_inc(dve_evac, 1)
                    v.wait_ge(pe_done, done("taps"))
                    v.tensor_copy(cwcol[:, :], bank_of("taps")[:, 0:2 * TAPS]).then_inc(dve_evac, 1)
                    for j, (m, r) in enumerate(((SCALE1, R_N1), (SCALE2, R_N2))):
                        ins = v.scalar_tensor_tensor(scl[:, j, :], pcol[:, m * K:(m + 1) * K], 1.0,
                                                     pcol[:, r:r + K], ALU.add, ALU.mult)
                    ins.then_inc(s["scl_ready"], 1)
                    v.memset(convin[:, :, 0:TAPS - 1], 0.0)
                    v.wait_ge(s["rstd_done"], 1)
                    step(v.reciprocal(rs, rs))
                    for t in range(T):
                        ins = v.tensor_scalar(xn[:, t, :], x[:, t, :], rs[:, t:t + 1], None, ALU.mult)
                    ins.then_inc(s["xn_done"], 1)

                    def rope(tiles, heads, half, table):
                        cos = cs[:, :, table:table + half].unsqueeze(2).to_broadcast([P, T, heads, half])
                        sin = sn[:, :, table:table + half].unsqueeze(2).to_broadcast([P, T, heads, half])
                        a, b = tiles[:, :, :, 0:half], tiles[:, :, :, half:2 * half]
                        tmp = [ropet[:, i, :, 0:heads, 0:half] for i in range(4)]
                        v.tensor_tensor(tmp[0], a, cos, ALU.mult)
                        v.tensor_tensor(tmp[1], b, sin, ALU.mult)
                        v.tensor_tensor(tmp[2], b, cos, ALU.mult)
                        step(v.tensor_tensor(tmp[3], a, sin, ALU.mult))
                        v.tensor_tensor(a, tmp[0], tmp[1], ALU.subtract)
                        return v.tensor_tensor(b, tmp[2], tmp[3], ALU.add)

                    v.wait_ge(act_evac, emptied("A3"))
                    step(rope(tokA[:, :, G:G + (IH + 1) * ID].rearrange("p t (h d) -> p t h d", d=ID),
                              IH + 1, IROT, ROT))
                    v.tensor_copy(ik4[:, :, :].rearrange("p t (r d) -> p t r d", r=4),
                                  tokA[:, :, G + IH * ID:G + (IH + 1) * ID].unsqueeze(2)
                                  .to_broadcast([P, T, 4, ID])).then_inc(s["idx_roped"], 1)
                    for h in range(2):
                        v.wait_ge(act_evac, emptied(f"cg{h}"))
                        v.wait_ge(pe_done, done(f"ca{h}"))
                        step(v.tensor_tensor(convin[:, h, TAPS - 1:], bank_of(f"ca{h}")[:, :], sig[:, h, :],
                                             ALU.mult))
                        v.sem_inc(dve_evac, 1)
                        v.sem_inc(s["conv_in"], 1)
                    n = 0
                    for b in range(1, T):
                        w = (b + 1) * P
                        dst = score[:, SC[b]:SC[b] + w]
                        for h in range(IH):
                            iw = tokA[:, b, NA - IH + h:NA - IH + h + 1]
                            v.wait_ge(act_evac, emptied(f"idx{b}{h}"))
                            if h == 0:
                                ins = v.tensor_scalar(dst, relu[n % 2][:, 0:w], iw, None, ALU.mult)
                            else:
                                ins = v.scalar_tensor_tensor(dst, relu[n % 2][:, 0:w], iw, dst, ALU.mult, ALU.add)
                            n += 1
                            step(ins)
                            v.sem_inc(s["relu_free"], 1)
                        step(v.memset(score[0:CHUNK, SC[b] + w - CHUNK:SC[b] + w], NEG))

                    def select(b):
                        w = (b + 1) * P
                        sc = score[:, SC[b]:SC[b] + w]
                        for _ in range(TOPK // 8):
                            step(v.max(m8, sc))
                            step(v.match_replace(sc, m8, sc, GONE))
                        step(v.tensor_scalar(sc, sc, float(0.5 * (NEG + GONE)), MASK, ALU.is_gt, ALU.mult))

                    step(v.tensor_scalar(acc[:, 0, :], convin[:, 0, 0:S], cwcol[:, 0:1], pcol[:, R_CB:R_CB + 1],
                                         ALU.mult, ALU.add))
                    for w in range(1, TAPS):
                        step(v.scalar_tensor_tensor(acc[:, 0, :], convin[:, 0, w:w + S],
                                                    cwcol[:, 2 * w:2 * w + 1], acc[:, 0, :], ALU.mult, ALU.add))
                    v.sem_inc(s["conv_done"], 1)
                    select(1)
                    v.wait_ge(act_evac, emptied("B3"))
                    for t in range(T):
                        for h in range(2 * HEADS):
                            src = tokB[:, t, h * HD:(h + 1) * HD]
                            n = (t * 8 + h) % 16
                            ins = v.tensor_tensor_reduce(sq_flat[:, n * HD:(n + 1) * HD], src, src, 1.0, 0.0,
                                                         ALU.mult, ALU.add, ssq[:, t * 8 + h:t * 8 + h + 1])
                        if t == 1:
                            step(ins)
                    ins.then_inc(s["qk_ss"], 1)
                    select(2)
                    v.wait_ge(s["qk_rstd"], 1)
                    step(v.reciprocal(rsq, rsq))
                    v.wait_ge(s["norms_in"], 32)
                    qk = tokB[:, :, :].rearrange("p t (h d) -> p t h d", d=HD)
                    step(v.tensor_tensor(qk, qk, rsq.rearrange("p (t h) -> p t h", t=T).unsqueeze(3)
                                         .to_broadcast([P, T, 2 * HEADS, HD]), ALU.mult))
                    for j in range(2):
                        for t in range(T):
                            part = qk[:, t, j * HEADS:(j + 1) * HEADS, :]
                            ins = v.tensor_tensor(part, part, qkn[:, j, :].unsqueeze(1)
                                                  .to_broadcast([P, HEADS, HD]), ALU.mult)
                    step(ins)
                    rope(qk, 2 * HEADS, ROT, 0).then_inc(s["qk_roped"], 1)
                    v.wait_ge(act_evac, emptied("E3"))
                    for t in range(T):
                        step(v.bn_stats(bst[:, t, :], dv[:, t, :]))
                    for t in range(T):
                        ins = v.bn_aggr(bag[:, t, :], bst[:, t, :])
                    ins.then_inc(s["sgu_var"], 1)

                    def attention(b):
                        w = (b + 1) * P
                        bias = score[:, SC[b]:SC[b] + w] if b else c("mask0")
                        v.wait_ge(pe_done, done(f"probT{b - 1}3" if b else "E3"))
                        for h in range(HEADS):
                            v.wait_ge(pe_done, done(f"logit{b}{h}"))
                            ins = v.tensor_tensor_reduce(prob[:, h, 0:w], bank_of(f"logit{b}{h}")[:, 0:w], bias,
                                                         1.0, NEG, ALU.add, ALU.max, mx[:, h:h + 1])
                            if h < HEADS - 1:
                                ins.then_inc(dve_evac, 1)
                        step(ins)
                        v.sem_inc(dve_evac, 1)
                        v.tensor_scalar(nmx, mx, -float(HD ** -0.5), None, ALU.mult).then_inc(s["exp_in"], 1)
                        v.wait_ge(s["exp_done"], b + 1)
                        step(v.reciprocal(rsum, sums))
                        for h in range(HEADS):
                            ins = v.tensor_scalar(prob[:, h, 0:w], prob[:, h, 0:w], rsum[:, h:h + 1], None, ALU.mult)
                        ins.then_inc(s["prob_ready"], 1)

                    attention(0)
                    v.wait_ge(s["sgu_rstd"], 1)
                    step(v.reciprocal(rdv, rdv))
                    v.wait_ge(s["sgu_in"], 16 * 7)
                    for t in range(T):
                        ins = v.tensor_scalar(dv[:, t, :], dv[:, t, :], bag[:, t, 0:1], rdv[:, t:t + 1],
                                              ALU.subtract, ALU.mult)
                    step(ins)
                    step(v.tensor_tensor(dv, dv, sgn[:, 0, :].unsqueeze(1).to_broadcast([P, T, G]), ALU.mult))
                    v.tensor_tensor(dv, dv, sgn[:, 1, :].unsqueeze(1).to_broadcast([P, T, G]), ALU.add)\
                        .then_inc(s["sgu_normed"], 1)
                    v.wait_ge(pe_done, done("sgw"))
                    v.tensor_tensor(sgwT[:, :, :], bank_of("sgw")[:, :].rearrange("p (h t) -> p h t", h=SGU_H),
                                    c("upto").unsqueeze(1).to_broadcast([P, SGU_H, P]), ALU.mult)\
                        .then_inc(dve_evac, 1)
                    v.wait_ge(act_evac, emptied("u1"))
                    for p in range(2):
                        v.wait_ge(pe_done, done(f"sgu{p}"))
                        mixed = sq[:, p, :]
                        step(v.tensor_tensor(mixed.rearrange("p (n t) -> p n t", n=T),
                                             bank_of(f"sgu{p}")[:, :].rearrange("p (n t) -> p n t", n=T),
                                             sgb[:, p, :].unsqueeze(1).to_broadcast([P, T, P]), ALU.add))
                        v.sem_inc(dve_evac, 1)
                        v.tensor_tensor(uT[:, p, :], mixed, uT[:, p, :], ALU.mult)
                    for h in range(2):
                        v.wait_ge(pe_done, done(f"pl{h}"))
                        ins = v.tensor_scalar(mixT[:, 4 + h, :], bank_of(f"pl{h}")[:, :],
                                              pcol[:, R_QB + h:R_QB + h + 1], pcol[:, R_QS + h:R_QS + h + 1],
                                              ALU.add, ALU.mult)
                        if h == 0:
                            ins.then_inc(dve_evac, 1)
                    step(ins)
                    v.sem_inc(dve_evac, 1)
                    v.sem_inc(s["mix_ready"], 1)
                    attention(1)
                    select(3)
                    for h in range(2):
                        v.wait_ge(pe_done, done(f"cmean{h}"))
                        step(v.tensor_tensor(acc[:, h, :], acc[:, h, :], bank_of(f"cmean{h}")[:, :], ALU.subtract))
                        v.sem_inc(dve_evac, 1)
                        v.sem_inc(s["centered"], 1)
                    attention(2)
                    v.wait_ge(act_evac, emptied("cvar1"))
                    step(v.reciprocal(sq[:, :, :], sq[:, :, :]))
                    v.tensor_tensor(acc[:, :, :], acc[:, :, :], sq[:, :, :], ALU.mult).then_inc(s["conv_normed"], 1)
                    v.wait_ge(pe_done, done("pw1"))
                    for co in range(2):
                        ins = v.tensor_scalar(mixT[:, 2 + co, :], bank_of(f"pw{co}")[:, :],
                                              pcol[:, R_PB + co:R_PB + co + 1], None, ALU.add)
                        if co == 0:
                            ins.then_inc(dve_evac, 1)
                    step(ins)
                    v.sem_inc(dve_evac, 1)
                    v.sem_inc(s["mix_ready"], 1)

                    def normalise(g, n):
                        buf = mix_sq_buf[n % 2]
                        v.wait_ge(act_evac, emptied(f"rms{g}"))
                        step(v.reciprocal(buf[:, 0, :], buf[:, 0, :]))
                        for i in range(2):
                            m = 2 * g + i
                            ins = v.scalar_tensor_tensor(mixT[:, m, :], mixT[:, m, :],
                                                         pcol[:, R_ON + m:R_ON + m + 1], buf[:, 0, :],
                                                         ALU.mult, ALU.mult)
                        ins.then_inc(s["mix_normed"], 1)

                    normalise(2, 0)
                    normalise(3, 1)
                    attention(3)
                    normalise(1, 2)
                    normalise(0, 3)
                    v.wait_ge(s["gate1_in"], 16)
                    for n in range(N_OUT):
                        for t in range(T):
                            name = f"out{n}{t}"
                            tmp = sq[:, t % 2, :]
                            v.wait_ge(pe_done, done(name))
                            step(v.tensor_tensor(tmp, bank_of(name)[:, :], g1b[:, n * 512:(n + 1) * 512], ALU.mult))
                            v.sem_inc(dve_evac, 1)
                            part = x[:, t, n * 512:(n + 1) * 512]
                            ins = v.tensor_tensor(part, part, tmp, ALU.add)
                    ins.then_inc(s["x_added"], 1)
                    v.wait_ge(s["rstd_done"], 2)
                    step(v.reciprocal(rs, rs))
                    for t in range(T):
                        ins = v.tensor_scalar(xn[:, t, :], x[:, t, :], rs[:, t:t + 1], None, ALU.mult)
                    ins.then_inc(s["xn_done"], 1)

                    v.wait_ge(s["router_in"], 64)
                    v.wait_ge(pe_done, done("route"))
                    step(v.tensor_tensor(lg[:, :, :], bank_of("route")[:, 0:T * (NG + E)]
                                         .rearrange("p (t n) -> p t n", t=T),
                                         rb[:, :].unsqueeze(1).to_broadcast([P, T, NG + E]), ALU.add))
                    v.sem_inc(dve_evac, 1)
                    grp = lg[:, :, 0:NG]
                    io4 = c("iota")[:, 0:NG].unsqueeze(1).to_broadcast([P, T, NG])
                    step(v.tensor_reduce(gmax, grp, AX.X, ALU.max))
                    gm = gmax.unsqueeze(2).to_broadcast([P, T, NG])
                    v.tensor_tensor(r4[:, 0], grp, gm, ALU.subtract)
                    step(v.tensor_tensor(r4[:, 1], grp, gm, ALU.is_lt))
                    step(v.scalar_tensor_tensor(r4[:, 1], r4[:, 1], float(NG), io4, ALU.mult, ALU.add))
                    step(v.tensor_reduce(gidx, r4[:, 1], AX.X, ALU.min))
                    step(v.tensor_tensor(r4[:, 2], io4, gidx.unsqueeze(2).to_broadcast([P, T, NG]), ALU.is_equal))
                    step(v.tensor_scalar(r4[:, 2], r4[:, 2], 1.0, -MASK, ALU.subtract, ALU.mult))
                    for t in range(T):
                        ins = v.tensor_tensor(el[:, t, :].rearrange("p (g e) -> p g e", g=NG),
                                              lg[:, t, NG:].rearrange("p (g e) -> p g e", g=NG),
                                              r4[:, 2, t, :].unsqueeze(2).to_broadcast([P, NG, EPG]), ALU.add)
                    step(ins)
                    for t in range(T):
                        ins = v.max(top8[:, t, :], el[:, t, :])
                    step(ins)
                    for t in range(T):
                        v.max_index(topi[:, t, :], top8[:, t, :], el[:, t, :])
                    step(v.tensor_tensor(ediff, top8[:, :, 1], top8[:, :, 0], ALU.subtract))
                    v.sem_inc(s["gexp_in"], 1)
                    step(v.tensor_copy(topf, topi[:, :, :]))
                    io = c("iota").unsqueeze(1).to_broadcast([P, T, E])
                    for j in range(2):
                        ins = v.tensor_tensor(oh[:, j], topf[:, :, j:j + 1].to_broadcast([P, T, E]), io, ALU.is_equal)
                    step(ins)
                    v.tensor_tensor(oh[:, 2], oh[:, 0], oh[:, 1], ALU.add).then_inc(s["oh_ready"], 1)
                    v.wait_ge(s["gexp_out"], 1)
                    step(v.reduce_sum(psel, r4[:, 0], AX.X))
                    step(v.tensor_scalar(rsum, ediff, 1.0, None, ALU.add))
                    step(v.tensor_tensor(psel, psel, rsum, ALU.mult))
                    step(v.reciprocal(gates[:, 0, :], psel))
                    v.tensor_tensor(gates[:, 1, :], gates[:, 0, :], ediff, ALU.mult)
                    v.wait_ge(pe_done, done("rank"))
                    own, inc = cnt[:, 0:3, :], [cnt[:, 3:6, :], cnt[:, 6:9, :]]
                    v.tensor_copy(rank[:, :, :], bank_of("rank")[:, 0:T * E].rearrange("p (t e) -> p t e", t=T))
                    total = bank_of("rank")[:, T * E:(T + 1) * E]
                    step(v.tensor_scalar(own[:, 0, :], total, float(P), None, ALU.min))
                    step(v.tensor_tensor(own[:, 1, :], total, own[:, 0, :], ALU.subtract))
                    v.sem_inc(dve_evac, 1)
                    step(v.tensor_scalar(own[:, 2, :], own[:, 1, :], 0.0, None, ALU.is_gt))
                    for n in range(1, S // P - 1):
                        step(v.scalar_tensor_tensor(own[:, 2, :], own[:, 1, :], float(n * P), own[:, 2, :],
                                                    ALU.is_gt, ALU.add))
                    src, m = own, 0
                    for d in (1, 2, 4, 8, 16):
                        dst = inc[m % 2]
                        v.tensor_copy(dst[:, :, 0:d], src[:, :, 0:d])
                        step(v.tensor_tensor(dst[:, :, d:], src[:, :, d:], src[:, :, 0:E - d], ALU.add))
                        src, m = dst, m + 1
                    step(v.tensor_tensor(exc[:, 0:3, :], src, own, ALU.subtract))
                    start0, start1, nbx, far = (exc[:, i, :] for i in range(4))
                    step(v.tensor_scalar(start1, start1, src[:, 0, E - 1:E], None, ALU.add))
                    step(v.scalar_tensor_tensor(far, start1, -float(P), start0, ALU.add, ALU.subtract))
                    every = [P, T, E]
                    v.scalar_tensor_tensor(rtmp[:, :, :], rank[:, :, :], float(P),
                                           far.unsqueeze(1).to_broadcast(every), ALU.is_ge, ALU.mult)
                    step(v.tensor_tensor(rank[:, :, :], rank[:, :, :], start0.unsqueeze(1).to_broadcast(every),
                                         ALU.add))
                    step(v.tensor_tensor(rank[:, :, :], rank[:, :, :], rtmp[:, :, :], ALU.add))
                    for j in range(2):
                        step(v.tensor_tensor(oh[:, j], oh[:, j], rank[:, :, :], ALU.mult))
                        step(v.tensor_reduce(posr[:, j, :], oh[:, j], AX.X, ALU.add))
                    v.tensor_copy(posu[:, :, :], posr)
                    one, many = slice(0, 1), [1, OVER_BLOCKS, E]
                    rel, inside, row = (ovm[one, i] for i in range(3))
                    step(v.tensor_tensor(rel, c("blk")[one].unsqueeze(2).to_broadcast(many),
                                         nbx[one].unsqueeze(1).to_broadcast(many), ALU.subtract))
                    v.tensor_tensor(inside, rel, own[one, 2].unsqueeze(1).to_broadcast(many), ALU.is_lt)
                    step(v.scalar_tensor_tensor(row, rel, float(P), start1[one].unsqueeze(1).to_broadcast(many),
                                                ALU.mult, ALU.add))
                    step(v.scalar_tensor_tensor(inside, rel, 0.0, inside, ALU.is_ge, ALU.mult))
                    v.tensor_tensor(row, row, inside, ALU.mult)
                    step(v.tensor_tensor(inside, inside, c("iota")[one].unsqueeze(1).to_broadcast(many), ALU.mult))
                    v.tensor_reduce(ovf[one, 0], inside, AX.X, ALU.add)
                    step(v.tensor_reduce(ovf[one, 1], row, AX.X, ALU.add))
                    v.tensor_copy(ovi[one, 0:2 * OVER_BLOCKS], ovf[one].rearrange("p a b -> p (a b)"))
                    v.tensor_copy(ovi[one, 2 * OVER_BLOCKS:2 * OVER_BLOCKS + 1], src[one, 2, E - 1:E])
                    v.tensor_copy(starti[:, :], start0[one]).then_inc(s["routed"], 1)

                    v.sem_inc(s["y_ready"], 1)

                    def multiply(e):
                        v.wait_ge(s["silu_done"], e + 1)
                        v.wait_ge(s["up_mm"], e + 1)
                        v.tensor_tensor(hid, UB[:, :], sgate, ALU.mult).then_inc(s["hid_ready"], 1)

                    def evacuate_y(e, b):
                        v.wait_ge(s["y_written"], (e + 1) * 16)
                        v.wait_ge(s["down_mm"], e + 1)
                        v.tensor_copy(ybuf[b][:, 0:512], YB[0][:, :])
                        v.tensor_copy(ybuf[b][:, 512:D], YB[1][:, :]).then_inc(s["y_ready"], 1)

                    multiply(0)
                    with v.Fori(0, E // 2 - 1) as i:
                        for b, e in ((1, 2 * i + 1), (0, 2 * i + 2)):
                            multiply(e)
                            evacuate_y(e - 1, 1 - b)
                    multiply(E - 1)
                    evacuate_y(E - 2, 0)
                    evacuate_y(E - 1, 1)

                @block.tensor
                def _(pe):
                    def finish(mm):
                        mm.then_inc(pe_done, 1)

                    pe.wait_ge(s["rows_in"], 16 * 10)
                    pe.transpose(bank_of("params")[:, 0:NROW], prow[:, :], ident[0:NROW, 0:NROW]).then_inc(pe_done, 1)
                    pe.wait_ge(s["taps_in"], 16)
                    pe.transpose(bank_of("taps")[:, 0:2 * TAPS], cwrow[:, :], ident[0:2 * TAPS, 0:2 * TAPS])\
                        .then_inc(pe_done, 1)

                    def turn_tokens(prefix):
                        for k in range(K):
                            await_bank(pe, f"{prefix}{k}")
                            for t in range(T):
                                mm = pe.transpose(bank_of(f"{prefix}{k}")[:, t * P:(t + 1) * P],
                                                  xn[:, t, k * P:(k + 1) * P], ident)
                            mm.then_inc(pe_done, 1)

                    def by_token(names, n, width):
                        w = chunk_view(n, width)
                        pe.wait_ge(*loaded(n))
                        for t in range(T):
                            await_bank(pe, f"{names}{t}")
                            for k in range(K):
                                mm = pe.matmul(bank_of(f"{names}{t}")[:, 0:width], hT[:, k, t * P:(t + 1) * P],
                                               w[:, k, :], start=(k == 0), stop=(k == K - 1))
                            mm.then_inc(pe_done, 1)

                    def by_channel(name, n, at):
                        w = chunk_view(n, 512)
                        await_bank(pe, name)
                        for k in range(K):
                            mm = pe.matmul(bank_of(name)[:, :], w[:, k, at:at + P], hT[:, k, :],
                                           start=(k == 0), stop=(k == K - 1))
                        mm.then_inc(pe_done, 1)

                    pe.wait_ge(s["xn_done"], 1)
                    turn_tokens("h")
                    pe.wait_ge(act_evac, emptied(f"h{K - 1}"))
                    by_token("A", 0, NA)
                    pe.wait_ge(*loaded(1))
                    for h in range(2):
                        by_channel(f"cg{h}", 1, G + h * P)
                        by_channel(f"ca{h}", 1, h * P)
                    pe.wait_ge(s["idx_roped"], 1)
                    for name, src in (("iqT", tokA[:, :, G:G + P]), ("ikT", ik4[:, :, :])):
                        await_bank(pe, name)
                        for t in range(T):
                            mm = pe.transpose(bank_of(name)[:, t * P:(t + 1) * P], src[:, t, :], ident)
                        mm.then_inc(pe_done, 1)
                    pe.wait_ge(act_evac, emptied("ikT"))
                    for b in range(1, T):
                        for h in range(IH):
                            name, r, w = f"idx{b}{h}", slice(h * ID, (h + 1) * ID), (b + 1) * P
                            await_bank(pe, name)
                            pe.matmul(bank_of(name)[:, 0:w], iqT[r, b * P:(b + 1) * P], ikT[r, 0:w],
                                      start=True, stop=True).then_inc(pe_done, 1)
                    by_token("B", 2, 512)
                    pe.wait_ge(*loaded(3))
                    for h in range(2):
                        by_channel(f"pool{h}", 3, h * P)
                    for h in range(2):
                        by_channel(f"u{h}", 3, G + h * P)
                    by_token("E", 4, G)
                    pe.wait_ge(s["qk_roped"], 1)
                    for j, head in ((0, "qT"), (1, "kT")):
                        for pair in range(2):
                            name, a = f"{head}{pair}", (2 * j + pair) * P
                            await_bank(pe, name)
                            for t in range(T):
                                mm = pe.transpose(bank_of(name)[:, t * P:(t + 1) * P], tokB[:, t, a:a + P], ident)
                            mm.then_inc(pe_done, 1)

                    def attention(b):
                        w = (b + 1) * P
                        if b == 0:
                            pe.wait_ge(act_evac, emptied("kT1"))
                        for h in range(HEADS):
                            name, r = f"logit{b}{h}", slice(64 * (h % 2), 64 * (h % 2) + 64)
                            await_bank(pe, name)
                            pe.matmul(bank_of(name)[:, 0:w].rearrange("p (t n) -> p t n", n=P), qT[r, h // 2, b * P:(b + 1) * P],
                                      kT[r, 0:b + 1, (h // 2) * P:(h // 2 + 1) * P],
                                      start=True, stop=True).then_inc(pe_done, 1)
                        pe.wait_ge(s["prob_ready"], b + 1)
                        for pair in range(2):
                            for h in (2 * pair, 2 * pair + 1):
                                name = f"probT{b}{h}"
                                await_bank(pe, name)
                                for kt in range(b + 1):
                                    mm = pe.transpose(bank_of(name)[:, kt * P:(kt + 1) * P],
                                                      prob[:, h, kt * P:(kt + 1) * P], ident)
                                mm.then_inc(pe_done, 1)
                            name = f"pv{b}{pair}"
                            await_bank(pe, name)
                            pe.wait_ge(act_evac, emptied(f"probT{b}{2 * pair + 1}"))
                            for h in (2 * pair, 2 * pair + 1):
                                o = 64 * (h % 2)
                                for kt in range(b + 1):
                                    mm = pe.matmul(bank_of(name)[o:o + 64, 0:P], tokA[:, kt, h * HD:(h + 1) * HD],
                                                   probT[:, h % 2, kt * P:(kt + 1) * P],
                                                   start=(kt == 0), stop=(kt == b))
                            mm.then_inc(pe_done, 1)

                    attention(0)
                    pe.wait_ge(s["sgu_in"], 16 * 7)
                    await_bank(pe, "sgw")
                    for h in range(SGU_H):
                        mm = pe.transpose(bank_of("sgw")[:, h * P:(h + 1) * P], sgw[:, h, :], ident)
                    mm.then_inc(pe_done, 1)
                    pe.wait_ge(s["sgu_normed"], 1)
                    pe.wait_ge(dve_evac, emptied("sgw"))
                    for pair in range(2):
                        name = f"sgu{pair}"
                        await_bank(pe, name)
                        for n in range(T):
                            for h in (2 * pair, 2 * pair + 1):
                                o = 64 * (h % 2)
                                mm = pe.matmul(bank_of(name)[o:o + 64, n * P:(n + 1) * P],
                                               dv[:, n, h * 64:(h + 1) * 64], sgwT[:, h, :], start=True, stop=True)
                        mm.then_inc(pe_done, 1)
                    pe.wait_ge(s["pooled"], 1)
                    pe.wait_ge(s["pw_in"], 16 * 5)
                    for h in range(2):
                        await_bank(pe, f"pl{h}")
                        pe.matmul(bank_of(f"pl{h}")[:, :], plw[:, h, :], wsum[0][:, h, 16:], start=True, stop=True)\
                            .then_inc(pe_done, 1)
                    attention(1)
                    pe.wait_ge(s["conv_done"], 2)
                    for h in range(2):
                        await_bank(pe, f"cmean{h}")
                        pe.matmul(bank_of(f"cmean{h}")[:, :], c("mean64"), acc[:, h, :], start=True, stop=True)\
                            .then_inc(pe_done, 1)
                        pe.wait_ge(s["centered_sq"], h + 1)
                        await_bank(pe, f"cvar{h}")
                        pe.matmul(bank_of(f"cvar{h}")[:, :], c("mean64"), sq[:, h, :], start=True, stop=True)\
                            .then_inc(pe_done, 1)
                    attention(2)
                    pe.wait_ge(s["swished"], 2)
                    for co in range(2):
                        await_bank(pe, f"pw{co}")
                        for ci in range(2):
                            mm = pe.matmul(bank_of(f"pw{co}")[:, :], pww[:, ci, co * P:(co + 1) * P], acc[:, ci, :],
                                           start=(ci == 0), stop=(ci == 1))
                        mm.then_inc(pe_done, 1)

                    def mean_square(g, n):
                        pe.wait_ge(s["mix_sq"], n + 1)
                        await_bank(pe, f"rms{g}")
                        for i in range(2):
                            mm = pe.matmul(bank_of(f"rms{g}")[:, :], c("mean256"), mix_sq_buf[n % 2][:, i, :],
                                           start=(i == 0), stop=(i == 1))
                        mm.then_inc(pe_done, 1)

                    mean_square(2, 0)
                    mean_square(3, 1)
                    attention(3)
                    mean_square(1, 2)
                    mean_square(0, 3)
                    pe.wait_ge(s["mix_normed"], 4)
                    for n in range(N_OUT):
                        pe.wait_ge(*loaded(N_IN + n))
                        w = chunk_view(N_IN + n, 512)
                        for t in range(T):
                            await_bank(pe, f"out{n}{t}")
                            for k in range(K):
                                mm = pe.matmul(bank_of(f"out{n}{t}")[:, :], mixT[:, k, t * P:(t + 1) * P],
                                               w[:, k, :], start=(k == 0), stop=(k == K - 1))
                            mm.then_inc(pe_done, 1)
                    pe.wait_ge(s["xn_done"], 2)
                    turn_tokens("m")
                    pe.wait_ge(act_evac, emptied(f"m{K - 1}"))
                    pe.wait_ge(s["router_in"], 64)
                    await_bank(pe, "route")
                    for t in range(T):
                        for k in range(K):
                            mm = pe.matmul(bank_of("route")[:, t * (NG + E):(t + 1) * (NG + E)],
                                           hT[:, k, t * P:(t + 1) * P], wr[:, k, :], start=(k == 0), stop=(k == K - 1))
                    mm.then_inc(pe_done, 1)
                    pe.wait_ge(s["oh_ready"], 1)
                    await_bank(pe, "rank")
                    for t in range(T + 1):
                        dst = bank_of("rank")[:, t * E:(t + 1) * E]
                        sides = [(c("ones"), u) for u in range(t)] + ([(c("before"), t)] if t < T else [])
                        for n, (m, u) in enumerate(sides):
                            mm = pe.matmul(dst, m, oh[:, 2, u, :], start=(n == 0), stop=(n == len(sides) - 1))
                    mm.then_inc(pe_done, 1)

                    def expert_matrix(j, k):
                        return ring[:, j % RING, :].rearrange("p (k n) -> p k n", k=k)

                    def turn_rows(count, b, times):
                        pe.wait_ge(xs_in[b], 16 * times)
                        for k in range(K):
                            mm = pe.transpose(XP[k // 4][:, (k % 4) * P:(k % 4 + 1) * P],
                                              xs[b][:, k * P:(k + 1) * P], ident)
                        mm.then_inc(s["xs_tr"], 1)

                    def first_product(n, fill, out_bank, b, signal):
                        w = expert_matrix(n, K)
                        pe.wait_ge(slot[n % RING], 16 * fill)
                        for k in range(K):
                            mm = pe.matmul(out_bank[:, :], xT[b][:, k, :], w[:, k, :],
                                           start=(k == 0), stop=(k == K - 1))
                        mm.then_inc(signal, 1)

                    def turn_hidden(e):
                        pe.wait_ge(s["hid_ready"], e + 1)
                        for k in range(4):
                            mm = pe.transpose(HB[:, k * P:(k + 1) * P], hid[:, k * P:(k + 1) * P], ident)
                        mm.then_inc(s["hid_tr"], 1)

                    def down(e, n, fill):
                        w = expert_matrix(n, 4)
                        pe.wait_ge(slot[n % RING], 16 * fill)
                        pe.wait_ge(s["hidt_ready"], e + 1)
                        pe.wait_ge(s["y_ready"], e + 1)
                        for half in range(2):
                            for k in range(4):
                                mm = pe.matmul(YB[half][:, :], hidT[:, k, :], w[:, k, half * 512:(half + 1) * 512],
                                               start=(k == 0), stop=(k == 3))
                        mm.then_inc(s["down_mm"], 1)

                    pe.wait_ge(s["routed"], 1)
                    turn_rows(0, 0, 1)
                    pe.wait_ge(s["xt_ready"], 1)
                    first_product(N_PRE, (N_PRE // RING) + 1, GB, 0, s["gate_mm"])
                    first_product(N_PRE + 1, (N_PRE + 1) // RING + 1, UB, 0, s["up_mm"])
                    turn_rows(1, 1, 1)

                    def step_expert(e, b, n, fill, times, rows=True):
                        pe.wait_ge(s["xt_ready"], e + 1)
                        pe.wait_ge(s["silu_done"], e)
                        first_product(n, fill, GB, b, s["gate_mm"])
                        turn_hidden(e - 1)
                        first_product(n + 1, fill, UB, b, s["up_mm"])
                        down(e - 1, n + 2, fill)
                        if rows:
                            turn_rows(e + 1, 1 - b, times)

                    with pe.Fori(0, E // 2 - 1) as i:
                        step_expert(2 * i + 1, 1, 9, i + 2, i + 2)
                        step_expert(2 * i + 2, 0, 12, i + 3, i + 2)
                    step_expert(E - 1, 1, 9, E // 2 + 1, 0, rows=False)
                    turn_hidden(E - 1)
                    n = N_CHUNKS - 1
                    down(E - 1, n, n // RING + 1)

            clear_semaphores()

            n_over = nc.values_load(ovi[0:1, 2 * OVER_BLOCKS:2 * OVER_BLOCKS + 1], min_val=0, max_val=OVER_BLOCKS)
            with nc.Fori(0, OVER_BLOCKS) as i:
                with nc.If(n_over > i):
                    with nc.Block() as block:
                        @block.sync
                        def _(sp):
                            e = sp.value_load(ovi[0:1, bass.ds(i, 1)], min_val=0, max_val=E - 1)
                            row = sp.value_load(ovi[0:1, bass.ds(i + OVER_BLOCKS, 1)], min_val=0, max_val=ROWS - P)
                            for j, (src, k) in enumerate(((wg_v, K), (wu_v, K), (wd_v, 4))):
                                sp.dma_start(ring[:, j, :].rearrange("p (k n) -> p k n", k=k),
                                             src[l, bass.ds(e, 1)].rearrange("e p k n -> (e p) k n"))\
                                    .then_inc(slot[j], 16)
                            sp.dma_start(xs[0], xs_dram[bass.ds(row, P), :]).then_inc(xs_in[0], 16)
                            sp.wait_ge(s["y_ready"], 1)
                            sp.dma_start(ys_dram[bass.ds(row, P), :], ybuf[0]).then_inc(s["y_written"], 16)
                            sp.wait_ge(s["y_written"], 16)

                        @block.gpsimd
                        def _(pool):
                            pool.memset(small[:, 228:229], 0.0)

                        @block.scalar
                        def _(act):
                            act.wait_ge(s["xs_tr"], 1)
                            for k in range(K):
                                ins = act.activation(xT[0][:, k, :], XP[k // 4][:, (k % 4) * P:(k % 4 + 1) * P],
                                                     ACT.Identity, scale=scl[:, 1, k:k + 1],
                                                     bias=pcol[:, SHIFT2 * K + k:SHIFT2 * K + k + 1])
                            ins.then_inc(s["xt_ready"], 1)
                            act.wait_ge(s["gate_mm"], 1)
                            act.activation(sgate, GB[:, :], ACT.Silu).then_inc(s["silu_done"], 1)
                            act.wait_ge(s["hid_tr"], 1)
                            act.activation(hidT, HB[:, :].rearrange("p (k s) -> p k s", k=4), ACT.Copy)\
                               .then_inc(s["hidt_ready"], 1)

                        @block.vector
                        def _(v):
                            v.wait_ge(s["silu_done"], 1)
                            v.wait_ge(s["up_mm"], 1)
                            v.tensor_tensor(hid, UB[:, :], sgate, ALU.mult).then_inc(s["hid_ready"], 1)
                            v.wait_ge(s["down_mm"], 1)
                            v.tensor_copy(ybuf[0][:, 0:512], YB[0][:, :])
                            v.tensor_copy(ybuf[0][:, 512:D], YB[1][:, :]).then_inc(s["y_ready"], 1)

                        @block.tensor
                        def _(pe):
                            pe.wait_ge(xs_in[0], 16)
                            for k in range(K):
                                mm = pe.transpose(XP[k // 4][:, (k % 4) * P:(k % 4 + 1) * P],
                                                  xs[0][:, k * P:(k + 1) * P], ident)
                            mm.then_inc(s["xs_tr"], 1)
                            pe.wait_ge(s["xt_ready"], 1)
                            for j, (dst, signal) in enumerate(((GB, s["gate_mm"]), (UB, s["up_mm"]))):
                                w = ring[:, j, :].rearrange("p (k n) -> p k n", k=K)
                                pe.wait_ge(slot[j], 16)
                                for k in range(K):
                                    mm = pe.matmul(dst[:, :], xT[0][:, k, :], w[:, k, :],
                                                   start=(k == 0), stop=(k == K - 1))
                                mm.then_inc(signal, 1)
                            pe.wait_ge(s["hid_ready"], 1)
                            for k in range(4):
                                mm = pe.transpose(HB[:, k * P:(k + 1) * P], hid[:, k * P:(k + 1) * P], ident)
                            mm.then_inc(s["hid_tr"], 1)
                            pe.wait_ge(s["hidt_ready"], 1)
                            pe.wait_ge(slot[2], 16)
                            w = ring[:, 2, :].rearrange("p (k n) -> p k n", k=4)
                            for half in range(2):
                                for k in range(4):
                                    mm = pe.matmul(YB[half][:, :], hidT[:, k, :],
                                                   w[:, k, half * 512:(half + 1) * 512],
                                                   start=(k == 0), stop=(k == 3))
                            mm.then_inc(s["down_mm"], 1)
                    clear_semaphores()

            with nc.Block() as block:
                @block.sync
                def _(sp):
                    sp.dma_start(g2b, mod_dram.rearrange("(m r) p -> m (r p)", r=K)
                                 [bass.ds(l * 6 + GATE2, 1), :].partition_broadcast(P)).then_inc(s["gate2_in"], 16)
                    sp.wait_ge(s["gate2_in"], 16)

                @block.gpsimd
                def _(pool):
                    for t in range(T):
                        if t >= 2:
                            pool.wait_ge(s["combined"], t - 1)
                        for j in range(2):
                            pool.indirect_dma_start(
                                got[t % 2][j], None, ys_dram,
                                bass.IndirectOffsetOnAxis(ap=posu[:, j, t:t + 1], axis=0),
                                bounds_check=ROWS - 1, oob_is_err=True).then_inc(got_in[t % 2], 16)

                @block.scalar
                def _(act):
                    for t in range(T):
                        act.wait_ge(got_in[t % 2], l * (16 * T) + 32 * (t // 2 + 1))
                        act.activation(got[t % 2][0], got[t % 2][0], ACT.Copy, scale=gates[:, 0, t:t + 1])\
                           .then_inc(s["scaled"], 1)

                @block.vector
                def _(v):
                    step = stepper(v, dve_step)
                    v.wait_ge(s["gate2_in"], 16)
                    for t in range(T):
                        a, b = got[t % 2]
                        v.wait_ge(s["scaled"], t + 1)
                        step(v.scalar_tensor_tensor(b, b, gates[:, 1, t:t + 1], a, ALU.mult, ALU.add))
                        step(v.tensor_tensor(b, b, g2b, ALU.mult))
                        v.tensor_tensor(x[:, t, :], x[:, t, :], b, ALU.add).then_inc(s["combined"], 1)
            clear_semaphores()

        with nc.Block() as block:
            @block.sync
            def _(sp):
                sp.dma_start(out_tok, x[:, :, :]).then_inc(s["stored"], 16)
                sp.wait_ge(s["stored"], 16)


_INS = ["x", "c", "positions", "w_ada", "b_ada", "norm1", "w_in", "q_norm", "k_norm", "conv_w", "conv_b",
        "conv_ln_g", "conv_ln_b", "conv_pw_w", "conv_pw_b", "pool_w", "pool_b", "pool_scale", "sgu_ln_g",
        "sgu_ln_b", "sgu_w", "sgu_b", "out_norm", "w_out", "norm2", "w_rg", "b_rg", "w_re", "b_re", "w_gate",
        "w_up", "w_down"]


def kernel(**inputs):
    import concourse.bacc as _bacc
    from concourse.bass_utils import run_bass_kernel_spmd as _run

    arrays = {name: np.ascontiguousarray(inputs[name]) for name in _INS}
    arrays["constants"] = constants()[0]
    nc = _bacc.Bacc("TRN2", target_bir_lowering=False, num_devices=1)
    A = {name: nc.dram_tensor(f"in_{name}", a.shape, mybir.dt.from_np(a.dtype), kind="ExternalInput").ap()
         for name, a in arrays.items()}
    out = nc.dram_tensor("out_0", (1, S, D), F32, kind="ExternalOutput").ap()
    build(nc, A, out)
    r = _run(nc, [{f"in_{name}": a for name, a in arrays.items()}], core_ids=[0])
    return r.results[0]["out_0"]
```

```python
from contextlib import ExitStack

import numpy as np

import concourse.bass as bass
from concourse import mybir

F32 = mybir.dt.float32
I32 = mybir.dt.int32
U32 = mybir.dt.uint32
ALU = mybir.AluOpType
ACT = mybir.ActivationFunctionType
AX = mybir.AxisListType

P = 128
D = 1024
S = 512
DEPTH = 2
T = S // P
K = D // P
G = D // 4
HEADS, HD = 4, 64
ROT = HD // 8
IH, ID = 4, 32
IROT = ID // 8
CHUNK = 64
TOPK = min(256, S // 4)
TAPS = 31
SGU_H = 4
NG, EPG = 4, 8
E = NG * EPG
FF = 512
EPS = 1e-6
THETA = 500000.0
D_IN = 8 * G + IH * ID + ID + IH

C_Q, C_V, C_CONV = 0, 2 * G, 3 * G + IH * ID + ID + IH
C_POOL, C_SGU = C_CONV + 2 * G, C_CONV + 3 * G
NA = C_CONV - C_V

R_MOD, R_N1, R_N2, R_ON, R_CB, R_LG, R_LB, R_PB, R_QB, R_QS = 0, 48, 56, 64, 72, 74, 76, 78, 80, 82
NROW = 84
SHIFT1, SCALE1, GATE1, SHIFT2, SCALE2, GATE2 = range(6)

RING = 6
ADA_COLS = 512
ADA_CHUNKS = 6 * D // ADA_COLS
N_IN, N_OUT = 5, 2
N_PRE = N_IN + N_OUT
N_CHUNKS = N_PRE + 3 * E

OVER_BLOCKS = 7
ROWS = 2 * S + P
NEG = -3.0e38
GONE = -3.4e38
MASK = -1.0e30
MAGIC = 12582912.0
TWO_PI = 2 * np.pi
PI1 = 6.28125
PI2 = float(np.float32(TWO_PI - PI1) - np.float32(TWO_PI - PI1) % np.float32(2.0 ** -20))
PI3 = float(TWO_PI - PI1 - PI2)


def constants():
    p = np.arange(P)[:, None]
    j = np.arange(P)[None, :]
    parts = {
        "ident": (p == j),
        "mean256": np.full((P, P), 1.0 / G),
        "mean64": (p // 64 == j // 64) / 64.0,
        "upto": (p <= j),
        "before": (p < j),
        "ones": np.ones((P, P)),
        "mask0": np.where((p < CHUNK) & (j >= CHUNK), MASK, 0.0),
        "iota": np.broadcast_to(np.arange(E), (P, E)),
        "invf": np.broadcast_to(np.concatenate([
            np.power(np.float32(THETA), (-2.0 * np.arange(ROT, dtype=np.float32) / np.float32(2 * ROT))),
            np.power(np.float32(THETA), (-2.0 * np.arange(IROT, dtype=np.float32) / np.float32(2 * IROT))),
        ]), (P, ROT + IROT)),
        "eps": np.full((P, 1), EPS),
    }
    win = np.array([2, 4, 8, 16])
    own = np.stack([win[0 + (p[:, 0] // 64)], win[2 + (p[:, 0] // 64)]], 1)
    parts["invw"] = 1.0 / own
    first = np.minimum(np.arange(1, 17)[None, None, :], own[:, :, None])
    parts["invc"] = (1.0 / first).reshape(P, 32)
    parts["blk"] = np.broadcast_to(np.arange(OVER_BLOCKS), (P, OVER_BLOCKS))
    where, at = {}, 0
    for name, a in parts.items():
        where[name] = (at, at + a.shape[1])
        at += a.shape[1]
    return np.concatenate([np.asarray(a, np.float32) for a in parts.values()], 1), where


def build(nc, A, out, debug=None):
    ctx = ExitStack()
    cw = constants()[1]
    NCONST = max(b for _, b in cw.values())

    def sb(name, shape, dt=F32):
        return ctx.enter_context(nc.sbuf_tensor(name, shape, dt))

    sems = []

    def sem(name, cleared=True):
        q = ctx.enter_context(nc.semaphore(name))
        if cleared:
            sems.append(q)
        return q

    mod_dram = nc.dram_tensor("mod_scratch", [DEPTH * 48, P], F32, kind="Internal").ap()
    xs_dram = nc.dram_tensor("sorted_tokens", [ROWS, D], F32, kind="Internal").ap()
    ys_dram = nc.dram_tensor("sorted_outputs", [ROWS, D], F32, kind="Internal").ap()
    x_tok = A["x"].rearrange("b (t p) d -> p (b t) d", p=P)
    out_tok = out.rearrange("b (t p) d -> p (b t) d", p=P)
    ada_v = A["w_ada"].rearrange("l (k p) n -> l p k n", p=P)
    win_v = A["w_in"].rearrange("l (k p) n -> l p k n", p=P)
    wout_v = A["w_out"].rearrange("l (k p) n -> l p k n", p=P)
    wg_v = A["w_gate"].rearrange("l e (k p) n -> l e p k n", p=P)
    wu_v = A["w_up"].rearrange("l e (k p) n -> l e p k n", p=P)
    wd_v = A["w_down"].rearrange("l e (k p) n -> l e p k n", p=P)

    with ctx:
        cst = sb("cst", [P, NCONST])

        def c(name):
            a, b = cw[name]
            return cst[:, a:b]

        ident = c("ident")
        x = sb("x_resident", [P, T, D])
        ring = sb("ring", [P, RING, 4096])
        work = sb("work", [P, 2 * 4096 + 4752])
        hT = work[:, 0:4096].rearrange("p (k s) -> p k s", k=K)
        mixT = work[:, 4096:8192].rearrange("p (k s) -> p k s", k=K)
        xn = work[:, 4096:8192].rearrange("p (t d) -> p t d", t=T)
        tokA = work[:, 8192:8192 + T * NA].rearrange("p (t n) -> p t n", t=T)
        tokB = work[:, 8192 + T * NA:8192 + T * (NA + 512)].rearrange("p (t n) -> p t n", t=T)
        dv = work[:, 8192 + T * (NA + 512):].rearrange("p (t n) -> p t n", t=T)
        prob = work[:, 0:2048].rearrange("p (h n) -> p h n", h=HEADS)
        probT = work[:, 2048:3072].rearrange("p (b n) -> p b n", b=2)
        xT = [work[:, i * 1024:(i + 1) * 1024].rearrange("p (k s) -> p k s", k=K) for i in range(2)]
        sgate = work[:, 2048:2560]
        hid = work[:, 2560:3072]
        hidT = work[:, 3072:3584].rearrange("p (k s) -> p k s", k=4)
        xs = [work[:, 4096 + i * 1024:5120 + i * 1024] for i in range(2)]
        ybuf = [work[:, 6144 + i * 1024:7168 + i * 1024] for i in range(2)]
        xn2 = work[:, 0:4096].rearrange("p (t d) -> p t d", t=T)
        h2T = mixT
        got = [[work[:, 4096 + (2 * t + j) * 1024:5120 + (2 * t + j) * 1024] for j in range(2)] for t in range(T)]
        mrow = work[0:1, 0:DEPTH * 6 * D]
        score = sb("score", [P, 1152])
        crow = score[0:K, 0:P]
        ccol = sb("ccol", [P, K])
        posi = sb("posi", [P, T], I32)
        posf = sb("posf", [P, T])
        ang = sb("ang", [P, T, ROT + IROT])
        turn = sb("turn", [P, T, ROT + IROT])
        sn = sb("sn", [P, T, ROT + IROT])
        cs = sb("cs", [P, T, ROT + IROT])
        prow = sb("prow", [NROW, P])
        cwrow = sb("cwrow", [2 * TAPS, P])
        pcol = sb("pcol", [P, NROW])
        cwcol = sb("cwcol", [P, 2 * TAPS])
        scl = sb("scl", [P, 2, K])
        qkn = sb("qkn", [P, 2, HD])
        sgn = sb("sgn", [P, 2, G])
        sgb = sb("sgb", [P, 2, P])
        sgw = sb("sgw", [P, SGU_H, P])
        sgwT = sb("sgwT", [P, SGU_H, P])
        pww = sb("pww", [P, 2, G])
        plw = sb("plw", [P, 2, P])
        wr = sb("wr", [P, K, NG + E])
        rb = sb("rb", [P, NG + E])
        convin = sb("convin", [P, 2, TAPS - 1 + S])
        ada_sum = [convin[:, i, 0:ADA_COLS] for i in range(2)]
        acc = mixT[:, 2:4, :]
        uT = mixT[:, 6:8, :]
        sig = uT
        poolin = sb("poolin", [P, 2, 16 + S])
        qT = work[:, 3072:4096].rearrange("p (h n) -> p h n", h=2)
        kT = tokB[:, :, 0:2 * P]
        sums_tile = sb("window_sums", [P, 2 * 2 * (16 + S)])
        wsum = [sums_tile[:, i * 2 * (16 + S):(i + 1) * 2 * (16 + S)].rearrange("p (h n) -> p h n", h=2)
                for i in range(2)]
        iqT, ikT = wsum[0][:, 0, 0:S], wsum[0][:, 1, 0:S]
        tokB_flat = work[:, 8192 + T * NA:8192 + T * (NA + 512)]
        ik4 = tokB_flat[:, 0:S].rearrange("p (t n) -> p t n", t=T)
        sq = sb("sq", [P, 2, S])
        relu = [tokB_flat[:, (1 + i) * S:(2 + i) * S] for i in range(2)]
        SC = [0, 0, 256, 640]
        g1b = convin[:, :, :].rearrange("p h n -> p (h n)")[:, 0:D]
        g2b = work[:, 0:D]
        small = sb("small", [P, 256])
        ss = small[:, 0:4]
        rs = small[:, 4:8]
        ssq = small[:, 8:40]
        rsq = small[:, 40:72]
        m8 = small[:, 72:80]
        mx = small[:, 80:84]
        nmx = small[:, 84:88]
        sums = small[:, 88:92]
        rsum = small[:, 92:96]
        bst = small[:, 96:120].rearrange("p (t n) -> p t n", t=T)
        bag = small[:, 120:128].rearrange("p (t n) -> p t n", t=T)
        rdv = small[:, 128:132]
        gidx = small[:, 132:136]
        gmax = small[:, 136:140]
        psel = small[:, 140:144]
        gates = small[:, 144:152].rearrange("p (j t) -> p j t", j=2)
        posr = small[:, 152:160].rearrange("p (j t) -> p j t", j=2)
        top8 = small[:, 160:192].rearrange("p (t n) -> p t n", t=T)
        topf = small[:, 192:224].rearrange("p (t n) -> p t n", t=T)
        ediff = small[:, 224:228]
        ropet = sq[:, :, :].rearrange("p h n -> p (h n)").rearrange("p (i t h r) -> p i t h r", i=4, t=T, h=8)
        sq_flat = sq[:, :, :].rearrange("p h n -> p (h n)")
        taken = [0]

        def late(*shape):
            n = int(np.prod(shape))
            a = taken[0]
            taken[0] += n
            assert taken[0] <= 4 * (16 + S)
            flat = sums_tile[:, a:a + n]
            if len(shape) == 2:
                return flat.rearrange("p (a b) -> p a b", a=shape[0])
            return flat.rearrange("p (a b c) -> p a b c", a=shape[0], b=shape[1])

        lg = late(T, NG + E)
        r4 = late(3, T, NG)
        el = late(T, E)
        oh = late(3, T, E)
        rank = late(T, E)
        rtmp = late(T, E)
        cnt = late(9, E)
        exc = late(4, E)
        ovm = late(3, OVER_BLOCKS, E)
        topi = sb("topi", [P, T, 8], U32)
        ovf = sb("ovf", [P, 2, OVER_BLOCKS])
        posu = sb("posu", [P, 2, T], U32)
        starti = sb("starti", [1, E], I32)
        ovi = sb("ovi", [1, 16], I32)

        bank = [ctx.enter_context(nc.psum_tensor(f"bank{i}", [P, 512], F32)) for i in range(8)]

        GB, UB, HB = bank[0], bank[1], bank[2]
        YB, XP = bank[3:5], bank[5:7]
        mix_sq_buf = {3: sq[:, :, :], 2: wsum[0][:, :, 16:], 1: wsum[1][:, :, 16:], 0: wsum[0][:, :, 16:]}
        rmix = small[:, 232:248].rearrange("p (g t) -> p g t", g=4)

        slot = [sem(f"slot{i}_loaded") for i in range(RING)]
        pe_done = sem("pe_done")
        act_evac = sem("act_evac")
        dve_evac = sem("dve_evac")
        act_step = sem("act_step")
        dve_step = sem("dve_step")
        pool_step = sem("pool_step")
        xs_in = [sem(f"xs_in{i}") for i in range(2)]
        zeroed = sem("zeroed", cleared=False)
        scattered = sem("scattered", cleared=False)
        got_in = [sem(f"got_in{t}", cleared=False) for t in range(T)]
        s = {name: sem(name) for name in (
            "consts_in", "x_in", "c_in", "pos_in", "bada_in", "mod_out", "rows_in", "taps_in",
            "norms_in", "sgu_in", "pw_in", "router_in", "gate1_in", "gate2_in", "y_written", "stored",
            "mod_done", "mod_evac", "c_silu", "turns_ready", "ada_summed", "ada_step",
            "rstd_done", "xn_done", "scl_ready", "conv_in", "idx_roped", "relu_free", "conv_done",
            "qk_ss", "qk_rstd", "qk_roped", "sgu_var", "sgu_rstd", "sgu_normed", "pool_in", "pooled", "exp_in",
            "exp_done", "prob_ready", "centered", "centered_sq", "conv_sd", "conv_normed", "swished", "mix_ready",
            "mix_sq", "wout_scaled", "x_added",
            "gexp_in", "gexp_out", "oh_ready", "rows_known", "routed",
            "gate_mm", "up_mm", "hid_tr", "down_mm", "xs_tr", "xt_ready", "silu_done", "hid_ready", "hidt_ready",
            "y_ready", "scaled", "combined")}

        def clear_semaphores():
            nums = sorted(q.num for q in sems)
            kept = [q.num for q in (zeroed, scattered, *got_in)]
            nc.all_engine_barrier()
            nc.gpsimd.sem_clear(range(nums[0], kept[0]))
            nc.gpsimd.sem_clear(range(kept[-1] + 1, nums[-1] + 1))
            nc.all_engine_barrier()

        def stepper(eng, done):
            n = [0]

            def step(ins):
                n[0] += 1
                ins.then_inc(done, 1)
                eng.wait_ge(done, n[0])
            return step

        HALF = ADA_CHUNKS // RING
        with nc.Block() as block:
            @block.sync
            def _(sp):
                sp.dma_start(cst[:, :], A["constants"]).then_inc(s["consts_in"], 16)
                with sp.Fori(0, DEPTH) as l:
                    with sp.Fori(0, HALF) as i:
                        for j in range(RING):
                            src = ada_v[l, :, :, bass.ds((i * RING + j) * ADA_COLS, ADA_COLS)]
                            dst = ring[:, j, :].rearrange("p (k n) -> p k n", k=K)
                            sp.wait_ge(s["ada_summed"], (l * HALF + i) * RING + j + 1)
                            sp.dma_start(dst, src).then_inc(slot[j], 16)
                sp.dma_start(x[:, :, :], x_tok).then_inc(s["x_in"], 16)
                sp.wait_ge(s["x_in"], 16)

            @block.scalar
            def _(act):
                act.sem_inc(s["mod_evac"], RING)
                act.dma_start(crow[:, :], A["c"].rearrange("b (k p) -> (b k) p", p=P)).then_inc(s["c_in"], 16)
                act.dma_start(posi[:, :], A["positions"].rearrange("b (t p) -> p (b t)", p=P),
                              allow_slow_non_contiguous=True).then_inc(s["pos_in"], 16)
                act.dma_start(mrow, A["b_ada"].rearrange("(a l) n -> a (l n)", a=1)).then_inc(s["bada_in"], 16)
                act.wait_ge(s["c_in"], 16)
                act.activation(crow[:, :], crow[:, :], ACT.Silu).then_inc(s["c_silu"], 1)
                with act.Fori(0, DEPTH) as l:
                    with act.Fori(0, HALF) as i:
                        for j in range(RING):
                            at = act.snap(((l * HALF + i) * RING + j) * ADA_COLS)
                            act.wait_ge(s["mod_done"], (l * HALF + i) * RING + j + 1 + 2)
                            act.activation(mrow[:, bass.ds(at, ADA_COLS)], bank[j][0:1, :], ACT.Copy)\
                               .then_inc(s["mod_evac"], 1)
                act.wait_ge(s["mod_evac"], RING + DEPTH * ADA_CHUNKS)
                act.dma_start(mod_dram.rearrange("(a r) p -> a (r p)", a=1), mrow).then_inc(s["mod_out"], 16)
                act.wait_ge(s["turns_ready"], 1)
                act.activation(sn[:, :, :], ang[:, :, :], ACT.Sin)
                act.activation(cs[:, :, :], turn[:, :, :], ACT.Sin)
                act.wait_ge(s["mod_out"], 16)

            @block.vector
            def _(v):
                step = stepper(v, dve_step)
                v.memset(poolin[:, :, 0:16], 0.0)
                v.memset(plw[:, :, :], 0.0)
                v.wait_ge(s["consts_in"], 16)
                v.wait_ge(s["pos_in"], 16)
                nf = ROT + IROT
                step(v.tensor_copy(posf[:, :], posi[:, :]))
                step(v.tensor_tensor(ang[:, :, :], posf[:, :].unsqueeze(2).to_broadcast([P, T, nf]),
                                     c("invf").unsqueeze(1).to_broadcast([P, T, nf]), ALU.mult))
                step(v.tensor_scalar(turn[:, :, :], ang[:, :, :], 1.0 / TWO_PI, MAGIC, ALU.mult, ALU.add))
                step(v.tensor_scalar(turn[:, :, :], turn[:, :, :], MAGIC, None, ALU.subtract))
                for part in (PI1, PI2, PI3):
                    step(v.scalar_tensor_tensor(ang[:, :, :], turn[:, :, :], -part, ang[:, :, :],
                                                ALU.mult, ALU.add))
                step(v.tensor_scalar(ang[:, :, :], ang[:, :, :], 3.1415925, -3.1415925, ALU.min, ALU.max))
                step(v.tensor_scalar(turn[:, :, :], ang[:, :, :], -1.0, None, ALU.mult))
                step(v.tensor_tensor(turn[:, :, :], turn[:, :, :], ang[:, :, :], ALU.min))
                v.tensor_scalar(turn[:, :, :], turn[:, :, :], float(np.pi / 2), None, ALU.add)\
                    .then_inc(s["turns_ready"], 1)
                v.wait_ge(pe_done, 1)
                v.tensor_copy(ccol[:, :], bank[7][:, 0:K]).then_inc(dve_evac, 1)
                v.wait_ge(dve_evac, 1)
                v.sem_inc(s["ada_summed"], RING)
                with v.Fori(0, DEPTH) as l:
                    with v.Fori(0, HALF) as i:
                        for j in range(RING):
                            w = ring[:, j, :].rearrange("p (k n) -> p k n", k=K)
                            dst = ada_sum[j % 2]
                            v.wait_ge(slot[j], (l * HALF + i + 1) * 16)
                            v.wait_ge(s["mod_done"], (l * HALF + i) * RING + j + 1)
                            for k in range(K):
                                if k == 0:
                                    ins = v.tensor_scalar(dst, w[:, k, :], ccol[:, k:k + 1], None, ALU.mult)
                                else:
                                    ins = v.scalar_tensor_tensor(dst, w[:, k, :], ccol[:, k:k + 1], dst,
                                                                 ALU.mult, ALU.add)
                                if k < K - 1:
                                    ins.then_inc(s["ada_step"], 1)
                                    v.wait_ge(s["ada_step"], ((l * HALF + i) * RING + j) * (K - 1) + k + 1)
                            ins.then_inc(s["ada_summed"], 1)

            @block.gpsimd
            def _(pool):
                pool.memset(sq[:, :, :], 0.0).then_inc(pool_step, 1)
                pool.wait_ge(pool_step, 1)
                zero = sq[:, :, :].rearrange("p h n -> p (h n)")
                for b in range((ROWS - 2 * S) // P):
                    for scratch in (xs_dram, ys_dram):
                        pool.dma_start(scratch[2 * S + b * P:2 * S + (b + 1) * P, :], zero)\
                            .then_inc(zeroed, 16)
                pool.wait_ge(zeroed, 2 * 16 * ((ROWS - 2 * S) // P))

            @block.tensor
            def _(pe):
                pe.sem_inc(s["mod_done"], 2)
                pe.wait_ge(s["consts_in"], 16)
                pe.wait_ge(s["c_silu"], 1)
                pe.transpose(bank[7][:, 0:K], crow[:, :], ident[0:K, 0:K]).then_inc(pe_done, 1)
                pe.wait_ge(s["bada_in"], 16)
                with pe.Fori(0, DEPTH) as l:
                    with pe.Fori(0, HALF) as i:
                        for j in range(RING):
                            at = pe.snap(((l * HALF + i) * RING + j) * ADA_COLS)
                            pe.wait_ge(s["ada_summed"], (l * HALF + i) * RING + j + 1 + RING)
                            pe.wait_ge(s["mod_evac"], (l * HALF + i) * RING + j + 1)
                            pe.matmul(bank[j][:, :], c("ones"), ada_sum[j % 2], start=True, stop=False)
                            pe.matmul(bank[j][:, :], c("ones")[0:1, :], mrow[:, bass.ds(at, ADA_COLS)],
                                      start=False, stop=True).then_inc(s["mod_done"], 1)
        clear_semaphores()

        jobs = [("params", "dve"), ("taps", "dve")]
        jobs += [(f"h{k}", "act") for k in range(K)]
        jobs += [(f"A{t}", "act") for t in range(T)]
        jobs += [("cg0", "act"), ("ca0", "dve"), ("cg1", "act"), ("ca1", "dve"), ("iqT", "act"), ("ikT", "act")]
        jobs += [(f"idx{b}{h}", "act") for b in range(1, T) for h in range(IH)]
        jobs += [(f"B{t}", "act") for t in range(T)]
        jobs += [("pool0", "act"), ("pool1", "act"), ("u0", "act"), ("u1", "act")]
        jobs += [(f"E{t}", "act") for t in range(T)]
        jobs += [("qT0", "act"), ("qT1", "act"), ("kT0", "act"), ("kT1", "act")]

        def logit_jobs(b):
            return [(f"logit{b}{h}", "dve") for h in range(HEADS)]

        def value_jobs(b):
            out_ = []
            for pair in range(2):
                out_ += [(f"probT{b}{2 * pair}", "act"), (f"probT{b}{2 * pair + 1}", "act"), (f"pv{b}{pair}", "act")]
            return out_

        TN = [(t, n) for t in range(T) for n in range(N_OUT)]

        def out_jobs(g, tn):
            return [(f"out{g}{t}{n}", "dve") for t, n in tn]

        jobs += logit_jobs(0) + [("sgw", "dve")] + value_jobs(0) + [("sgu0", "dve"), ("sgu1", "dve")]
        jobs += logit_jobs(1) + [("ms3", "act")] + value_jobs(1)
        jobs += logit_jobs(2) + out_jobs(3, TN[:4]) + value_jobs(2)
        jobs += [("pl0", "dve"), ("pl1", "dve"), ("cmean0", "dve"), ("cmean1", "dve")] + out_jobs(3, TN[4:])
        jobs += [("ms2", "act"), ("cvar0", "act"), ("cvar1", "act")] + out_jobs(2, TN[:4])
        jobs += [("pw0", "dve"), ("pw1", "dve")] + out_jobs(2, TN[4:]) + [("ms1", "act")] + out_jobs(1, TN[:2])
        jobs += logit_jobs(3) + out_jobs(1, TN[2:]) + value_jobs(3) + [("ms0", "act")] + out_jobs(0, TN)
        jobs += [(f"m{k}", "act") for k in range(K)]
        jobs += [("route", "dve"), ("rank", "dve")]
        index = {name: i for i, (name, _) in enumerate(jobs)}

        def done(name):
            return index[name] + 1

        def emptied(name):
            i = index[name]
            return sum(1 for _, e in jobs[:i + 1] if e == jobs[i][1])

        def bank_of(name):
            return bank[index[name] % 8]

        def await_bank(pe, name):
            i = index[name] - 8
            if i >= 0:
                pe.wait_ge(act_evac if jobs[i][1] == "act" else dve_evac, emptied(jobs[i][0]))

        IN_COLS = [(C_V, NA), (C_CONV, 2 * G), (C_Q, 2 * G), (C_POOL, 2 * G), (C_SGU + G, G)]
        IN_LAST = ["A3", "ca1", "B3", "u1", "E3", "out030", "out031"]

        def chunk_view(n, width):
            return ring[:, n % RING, 0:K * width].rearrange("p (k n) -> p k n", k=K)

        def loaded(n):
            return slot[n % RING], 16 * (n // RING + 1)

        with nc.Fori(0, DEPTH) as l:
            with nc.Block() as block:
                @block.sync
                def _(sp):
                    def expert_chunk(n, kind, e):
                        src = {"g": wg_v, "u": wu_v, "d": wd_v}[kind][l, e]
                        k = K if kind in "gu" else FF // P
                        sp.dma_start(ring[:, n % RING, :].rearrange("p (k n) -> p k n", k=k), src)\
                            .then_inc(slot[n % RING], 16)

                    def static_wait(n):
                        if n >= RING:
                            sp.wait_ge(pe_done, done(IN_LAST[n - RING]))

                    sp.dma_start(prow[R_MOD:R_MOD + 48, :], mod_dram[bass.ds(l * 48, 48), :])\
                      .then_inc(s["rows_in"], 16)
                    for r, name, n in ((R_N1, "norm1", K), (R_N2, "norm2", K), (R_ON, "out_norm", K),
                                       (R_CB, "conv_b", 2), (R_LG, "conv_ln_g", 2), (R_LB, "conv_ln_b", 2),
                                       (R_PB, "conv_pw_b", 2), (R_QS, "pool_scale", 2)):
                        sp.dma_start(prow[r:r + n, :], A[name][l].rearrange("(r p) -> r p", p=P))\
                          .then_inc(s["rows_in"], 16)
                    sp.dma_start(prow[R_QB:R_QB + 2, :], A["pool_b"][l].rearrange("(r a) c -> r (a c)", a=2))\
                      .then_inc(s["rows_in"], 16)
                    sp.dma_start(cwrow[:, :], A["conv_w"][l].rearrange("w (h p) -> (w h) p", p=P))\
                      .then_inc(s["taps_in"], 16)
                    for n, (a, w) in enumerate(IN_COLS):
                        sp.dma_start(chunk_view(n, w), win_v[l, :, :, a:a + w]).then_inc(slot[n], 16)
                    for j in range(N_OUT):
                        n = N_IN + j
                        static_wait(n)
                        sp.dma_start(chunk_view(n, 512), wout_v[l, :, :, j * 512:(j + 1) * 512])\
                            .then_inc(slot[n % RING], 16)
                    for n, (kind, e) in enumerate([("g", 0), ("u", 0), ("g", 1), ("u", 1), ("d", 0), ("g", 2)], N_PRE):
                        static_wait(n)
                        expert_chunk(n, kind, e)
                    sp.sem_inc(s["y_written"], 16)
                    sp.wait_ge(s["routed"], 1)

                    def write_y(e):
                        row = sp.value_load(starti[0:1, bass.ds(e, 1)], min_val=0, max_val=2 * S)
                        dst = ys_dram[bass.ds(row, P), :]
                        return dst

                    def step_pair(i, first=False, last=False):
                        n = 13
                        sp.wait_ge(s["gate_mm"] if first else s["up_mm"], 1 if first else 2 * i + 1)
                        expert_chunk(n, "u", 2 * i + 2)
                        if first:
                            sp.wait_ge(s["up_mm"], 1)
                        else:
                            sp.wait_ge(s["down_mm"], 2 * i)
                        expert_chunk(n + 1, "d", 2 * i + 1)
                        if not first:
                            dst = write_y(2 * i - 1)
                            sp.wait_ge(s["y_ready"], 2 * i + 1)
                            sp.dma_start(dst, ybuf[1]).then_inc(s["y_written"], 16)
                        sp.wait_ge(s["gate_mm"], 2 * i + 2)
                        expert_chunk(n + 2, "g", 2 * i + 3)
                        sp.wait_ge(s["up_mm"], 2 * i + 2)
                        expert_chunk(n + 3, "u", 2 * i + 3)
                        sp.wait_ge(s["down_mm"], 2 * i + 1)
                        expert_chunk(n + 4, "d", 2 * i + 2)
                        dst = write_y(2 * i)
                        sp.wait_ge(s["y_ready"], 2 * i + 2)
                        sp.dma_start(dst, ybuf[0]).then_inc(s["y_written"], 16)
                        sp.wait_ge(s["gate_mm"], 2 * i + 3)
                        if last:
                            expert_chunk(n + 5, "d", E - 1)
                        else:
                            expert_chunk(n + 5, "g", 2 * i + 4)

                    step_pair(0, first=True)
                    with sp.Fori(1, E // 2 - 2) as i:
                        step_pair(i)
                    step_pair(E // 2 - 2, last=True)
                    for e in range(E - 3, E):
                        dst = write_y(e)
                        sp.wait_ge(s["y_ready"], e + 2)
                        sp.dma_start(dst, ybuf[e % 2]).then_inc(s["y_written"], 16)
                    sp.wait_ge(s["y_written"], 16 * (E + 1))

                @block.scalar
                def _(act):
                    step = stepper(act, act_step)
                    def root_mean_square(t, count):
                        step(act.activation(sq_flat, x[:, t, :], ACT.Square, accum_out=ss[:, t:t + 1]))
                        act.activation(rs[:, t:t + 1], ss[:, t:t + 1], ACT.Sqrt, bias=c("eps"), scale=1.0 / D)\
                           .then_inc(s["rstd_done"], 1)

                    for t in range(T):
                        root_mean_square(t, t)
                    act.dma_start(g1b, mod_dram.rearrange("(m r) p -> m (r p)", r=K)
                                  [bass.ds(l * 6 + GATE1, 1), :].partition_broadcast(P)).then_inc(s["gate1_in"], 16)
                    for j, name in enumerate(("q_norm", "k_norm")):
                        act.dma_start(qkn[:, j, :], A[name][l].partition_broadcast(P)).then_inc(s["norms_in"], 16)
                    for j, name in enumerate(("sgu_ln_g", "sgu_ln_b")):
                        act.dma_start(sgn[:, j, :], A[name][l].partition_broadcast(P)).then_inc(s["sgu_in"], 16)
                    for h in range(SGU_H):
                        act.dma_start(sgb[64 * (h % 2):64 * (h % 2) + 64, h // 2, :],
                                      A["sgu_b"][l, h].partition_broadcast(64)).then_inc(s["sgu_in"], 16)
                    act.dma_start(sgw[:, :, :], A["sgu_w"][l].rearrange("h t s -> t h s")).then_inc(s["sgu_in"], 16)
                    act.dma_start(pww[:, :, :], A["conv_pw_w"][l].rearrange("(i p) n -> p i n", p=P))\
                       .then_inc(s["pw_in"], 16)
                    for g in range(4):
                        o = 64 * (g % 2)
                        act.dma_start(plw[o:o + 64, g // 2, o:o + 64], A["pool_w"][l, g]).then_inc(s["pw_in"], 16)
                    act.dma_start(wr[:, :, 0:NG], A["w_rg"][l].rearrange("(k p) g -> p k g", p=P))\
                       .then_inc(s["router_in"], 16)
                    act.dma_start(wr[:, :, NG:], A["w_re"][l].rearrange("(k p) g e -> p k (g e)", p=P))\
                       .then_inc(s["router_in"], 16)
                    act.dma_start(rb[:, 0:NG], A["b_rg"][l].partition_broadcast(P)).then_inc(s["router_in"], 16)
                    act.dma_start(rb[:, NG:], A["b_re"][l].rearrange("g e -> (g e)").partition_broadcast(P))\
                       .then_inc(s["router_in"], 16)

                    act.wait_ge(s["scl_ready"], 1)
                    for k in range(K):
                        act.wait_ge(pe_done, done(f"h{k}"))
                        act.activation(hT[:, k, :], bank_of(f"h{k}")[:, :], ACT.Identity,
                                       bias=pcol[:, SHIFT1 * K + k:SHIFT1 * K + k + 1], scale=scl[:, 0, k:k + 1])\
                           .then_inc(act_evac, 1)
                    for t in range(T):
                        act.wait_ge(pe_done, done(f"A{t}"))
                        act.activation(tokA[:, t, :], bank_of(f"A{t}")[:, 0:NA], ACT.Copy).then_inc(act_evac, 1)
                    for h in range(2):
                        act.wait_ge(pe_done, done(f"cg{h}"))
                        act.activation(sig[:, h, :], bank_of(f"cg{h}")[:, :], ACT.Sigmoid).then_inc(act_evac, 1)
                    for name, dst in (("iqT", iqT), ("ikT", ikT)):
                        act.wait_ge(pe_done, done(name))
                        act.activation(dst[:, :], bank_of(name)[:, :], ACT.Copy).then_inc(act_evac, 1)
                    n_relu = 0
                    for b in range(1, T):
                        for h in range(IH):
                            act.wait_ge(pe_done, done(f"idx{b}{h}"))
                            if n_relu >= 2:
                                act.wait_ge(s["relu_free"], n_relu - 1)
                            w = (b + 1) * P
                            act.activation(relu[n_relu % 2][:, 0:w], bank_of(f"idx{b}{h}")[:, 0:w], ACT.Relu,
                                           scale=float(ID ** -0.5 * IH ** -0.5)).then_inc(act_evac, 1)
                            n_relu += 1
                    act.wait_ge(s["relu_free"], n_relu)
                    for t in range(T):
                        act.wait_ge(pe_done, done(f"B{t}"))
                        act.activation(tokB[:, t, :], bank_of(f"B{t}")[:, :], ACT.Copy).then_inc(act_evac, 1)
                    for h in range(2):
                        act.wait_ge(pe_done, done(f"pool{h}"))
                        act.activation(poolin[:, h, 16:], bank_of(f"pool{h}")[:, :], ACT.Copy).then_inc(act_evac, 1)
                    act.wait_ge(s["qk_ss"], 1)
                    act.activation(rsq, ssq, ACT.Sqrt, bias=c("eps"), scale=1.0 / HD).then_inc(s["qk_rstd"], 1)
                    act.wait_ge(s["conv_in"], 2)
                    for h in range(2):
                        act.wait_ge(pe_done, done(f"u{h}"))
                        act.activation(uT[:, h, :], bank_of(f"u{h}")[:, :], ACT.Copy).then_inc(act_evac, 1)
                    for t in range(T):
                        act.wait_ge(pe_done, done(f"E{t}"))
                        act.activation(dv[:, t, :], bank_of(f"E{t}")[:, 0:G], ACT.Copy).then_inc(act_evac, 1)
                    for name, dst in (("qT0", qT[:, 0]), ("qT1", qT[:, 1]), ("kT0", kT[:, :, 0:P]), ("kT1", kT[:, :, P:2 * P])):
                        act.wait_ge(pe_done, done(name))
                        src = bank_of(name)[:, :]
                        if name[0] == "k":
                            src = src.rearrange("p (t n) -> p t n", t=T)
                        act.activation(dst, src, ACT.Copy).then_inc(act_evac, 1)

                    def exponentials(b):
                        w = (b + 1) * P
                        act.wait_ge(s["exp_in"], b + 1)
                        for h in range(HEADS):
                            ins = act.activation(prob[:, h, 0:w], prob[:, h, 0:w], ACT.Exp,
                                                 bias=nmx[:, h:h + 1], scale=float(HD ** -0.5),
                                                 accum_out=sums[:, h:h + 1])
                        ins.then_inc(s["exp_done"], 1)

                    def values(b):
                        w = (b + 1) * P
                        for pair in range(2):
                            before = f"pv{b}0" if pair else (f"pv{b - 1}1" if b else None)
                            if before:
                                act.wait_ge(pe_done, done(before))
                            for h in (2 * pair, 2 * pair + 1):
                                act.wait_ge(pe_done, done(f"probT{b}{h}"))
                                act.activation(probT[:, h % 2, 0:w], bank_of(f"probT{b}{h}")[:, 0:w], ACT.Copy)\
                                   .then_inc(act_evac, 1)
                            act.wait_ge(pe_done, done(f"pv{b}{pair}"))
                            act.activation(mixT[:, pair, b * P:(b + 1) * P], bank_of(f"pv{b}{pair}")[:, 0:P],
                                           ACT.Copy).then_inc(act_evac, 1)

                    def squares(g):
                        act.activation(mix_sq_buf[g], mixT[:, 2 * g:2 * g + 2, :], ACT.Square)\
                           .then_inc(s["mix_sq"], 1)

                    def mixer_root(g):
                        act.wait_ge(pe_done, done(f"ms{g}"))
                        act.activation(rmix[:, g, :], bank_of(f"ms{g}")[:, 0:T], ACT.Sqrt, bias=c("eps"))\
                           .then_inc(act_evac, 1)

                    act.wait_ge(s["sgu_var"], 1)
                    act.activation(rdv, bag[:, :, 1], ACT.Sqrt, bias=c("eps")).then_inc(s["sgu_rstd"], 1)
                    exponentials(0)
                    values(0)
                    exponentials(1)
                    act.wait_ge(s["mix_ready"], 1)
                    squares(3)
                    mixer_root(3)
                    values(1)
                    exponentials(2)
                    values(2)
                    act.wait_ge(s["mix_ready"], 2)
                    squares(2)
                    for h in range(2):
                        act.wait_ge(s["centered"], h + 1)
                        act.activation(sq[:, h, :], acc[:, h, :], ACT.Square).then_inc(s["centered_sq"], 1)
                    mixer_root(2)
                    for h in range(2):
                        act.wait_ge(pe_done, done(f"cvar{h}"))
                        act.activation(sq[:, h, :], bank_of(f"cvar{h}")[:, :], ACT.Sqrt, bias=c("eps"))\
                           .then_inc(act_evac, 1)
                    act.wait_ge(s["conv_normed"], 1)
                    for h in range(2):
                        act.activation(acc[:, h, :], acc[:, h, :], ACT.Silu,
                                       bias=pcol[:, R_LB + h:R_LB + h + 1], scale=pcol[:, R_LG + h:R_LG + h + 1])\
                           .then_inc(s["swished"], 1)
                    act.wait_ge(s["mix_ready"], 3)
                    squares(1)
                    mixer_root(1)
                    exponentials(3)
                    values(3)
                    act.wait_ge(act_evac, emptied("pv31"))
                    squares(0)
                    mixer_root(0)
                    for t in range(T):
                        act.wait_ge(s["x_added"], t + 1)
                        root_mean_square(t, T + t)
                    for k in range(K):
                        act.wait_ge(pe_done, done(f"m{k}"))
                        act.activation(h2T[:, k, :], bank_of(f"m{k}")[:, :], ACT.Identity,
                                       bias=pcol[:, SHIFT2 * K + k:SHIFT2 * K + k + 1], scale=scl[:, 1, k:k + 1])\
                           .then_inc(act_evac, 1)
                    act.wait_ge(s["gexp_in"], 1)
                    act.activation(r4[:, 0], r4[:, 0], ACT.Exp)
                    act.activation(ediff, ediff, ACT.Exp).then_inc(s["gexp_out"], 1)

                    act.wait_ge(s["routed"], 1)
                    act.wait_ge(scattered, (l + 1) * (16 * 2 * T))
                    act.sem_inc(act_step, 1)

                    def load_rows(e, b):
                        row = act.value_load(starti[0:1, bass.ds(e, 1)], min_val=0, max_val=2 * S)
                        act.dma_start(xs[b], xs_dram[bass.ds(row, P), :]).then_inc(xs_in[b], 16)

                    def evacuate_rows(count, b):
                        act.wait_ge(s["xs_tr"], count + 1)
                        for k in range(K):
                            ins = act.activation(xT[b][:, k, :], XP[k // 4][:, (k % 4) * P:(k % 4 + 1) * P],
                                                 ACT.Identity, scale=scl[:, 1, k:k + 1],
                                                 bias=pcol[:, SHIFT2 * K + k:SHIFT2 * K + k + 1])
                        ins.then_inc(s["xt_ready"], 1)

                    def silu(e):
                        act.wait_ge(s["gate_mm"], e + 1)
                        act.activation(sgate, GB[:, :], ACT.Silu).then_inc(s["silu_done"], 1)

                    def evacuate_hidden(e):
                        act.wait_ge(s["hid_tr"], e + 1)
                        act.activation(hidT, HB[:, :].rearrange("p (k s) -> p k s", k=4), ACT.Copy)\
                           .then_inc(s["hidt_ready"], 1)

                    load_rows(0, 0)
                    load_rows(1, 1)
                    evacuate_rows(0, 0)
                    load_rows(2, 0)
                    silu(0)
                    evacuate_rows(1, 1)
                    load_rows(3, 1)

                    def step_expert(e, b, more=True, rows=True):
                        act.wait_ge(s["hid_ready"], e)
                        silu(e)
                        evacuate_hidden(e - 1)
                        if rows:
                            evacuate_rows(e + 1, 1 - b)
                        if more:
                            load_rows(e + 3, 1 - b)

                    with act.Fori(0, E // 2 - 2) as i:
                        step_expert(2 * i + 1, 1)
                        step_expert(2 * i + 2, 0)
                    step_expert(E - 3, 1, more=False)
                    step_expert(E - 2, 0, more=False)
                    step_expert(E - 1, 1, more=False, rows=False)
                    evacuate_hidden(E - 1)

                @block.gpsimd
                def _(pool):
                    step = stepper(pool, pool_step)

                    pool.wait_ge(s["conv_in"], 2)
                    step(pool.tensor_scalar(acc[:, 1, :], convin[:, 1, 0:S], cwcol[:, 1:2],
                                            pcol[:, R_CB + 1:R_CB + 2], ALU.mult, ALU.add))
                    for w in range(1, TAPS):
                        product = wsum[1][:, w % 2, 0:S]
                        step(pool.tensor_scalar(product, convin[:, 1, w:w + S], cwcol[:, 2 * w + 1:2 * w + 2],
                                                None, ALU.mult))
                        step(pool.tensor_tensor(acc[:, 1, :], acc[:, 1, :], product, ALU.add))
                    pool.sem_inc(s["conv_done"], 1)
                    pool.wait_ge(act_evac, emptied("pool1"))
                    a, b = wsum
                    step(pool.tensor_tensor(a[:, :, 1:], poolin[:, :, 1:], poolin[:, :, 0:15 + S], ALU.add))
                    step(pool.tensor_tensor(b[:, :, 3:], a[:, :, 3:], a[:, :, 1:14 + S], ALU.add))
                    step(pool.tensor_tensor(a[:, 1, 7:], b[:, 1, 7:], b[:, 1, 3:12 + S], ALU.add))
                    step(pool.tensor_tensor(b[64:, 1, 15:], a[64:, 1, 15:], a[64:, 1, 7:8 + S], ALU.add))
                    invw, invc = c("invw"), c("invc").rearrange("p (h n) -> p h n", h=2)
                    for lo, src in ((0, a), (64, b)):
                        r = slice(lo, lo + 64)
                        step(pool.tensor_tensor(a[r, :, 16:32], src[r, :, 16:32], invc[r, :, :], ALU.mult))
                        step(pool.tensor_tensor(a[r, :, 16:32], a[r, :, 16:32], poolin[r, :, 16:32], ALU.subtract))
                        for h in range(2):
                            step(pool.tensor_scalar(a[r, h, 32:], src[r, h, 32:], invw[r, h:h + 1], None, ALU.mult))
                            step(pool.tensor_tensor(a[r, h, 32:], a[r, h, 32:], poolin[r, h, 32:], ALU.subtract))
                    pool.sem_inc(s["pooled"], 1)
                    pool.wait_ge(s["rows_known"], 1)
                    for t in range(T):
                        for j in range(2):
                            pool.indirect_dma_start(
                                xs_dram, bass.IndirectOffsetOnAxis(ap=posu[:, j, t:t + 1], axis=0),
                                xn2[:, t, :], None, bounds_check=ROWS - 1, oob_is_err=True)\
                                .then_inc(scattered, 16)

                @block.vector
                def _(v):
                    step = stepper(v, dve_step)
                    v.wait_ge(pe_done, done("params"))
                    step(v.tensor_copy(pcol[:, :], bank_of("params")[:, 0:NROW]))
                    v.sem_inc(dve_evac, 1)
                    v.wait_ge(pe_done, done("taps"))
                    v.tensor_copy(cwcol[:, :], bank_of("taps")[:, 0:2 * TAPS]).then_inc(dve_evac, 1)
                    for j, (m, r) in enumerate(((SCALE1, R_N1), (SCALE2, R_N2))):
                        ins = v.scalar_tensor_tensor(scl[:, j, :], pcol[:, m * K:(m + 1) * K], 1.0,
                                                     pcol[:, r:r + K], ALU.add, ALU.mult)
                    ins.then_inc(s["scl_ready"], 1)

                    def normalise_tile(dst, t, count):
                        v.wait_ge(s["rstd_done"], count)
                        step(v.reciprocal(rs[:, t:t + 1], rs[:, t:t + 1]))
                        v.tensor_scalar(dst[:, t, :], x[:, t, :], rs[:, t:t + 1], None, ALU.mult)\
                         .then_inc(s["xn_done"], 1)

                    for t in range(T):
                        normalise_tile(xn, t, t + 1)

                    def scale_w_out(n):
                        w = chunk_view(N_IN + n, 512)
                        v.wait_ge(*loaded(N_IN + n))
                        for k in range(K):
                            ins = v.scalar_tensor_tensor(w[:, k, :], w[:, k, :], pcol[:, R_ON + k:R_ON + k + 1],
                                                         g1b[:, n * 512:(n + 1) * 512], ALU.mult, ALU.mult)
                        step(ins)
                        v.sem_inc(s["wout_scaled"], 1)

                    v.wait_ge(s["gate1_in"], 16)
                    scale_w_out(0)

                    def rope(tiles, heads, half, table):
                        cos = cs[:, :, table:table + half].unsqueeze(2).to_broadcast([P, T, heads, half])
                        sin = sn[:, :, table:table + half].unsqueeze(2).to_broadcast([P, T, heads, half])
                        a, b = tiles[:, :, :, 0:half], tiles[:, :, :, half:2 * half]
                        tmp = [ropet[:, i, :, 0:heads, 0:half] for i in range(4)]
                        v.tensor_tensor(tmp[0], a, cos, ALU.mult)
                        v.tensor_tensor(tmp[1], b, sin, ALU.mult)
                        v.tensor_tensor(tmp[2], b, cos, ALU.mult)
                        step(v.tensor_tensor(tmp[3], a, sin, ALU.mult))
                        v.tensor_tensor(a, tmp[0], tmp[1], ALU.subtract)
                        return v.tensor_tensor(b, tmp[2], tmp[3], ALU.add)

                    v.wait_ge(act_evac, emptied("A3"))
                    step(rope(tokA[:, :, G:G + (IH + 1) * ID].rearrange("p t (h d) -> p t h d", d=ID),
                              IH + 1, IROT, ROT))
                    v.tensor_copy(ik4[:, :, :].rearrange("p t (r d) -> p t r d", r=4),
                                  tokA[:, :, G + IH * ID:G + (IH + 1) * ID].unsqueeze(2)
                                  .to_broadcast([P, T, 4, ID])).then_inc(s["idx_roped"], 1)
                    scale_w_out(1)
                    v.memset(convin[:, :, 0:TAPS - 1], 0.0)
                    for h in range(2):
                        v.wait_ge(act_evac, emptied(f"cg{h}"))
                        v.wait_ge(pe_done, done(f"ca{h}"))
                        step(v.tensor_tensor(convin[:, h, TAPS - 1:], bank_of(f"ca{h}")[:, :], sig[:, h, :],
                                             ALU.mult))
                        v.sem_inc(dve_evac, 1)
                        v.sem_inc(s["conv_in"], 1)
                    n = 0
                    for b in range(1, T):
                        w = (b + 1) * P
                        dst = score[:, SC[b]:SC[b] + w]
                        for h in range(IH):
                            iw = tokA[:, b, NA - IH + h:NA - IH + h + 1]
                            v.wait_ge(act_evac, emptied(f"idx{b}{h}"))
                            if h == 0:
                                ins = v.tensor_scalar(dst, relu[n % 2][:, 0:w], iw, None, ALU.mult)
                            else:
                                ins = v.scalar_tensor_tensor(dst, relu[n % 2][:, 0:w], iw, dst, ALU.mult, ALU.add)
                            n += 1
                            step(ins)
                            v.sem_inc(s["relu_free"], 1)
                        step(v.memset(score[0:CHUNK, SC[b] + w - CHUNK:SC[b] + w], NEG))

                    def select(b, rounds=range(TOPK // 8)):
                        w = (b + 1) * P
                        sc = score[:, SC[b]:SC[b] + w]
                        for n in rounds:
                            step(v.max(m8, sc))
                            step(v.match_replace(sc, m8, sc, GONE))
                        if n == TOPK // 8 - 1:
                            step(v.tensor_scalar(sc, sc, float(0.5 * (NEG + GONE)), MASK, ALU.is_gt, ALU.mult))

                    step(v.tensor_scalar(acc[:, 0, :], convin[:, 0, 0:S], cwcol[:, 0:1], pcol[:, R_CB:R_CB + 1],
                                         ALU.mult, ALU.add))
                    for w in range(1, TAPS):
                        step(v.scalar_tensor_tensor(acc[:, 0, :], convin[:, 0, w:w + S],
                                                    cwcol[:, 2 * w:2 * w + 1], acc[:, 0, :], ALU.mult, ALU.add))
                    v.sem_inc(s["conv_done"], 1)
                    select(1)
                    v.wait_ge(act_evac, emptied("B3"))
                    for t in range(T):
                        for h in range(2 * HEADS):
                            src = tokB[:, t, h * HD:(h + 1) * HD]
                            n = (t * 8 + h) % 16
                            ins = v.tensor_tensor_reduce(sq_flat[:, n * HD:(n + 1) * HD], src, src, 1.0, 0.0,
                                                         ALU.mult, ALU.add, ssq[:, t * 8 + h:t * 8 + h + 1])
                        if t == 1:
                            step(ins)
                    ins.then_inc(s["qk_ss"], 1)
                    select(2)
                    v.wait_ge(s["qk_rstd"], 1)
                    step(v.reciprocal(rsq, rsq))
                    v.wait_ge(s["norms_in"], 32)
                    qk = tokB[:, :, :].rearrange("p t (h d) -> p t h d", d=HD)
                    step(v.tensor_tensor(qk, qk, rsq.rearrange("p (t h) -> p t h", t=T).unsqueeze(3)
                                         .to_broadcast([P, T, 2 * HEADS, HD]), ALU.mult))
                    for j in range(2):
                        for t in range(T):
                            part = qk[:, t, j * HEADS:(j + 1) * HEADS, :]
                            ins = v.tensor_tensor(part, part, qkn[:, j, :].unsqueeze(1)
                                                  .to_broadcast([P, HEADS, HD]), ALU.mult)
                    step(ins)
                    rope(qk, 2 * HEADS, ROT, 0).then_inc(s["qk_roped"], 1)
                    v.wait_ge(act_evac, emptied("E3"))
                    for t in range(T):
                        step(v.bn_stats(bst[:, t, :], dv[:, t, :]))
                    for t in range(T):
                        ins = v.bn_aggr(bag[:, t, :], bst[:, t, :])
                    ins.then_inc(s["sgu_var"], 1)

                    def logits(b):
                        w = (b + 1) * P
                        bias = score[:, SC[b]:SC[b] + w] if b else c("mask0")
                        v.wait_ge(pe_done, done(f"probT{b - 1}3" if b else "E3"))
                        for h in range(HEADS):
                            v.wait_ge(pe_done, done(f"logit{b}{h}"))
                            ins = v.tensor_tensor_reduce(prob[:, h, 0:w], bank_of(f"logit{b}{h}")[:, 0:w], bias,
                                                         1.0, NEG, ALU.add, ALU.max, mx[:, h:h + 1])
                            if h < HEADS - 1:
                                ins.then_inc(dve_evac, 1)
                        step(ins)
                        v.sem_inc(dve_evac, 1)
                        v.tensor_scalar(nmx, mx, -float(HD ** -0.5), None, ALU.mult).then_inc(s["exp_in"], 1)

                    def probabilities(b):
                        w = (b + 1) * P
                        v.wait_ge(s["exp_done"], b + 1)
                        step(v.reciprocal(rsum, sums))
                        for h in range(HEADS):
                            ins = v.tensor_scalar(prob[:, h, 0:w], prob[:, h, 0:w], rsum[:, h:h + 1], None, ALU.mult)
                        ins.then_inc(s["prob_ready"], 1)

                    def mixer_reciprocal(g):
                        v.wait_ge(act_evac, emptied(f"ms{g}"))
                        step(v.reciprocal(rmix[:, g, :], rmix[:, g, :]))

                    def add_out(g, t, n):
                        part = x[:, t, n * 512:(n + 1) * 512]
                        v.wait_ge(pe_done, done(f"out{g}{t}{n}"))
                        step(v.scalar_tensor_tensor(part, bank_of(f"out{g}{t}{n}")[:, :], rmix[:, g, t:t + 1], part,
                                                    ALU.mult, ALU.add))
                        v.sem_inc(dve_evac, 1)

                    def normalise_conv():
                        v.wait_ge(act_evac, emptied("cvar1"))
                        step(v.reciprocal(sq[:, :, :], sq[:, :, :]))
                        step(v.tensor_tensor(acc[:, :, :], acc[:, :, :], sq[:, :, :], ALU.mult))
                        v.sem_inc(s["conv_normed"], 1)

                    def conv_outputs():
                        v.wait_ge(pe_done, done("pw1"))
                        for co in range(2):
                            ins = v.tensor_scalar(mixT[:, 2 + co, :], bank_of(f"pw{co}")[:, :],
                                                  pcol[:, R_PB + co:R_PB + co + 1], None, ALU.add)
                            if co == 0:
                                ins.then_inc(dve_evac, 1)
                        step(ins)
                        v.sem_inc(dve_evac, 1)
                        v.sem_inc(s["mix_ready"], 1)

                    logits(0)
                    v.wait_ge(s["sgu_rstd"], 1)
                    step(v.reciprocal(rdv, rdv))
                    v.wait_ge(s["sgu_in"], 16 * 7)
                    for t in range(T):
                        ins = v.tensor_scalar(dv[:, t, :], dv[:, t, :], bag[:, t, 0:1], rdv[:, t:t + 1],
                                              ALU.subtract, ALU.mult)
                    step(ins)
                    probabilities(0)
                    step(v.tensor_tensor(dv, dv, sgn[:, 0, :].unsqueeze(1).to_broadcast([P, T, G]), ALU.mult))
                    v.tensor_tensor(dv, dv, sgn[:, 1, :].unsqueeze(1).to_broadcast([P, T, G]), ALU.add)\
                        .then_inc(s["sgu_normed"], 1)
                    v.wait_ge(pe_done, done("sgw"))
                    v.tensor_tensor(sgwT[:, :, :], bank_of("sgw")[:, :].rearrange("p (h t) -> p h t", h=SGU_H),
                                    c("upto").unsqueeze(1).to_broadcast([P, SGU_H, P]), ALU.mult)\
                        .then_inc(dve_evac, 1)
                    v.wait_ge(act_evac, emptied("u1"))
                    for p in range(2):
                        v.wait_ge(pe_done, done(f"sgu{p}"))
                        mixed = sq[:, p, :]
                        step(v.tensor_tensor(mixed.rearrange("p (n t) -> p n t", n=T),
                                             bank_of(f"sgu{p}")[:, :].rearrange("p (n t) -> p n t", n=T),
                                             sgb[:, p, :].unsqueeze(1).to_broadcast([P, T, P]), ALU.add))
                        v.sem_inc(dve_evac, 1)
                        ins = v.tensor_tensor(uT[:, p, :], mixed, uT[:, p, :], ALU.mult)
                    step(ins)
                    v.sem_inc(s["mix_ready"], 1)
                    logits(1)
                    probabilities(1)
                    select(3, range(0, 5))
                    logits(2)
                    mixer_reciprocal(3)
                    for t, n in TN[:4]:
                        add_out(3, t, n)
                    probabilities(2)
                    select(3, range(5, 9))
                    for h in range(2):
                        v.wait_ge(pe_done, done(f"pl{h}"))
                        ins = v.tensor_scalar(mixT[:, 4 + h, :], bank_of(f"pl{h}")[:, :],
                                              pcol[:, R_QB + h:R_QB + h + 1], pcol[:, R_QS + h:R_QS + h + 1],
                                              ALU.add, ALU.mult)
                        if h == 0:
                            ins.then_inc(dve_evac, 1)
                    step(ins)
                    v.sem_inc(dve_evac, 1)
                    v.sem_inc(s["mix_ready"], 1)
                    for h in range(2):
                        v.wait_ge(pe_done, done(f"cmean{h}"))
                        step(v.tensor_tensor(acc[:, h, :], acc[:, h, :], bank_of(f"cmean{h}")[:, :], ALU.subtract))
                        v.sem_inc(dve_evac, 1)
                        v.sem_inc(s["centered"], 1)
                    for t, n in TN[4:]:
                        add_out(3, t, n)
                    mixer_reciprocal(2)
                    normalise_conv()
                    for t, n in TN[:4]:
                        add_out(2, t, n)
                    select(3, range(9, 12))
                    conv_outputs()
                    for t, n in TN[4:]:
                        add_out(2, t, n)
                    select(3, range(12, TOPK // 8))
                    mixer_reciprocal(1)
                    for t, n in TN[:2]:
                        add_out(1, t, n)
                    logits(3)
                    for t, n in TN[2:5]:
                        add_out(1, t, n)
                    probabilities(3)
                    for t, n in TN[5:]:
                        add_out(1, t, n)
                    mixer_reciprocal(0)
                    for t in range(T):
                        add_out(0, t, 0)
                        add_out(0, t, 1)
                        v.sem_inc(s["x_added"], 1)
                        if t:
                            normalise_tile(xn2, t - 1, T + t)
                    normalise_tile(xn2, T - 1, 2 * T)

                    v.wait_ge(s["router_in"], 64)
                    v.wait_ge(pe_done, done("route"))
                    step(v.tensor_tensor(lg[:, :, :], bank_of("route")[:, 0:T * (NG + E)]
                                         .rearrange("p (t n) -> p t n", t=T),
                                         rb[:, :].unsqueeze(1).to_broadcast([P, T, NG + E]), ALU.add))
                    v.sem_inc(dve_evac, 1)
                    grp = lg[:, :, 0:NG]
                    io4 = c("iota")[:, 0:NG].unsqueeze(1).to_broadcast([P, T, NG])
                    step(v.tensor_reduce(gmax, grp, AX.X, ALU.max))
                    gm = gmax.unsqueeze(2).to_broadcast([P, T, NG])
                    v.tensor_tensor(r4[:, 0], grp, gm, ALU.subtract)
                    step(v.tensor_tensor(r4[:, 1], grp, gm, ALU.is_lt))
                    step(v.scalar_tensor_tensor(r4[:, 1], r4[:, 1], float(NG), io4, ALU.mult, ALU.add))
                    step(v.tensor_reduce(gidx, r4[:, 1], AX.X, ALU.min))
                    step(v.tensor_tensor(r4[:, 2], io4, gidx.unsqueeze(2).to_broadcast([P, T, NG]), ALU.is_equal))
                    step(v.tensor_scalar(r4[:, 2], r4[:, 2], 1.0, -MASK, ALU.subtract, ALU.mult))
                    for t in range(T):
                        ins = v.tensor_tensor(el[:, t, :].rearrange("p (g e) -> p g e", g=NG),
                                              lg[:, t, NG:].rearrange("p (g e) -> p g e", g=NG),
                                              r4[:, 2, t, :].unsqueeze(2).to_broadcast([P, NG, EPG]), ALU.add)
                    step(ins)
                    for t in range(T):
                        ins = v.max(top8[:, t, :], el[:, t, :])
                    step(ins)
                    for t in range(T):
                        v.max_index(topi[:, t, :], top8[:, t, :], el[:, t, :])
                    step(v.tensor_tensor(ediff, top8[:, :, 1], top8[:, :, 0], ALU.subtract))
                    v.sem_inc(s["gexp_in"], 1)
                    step(v.tensor_copy(topf, topi[:, :, :]))
                    io = c("iota").unsqueeze(1).to_broadcast([P, T, E])
                    for j in range(2):
                        ins = v.tensor_tensor(oh[:, j], topf[:, :, j:j + 1].to_broadcast([P, T, E]), io, ALU.is_equal)
                    step(ins)
                    v.tensor_tensor(oh[:, 2], oh[:, 0], oh[:, 1], ALU.add).then_inc(s["oh_ready"], 1)
                    v.wait_ge(s["gexp_out"], 1)
                    step(v.reduce_sum(psel, r4[:, 0], AX.X))
                    step(v.tensor_scalar(rsum, ediff, 1.0, None, ALU.add))
                    step(v.tensor_tensor(psel, psel, rsum, ALU.mult))
                    step(v.reciprocal(gates[:, 0, :], psel))
                    v.tensor_tensor(gates[:, 1, :], gates[:, 0, :], ediff, ALU.mult)
                    v.wait_ge(pe_done, done("rank"))
                    own, inc = cnt[:, 0:3, :], [cnt[:, 3:6, :], cnt[:, 6:9, :]]
                    v.tensor_copy(rank[:, :, :], bank_of("rank")[:, 0:T * E].rearrange("p (t e) -> p t e", t=T))
                    total = bank_of("rank")[:, T * E:(T + 1) * E]
                    step(v.tensor_scalar(own[:, 0, :], total, float(P), None, ALU.min))
                    step(v.tensor_tensor(own[:, 1, :], total, own[:, 0, :], ALU.subtract))
                    v.sem_inc(dve_evac, 1)
                    step(v.tensor_scalar(own[:, 2, :], own[:, 1, :], 0.0, None, ALU.is_gt))
                    for n in range(1, S // P - 1):
                        step(v.scalar_tensor_tensor(own[:, 2, :], own[:, 1, :], float(n * P), own[:, 2, :],
                                                    ALU.is_gt, ALU.add))
                    src, m = own, 0
                    for d in (1, 2, 4, 8, 16):
                        dst = inc[m % 2]
                        v.tensor_copy(dst[:, :, 0:d], src[:, :, 0:d])
                        step(v.tensor_tensor(dst[:, :, d:], src[:, :, d:], src[:, :, 0:E - d], ALU.add))
                        src, m = dst, m + 1
                    step(v.tensor_tensor(exc[:, 0:3, :], src, own, ALU.subtract))
                    start0, start1, nbx, far = (exc[:, i, :] for i in range(4))
                    step(v.tensor_scalar(start1, start1, src[:, 0, E - 1:E], None, ALU.add))
                    step(v.scalar_tensor_tensor(far, start1, -float(P), start0, ALU.add, ALU.subtract))
                    every = [P, T, E]
                    v.scalar_tensor_tensor(rtmp[:, :, :], rank[:, :, :], float(P),
                                           far.unsqueeze(1).to_broadcast(every), ALU.is_ge, ALU.mult)
                    step(v.tensor_tensor(rank[:, :, :], rank[:, :, :], start0.unsqueeze(1).to_broadcast(every),
                                         ALU.add))
                    step(v.tensor_tensor(rank[:, :, :], rank[:, :, :], rtmp[:, :, :], ALU.add))
                    for j in range(2):
                        step(v.tensor_tensor(oh[:, j], oh[:, j], rank[:, :, :], ALU.mult))
                        step(v.tensor_reduce(posr[:, j, :], oh[:, j], AX.X, ALU.add))
                    v.tensor_copy(posu[:, :, :], posr).then_inc(s["rows_known"], 1)
                    one, many = slice(0, 1), [1, OVER_BLOCKS, E]
                    rel, inside, row = (ovm[one, i] for i in range(3))
                    step(v.tensor_tensor(rel, c("blk")[one].unsqueeze(2).to_broadcast(many),
                                         nbx[one].unsqueeze(1).to_broadcast(many), ALU.subtract))
                    v.tensor_tensor(inside, rel, own[one, 2].unsqueeze(1).to_broadcast(many), ALU.is_lt)
                    step(v.scalar_tensor_tensor(row, rel, float(P), start1[one].unsqueeze(1).to_broadcast(many),
                                                ALU.mult, ALU.add))
                    step(v.scalar_tensor_tensor(inside, rel, 0.0, inside, ALU.is_ge, ALU.mult))
                    v.tensor_tensor(row, row, inside, ALU.mult)
                    step(v.tensor_tensor(inside, inside, c("iota")[one].unsqueeze(1).to_broadcast(many), ALU.mult))
                    v.tensor_reduce(ovf[one, 0], inside, AX.X, ALU.add)
                    step(v.tensor_reduce(ovf[one, 1], row, AX.X, ALU.add))
                    v.tensor_copy(ovi[one, 0:2 * OVER_BLOCKS], ovf[one].rearrange("p a b -> p (a b)"))
                    v.tensor_copy(ovi[one, 2 * OVER_BLOCKS:2 * OVER_BLOCKS + 1], src[one, 2, E - 1:E])
                    v.tensor_copy(starti[:, :], start0[one]).then_inc(s["routed"], 1)

                    v.sem_inc(s["y_ready"], 1)

                    def multiply(e):
                        v.wait_ge(s["silu_done"], e + 1)
                        v.wait_ge(s["up_mm"], e + 1)
                        v.tensor_tensor(hid, UB[:, :], sgate, ALU.mult).then_inc(s["hid_ready"], 1)

                    def evacuate_y(e, b):
                        v.wait_ge(s["y_written"], (e + 1) * 16)
                        v.wait_ge(s["down_mm"], e + 1)
                        v.tensor_copy(ybuf[b][:, 0:512], YB[0][:, :])
                        v.tensor_copy(ybuf[b][:, 512:D], YB[1][:, :]).then_inc(s["y_ready"], 1)

                    multiply(0)
                    with v.Fori(0, E // 2 - 1) as i:
                        for b, e in ((1, 2 * i + 1), (0, 2 * i + 2)):
                            multiply(e)
                            evacuate_y(e - 1, 1 - b)
                    multiply(E - 1)
                    evacuate_y(E - 2, 0)
                    evacuate_y(E - 1, 1)

                @block.tensor
                def _(pe):
                    def finish(mm):
                        mm.then_inc(pe_done, 1)

                    pe.wait_ge(s["rows_in"], 16 * 10)
                    pe.transpose(bank_of("params")[:, 0:NROW], prow[:, :], ident[0:NROW, 0:NROW]).then_inc(pe_done, 1)
                    pe.wait_ge(s["taps_in"], 16)
                    pe.transpose(bank_of("taps")[:, 0:2 * TAPS], cwrow[:, :], ident[0:2 * TAPS, 0:2 * TAPS])\
                        .then_inc(pe_done, 1)

                    def turn_tokens(prefix, tokens):
                        for k in range(K):
                            await_bank(pe, f"{prefix}{k}")
                            for t in range(T):
                                mm = pe.transpose(bank_of(f"{prefix}{k}")[:, t * P:(t + 1) * P],
                                                  tokens[:, t, k * P:(k + 1) * P], ident)
                            mm.then_inc(pe_done, 1)

                    def by_token(names, n, width):
                        w = chunk_view(n, width)
                        pe.wait_ge(*loaded(n))
                        for t in range(T):
                            await_bank(pe, f"{names}{t}")
                            for k in range(K):
                                mm = pe.matmul(bank_of(f"{names}{t}")[:, 0:width], hT[:, k, t * P:(t + 1) * P],
                                               w[:, k, :], start=(k == 0), stop=(k == K - 1))
                            mm.then_inc(pe_done, 1)

                    def by_channel(name, n, at):
                        w = chunk_view(n, 512)
                        await_bank(pe, name)
                        for k in range(K):
                            mm = pe.matmul(bank_of(name)[:, :], w[:, k, at:at + P], hT[:, k, :],
                                           start=(k == 0), stop=(k == K - 1))
                        mm.then_inc(pe_done, 1)

                    pe.wait_ge(s["xn_done"], T)
                    turn_tokens("h", xn)
                    pe.wait_ge(act_evac, emptied(f"h{K - 1}"))
                    by_token("A", 0, NA)
                    pe.wait_ge(*loaded(1))
                    for h in range(2):
                        by_channel(f"cg{h}", 1, G + h * P)
                        by_channel(f"ca{h}", 1, h * P)
                    pe.wait_ge(s["idx_roped"], 1)
                    for name, src in (("iqT", tokA[:, :, G:G + P]), ("ikT", ik4[:, :, :])):
                        await_bank(pe, name)
                        for t in range(T):
                            mm = pe.transpose(bank_of(name)[:, t * P:(t + 1) * P], src[:, t, :], ident)
                        mm.then_inc(pe_done, 1)
                    pe.wait_ge(act_evac, emptied("ikT"))
                    for b in range(1, T):
                        for h in range(IH):
                            name, r, w = f"idx{b}{h}", slice(h * ID, (h + 1) * ID), (b + 1) * P
                            await_bank(pe, name)
                            pe.matmul(bank_of(name)[:, 0:w], iqT[r, b * P:(b + 1) * P], ikT[r, 0:w],
                                      start=True, stop=True).then_inc(pe_done, 1)
                    by_token("B", 2, 512)
                    pe.wait_ge(*loaded(3))
                    for h in range(2):
                        by_channel(f"pool{h}", 3, h * P)
                    for h in range(2):
                        by_channel(f"u{h}", 3, G + h * P)
                    by_token("E", 4, G)
                    pe.wait_ge(s["qk_roped"], 1)
                    for j, head in ((0, "qT"), (1, "kT")):
                        for pair in range(2):
                            name, a = f"{head}{pair}", (2 * j + pair) * P
                            await_bank(pe, name)
                            for t in range(T):
                                mm = pe.transpose(bank_of(name)[:, t * P:(t + 1) * P], tokB[:, t, a:a + P], ident)
                            mm.then_inc(pe_done, 1)

                    def logits(b):
                        w = (b + 1) * P
                        if b == 0:
                            pe.wait_ge(act_evac, emptied("kT1"))
                        for h in range(HEADS):
                            name, r = f"logit{b}{h}", slice(64 * (h % 2), 64 * (h % 2) + 64)
                            await_bank(pe, name)
                            pe.matmul(bank_of(name)[:, 0:w].rearrange("p (t n) -> p t n", n=P),
                                      qT[r, h // 2, b * P:(b + 1) * P],
                                      kT[r, 0:b + 1, (h // 2) * P:(h // 2 + 1) * P],
                                      start=True, stop=True).then_inc(pe_done, 1)

                    def values(b):
                        pe.wait_ge(s["prob_ready"], b + 1)
                        for pair in range(2):
                            for h in (2 * pair, 2 * pair + 1):
                                name = f"probT{b}{h}"
                                await_bank(pe, name)
                                for kt in range(b + 1):
                                    mm = pe.transpose(bank_of(name)[:, kt * P:(kt + 1) * P],
                                                      prob[:, h, kt * P:(kt + 1) * P], ident)
                                mm.then_inc(pe_done, 1)
                            name = f"pv{b}{pair}"
                            await_bank(pe, name)
                            pe.wait_ge(act_evac, emptied(f"probT{b}{2 * pair + 1}"))
                            for h in (2 * pair, 2 * pair + 1):
                                o = 64 * (h % 2)
                                for kt in range(b + 1):
                                    mm = pe.matmul(bank_of(name)[o:o + 64, 0:P], tokA[:, kt, h * HD:(h + 1) * HD],
                                                   probT[:, h % 2, kt * P:(kt + 1) * P],
                                                   start=(kt == 0), stop=(kt == b))
                            mm.then_inc(pe_done, 1)

                    def mean_square(g, count):
                        pe.wait_ge(s["mix_sq"], count)
                        await_bank(pe, f"ms{g}")
                        for t in range(T):
                            for i in range(2):
                                mm = pe.matmul(bank_of(f"ms{g}")[:, t:t + 1], mix_sq_buf[g][:, i, t * P:(t + 1) * P],
                                               c("mean256")[:, 0:1], start=(i == 0), stop=(i == 1))
                        mm.then_inc(pe_done, 1)

                    def project_out(g, tn):
                        for t, n in tn:
                            name = f"out{g}{t}{n}"
                            w = chunk_view(N_IN + n, 512)
                            await_bank(pe, name)
                            for i in range(2):
                                mm = pe.matmul(bank_of(name)[:, :], mixT[:, 2 * g + i, t * P:(t + 1) * P],
                                               w[:, 2 * g + i, :], start=(i == 0), stop=(i == 1))
                            mm.then_inc(pe_done, 1)

                    logits(0)
                    pe.wait_ge(s["sgu_in"], 16 * 7)
                    await_bank(pe, "sgw")
                    for h in range(SGU_H):
                        mm = pe.transpose(bank_of("sgw")[:, h * P:(h + 1) * P], sgw[:, h, :], ident)
                    mm.then_inc(pe_done, 1)
                    values(0)
                    pe.wait_ge(s["sgu_normed"], 1)
                    pe.wait_ge(dve_evac, emptied("sgw"))
                    for pair in range(2):
                        name = f"sgu{pair}"
                        await_bank(pe, name)
                        for n in range(T):
                            for h in (2 * pair, 2 * pair + 1):
                                o = 64 * (h % 2)
                                mm = pe.matmul(bank_of(name)[o:o + 64, n * P:(n + 1) * P],
                                               dv[:, n, h * 64:(h + 1) * 64], sgwT[:, h, :], start=True, stop=True)
                        mm.then_inc(pe_done, 1)
                    logits(1)
                    mean_square(3, 1)
                    values(1)
                    logits(2)
                    pe.wait_ge(s["wout_scaled"], N_OUT)
                    project_out(3, TN[:4])
                    values(2)
                    pe.wait_ge(s["pooled"], 1)
                    pe.wait_ge(s["pw_in"], 16 * 5)
                    for h in range(2):
                        await_bank(pe, f"pl{h}")
                        pe.matmul(bank_of(f"pl{h}")[:, :], plw[:, h, :], wsum[0][:, h, 16:], start=True, stop=True)\
                            .then_inc(pe_done, 1)
                    pe.wait_ge(s["conv_done"], 2)
                    for h in range(2):
                        await_bank(pe, f"cmean{h}")
                        pe.matmul(bank_of(f"cmean{h}")[:, :], c("mean64"), acc[:, h, :], start=True, stop=True)\
                            .then_inc(pe_done, 1)
                    project_out(3, TN[4:])
                    mean_square(2, 2)
                    for h in range(2):
                        pe.wait_ge(s["centered_sq"], h + 1)
                        await_bank(pe, f"cvar{h}")
                        pe.matmul(bank_of(f"cvar{h}")[:, :], c("mean64"), sq[:, h, :], start=True, stop=True)\
                            .then_inc(pe_done, 1)
                    project_out(2, TN[:4])
                    pe.wait_ge(s["swished"], 2)
                    for co in range(2):
                        await_bank(pe, f"pw{co}")
                        for ci in range(2):
                            mm = pe.matmul(bank_of(f"pw{co}")[:, :], pww[:, ci, co * P:(co + 1) * P], acc[:, ci, :],
                                           start=(ci == 0), stop=(ci == 1))
                        mm.then_inc(pe_done, 1)
                    project_out(2, TN[4:])
                    mean_square(1, 3)
                    project_out(1, TN[:2])
                    logits(3)
                    project_out(1, TN[2:])
                    values(3)
                    mean_square(0, 4)
                    project_out(0, TN)
                    pe.wait_ge(s["xn_done"], 2 * T)
                    turn_tokens("m", xn2)
                    pe.wait_ge(act_evac, emptied(f"m{K - 1}"))
                    pe.wait_ge(s["router_in"], 64)
                    await_bank(pe, "route")
                    for t in range(T):
                        for k in range(K):
                            mm = pe.matmul(bank_of("route")[:, t * (NG + E):(t + 1) * (NG + E)],
                                           h2T[:, k, t * P:(t + 1) * P], wr[:, k, :], start=(k == 0), stop=(k == K - 1))
                    mm.then_inc(pe_done, 1)
                    pe.wait_ge(s["oh_ready"], 1)
                    await_bank(pe, "rank")
                    for t in range(T + 1):
                        dst = bank_of("rank")[:, t * E:(t + 1) * E]
                        sides = [(c("ones"), u) for u in range(t)] + ([(c("before"), t)] if t < T else [])
                        for n, (m, u) in enumerate(sides):
                            mm = pe.matmul(dst, m, oh[:, 2, u, :], start=(n == 0), stop=(n == len(sides) - 1))
                    mm.then_inc(pe_done, 1)

                    def expert_matrix(j, k):
                        return ring[:, j % RING, :].rearrange("p (k n) -> p k n", k=k)

                    def turn_rows(count, b, times):
                        pe.wait_ge(xs_in[b], 16 * times)
                        for k in range(K):
                            mm = pe.transpose(XP[k // 4][:, (k % 4) * P:(k % 4 + 1) * P],
                                              xs[b][:, k * P:(k + 1) * P], ident)
                        mm.then_inc(s["xs_tr"], 1)

                    def first_product(n, fill, out_bank, b, signal):
                        w = expert_matrix(n, K)
                        pe.wait_ge(slot[n % RING], 16 * fill)
                        for k in range(K):
                            mm = pe.matmul(out_bank[:, :], xT[b][:, k, :], w[:, k, :],
                                           start=(k == 0), stop=(k == K - 1))
                        mm.then_inc(signal, 1)

                    def turn_hidden(e):
                        pe.wait_ge(s["hid_ready"], e + 1)
                        for k in range(4):
                            mm = pe.transpose(HB[:, k * P:(k + 1) * P], hid[:, k * P:(k + 1) * P], ident)
                        mm.then_inc(s["hid_tr"], 1)

                    def down(e, n, fill):
                        w = expert_matrix(n, 4)
                        pe.wait_ge(slot[n % RING], 16 * fill)
                        pe.wait_ge(s["hidt_ready"], e + 1)
                        pe.wait_ge(s["y_ready"], e + 1)
                        for half in range(2):
                            for k in range(4):
                                mm = pe.matmul(YB[half][:, :], hidT[:, k, :], w[:, k, half * 512:(half + 1) * 512],
                                               start=(k == 0), stop=(k == 3))
                        mm.then_inc(s["down_mm"], 1)

                    pe.wait_ge(s["routed"], 1)
                    turn_rows(0, 0, 1)
                    pe.wait_ge(s["xt_ready"], 1)
                    first_product(N_PRE, (N_PRE // RING) + 1, GB, 0, s["gate_mm"])
                    first_product(N_PRE + 1, (N_PRE + 1) // RING + 1, UB, 0, s["up_mm"])
                    turn_rows(1, 1, 1)

                    def step_expert(e, b, n, fill, times, rows=True):
                        pe.wait_ge(s["xt_ready"], e + 1)
                        pe.wait_ge(s["silu_done"], e)
                        first_product(n, fill, GB, b, s["gate_mm"])
                        turn_hidden(e - 1)
                        first_product(n + 1, fill, UB, b, s["up_mm"])
                        if rows:
                            turn_rows(e + 1, 1 - b, times)
                        down(e - 1, n + 2, fill)

                    with pe.Fori(0, E // 2 - 1) as i:
                        step_expert(2 * i + 1, 1, 9, i + 2, i + 2)
                        step_expert(2 * i + 2, 0, 12, i + 3, i + 2)
                    step_expert(E - 1, 1, 9, E // 2 + 1, 0, rows=False)
                    turn_hidden(E - 1)
                    n = N_CHUNKS - 1
                    down(E - 1, n, n // RING + 1)

            clear_semaphores()

            n_over = nc.values_load(ovi[0:1, 2 * OVER_BLOCKS:2 * OVER_BLOCKS + 1], min_val=0, max_val=OVER_BLOCKS)
            with nc.Fori(0, OVER_BLOCKS) as i:
                with nc.If(n_over > i):
                    with nc.Block() as block:
                        @block.sync
                        def _(sp):
                            e = sp.value_load(ovi[0:1, bass.ds(i, 1)], min_val=0, max_val=E - 1)
                            row = sp.value_load(ovi[0:1, bass.ds(i + OVER_BLOCKS, 1)], min_val=0, max_val=ROWS - P)
                            for j, (src, k) in enumerate(((wg_v, K), (wu_v, K), (wd_v, 4))):
                                sp.dma_start(ring[:, j, :].rearrange("p (k n) -> p k n", k=k),
                                             src[l, bass.ds(e, 1)].rearrange("e p k n -> (e p) k n"))\
                                    .then_inc(slot[j], 16)
                            sp.dma_start(xs[0], xs_dram[bass.ds(row, P), :]).then_inc(xs_in[0], 16)
                            sp.wait_ge(s["y_ready"], 1)
                            sp.dma_start(ys_dram[bass.ds(row, P), :], ybuf[0]).then_inc(s["y_written"], 16)
                            sp.wait_ge(s["y_written"], 16)

                        @block.gpsimd
                        def _(pool):
                            pool.memset(small[:, 228:229], 0.0)

                        @block.scalar
                        def _(act):
                            act.wait_ge(s["xs_tr"], 1)
                            for k in range(K):
                                ins = act.activation(xT[0][:, k, :], XP[k // 4][:, (k % 4) * P:(k % 4 + 1) * P],
                                                     ACT.Identity, scale=scl[:, 1, k:k + 1],
                                                     bias=pcol[:, SHIFT2 * K + k:SHIFT2 * K + k + 1])
                            ins.then_inc(s["xt_ready"], 1)
                            act.wait_ge(s["gate_mm"], 1)
                            act.activation(sgate, GB[:, :], ACT.Silu).then_inc(s["silu_done"], 1)
                            act.wait_ge(s["hid_tr"], 1)
                            act.activation(hidT, HB[:, :].rearrange("p (k s) -> p k s", k=4), ACT.Copy)\
                               .then_inc(s["hidt_ready"], 1)

                        @block.vector
                        def _(v):
                            v.wait_ge(s["silu_done"], 1)
                            v.wait_ge(s["up_mm"], 1)
                            v.tensor_tensor(hid, UB[:, :], sgate, ALU.mult).then_inc(s["hid_ready"], 1)
                            v.wait_ge(s["down_mm"], 1)
                            v.tensor_copy(ybuf[0][:, 0:512], YB[0][:, :])
                            v.tensor_copy(ybuf[0][:, 512:D], YB[1][:, :]).then_inc(s["y_ready"], 1)

                        @block.tensor
                        def _(pe):
                            pe.wait_ge(xs_in[0], 16)
                            for k in range(K):
                                mm = pe.transpose(XP[k // 4][:, (k % 4) * P:(k % 4 + 1) * P],
                                                  xs[0][:, k * P:(k + 1) * P], ident)
                            mm.then_inc(s["xs_tr"], 1)
                            pe.wait_ge(s["xt_ready"], 1)
                            for j, (dst, signal) in enumerate(((GB, s["gate_mm"]), (UB, s["up_mm"]))):
                                w = ring[:, j, :].rearrange("p (k n) -> p k n", k=K)
                                pe.wait_ge(slot[j], 16)
                                for k in range(K):
                                    mm = pe.matmul(dst[:, :], xT[0][:, k, :], w[:, k, :],
                                                   start=(k == 0), stop=(k == K - 1))
                                mm.then_inc(signal, 1)
                            pe.wait_ge(s["hid_ready"], 1)
                            for k in range(4):
                                mm = pe.transpose(HB[:, k * P:(k + 1) * P], hid[:, k * P:(k + 1) * P], ident)
                            mm.then_inc(s["hid_tr"], 1)
                            pe.wait_ge(s["hidt_ready"], 1)
                            pe.wait_ge(slot[2], 16)
                            w = ring[:, 2, :].rearrange("p (k n) -> p k n", k=4)
                            for half in range(2):
                                for k in range(4):
                                    mm = pe.matmul(YB[half][:, :], hidT[:, k, :],
                                                   w[:, k, half * 512:(half + 1) * 512],
                                                   start=(k == 0), stop=(k == 3))
                            mm.then_inc(s["down_mm"], 1)
                    clear_semaphores()

            with nc.Block() as block:
                @block.sync
                def _(sp):
                    sp.dma_start(g2b, mod_dram.rearrange("(m r) p -> m (r p)", r=K)
                                 [bass.ds(l * 6 + GATE2, 1), :].partition_broadcast(P)).then_inc(s["gate2_in"], 16)
                    sp.wait_ge(s["gate2_in"], 16)

                @block.gpsimd
                def _(pool):
                    for t in range(T):
                        for j in range(2):
                            pool.indirect_dma_start(
                                got[t][j], None, ys_dram,
                                bass.IndirectOffsetOnAxis(ap=posu[:, j, t:t + 1], axis=0),
                                bounds_check=ROWS - 1, oob_is_err=True).then_inc(got_in[t], 16)

                @block.scalar
                def _(act):
                    for t in range(T):
                        act.wait_ge(got_in[t], l * 32 + 32)
                        act.activation(got[t][0], got[t][0], ACT.Copy, scale=gates[:, 0, t:t + 1])\
                           .then_inc(s["scaled"], 1)

                @block.vector
                def _(v):
                    step = stepper(v, dve_step)
                    v.wait_ge(s["gate2_in"], 16)
                    for t in range(T):
                        a, b = got[t]
                        v.wait_ge(s["scaled"], t + 1)
                        step(v.scalar_tensor_tensor(b, b, gates[:, 1, t:t + 1], a, ALU.mult, ALU.add))
                        step(v.tensor_tensor(b, b, g2b, ALU.mult))
                        v.tensor_tensor(x[:, t, :], x[:, t, :], b, ALU.add).then_inc(s["combined"], 1)
            clear_semaphores()

        with nc.Block() as block:
            @block.sync
            def _(sp):
                sp.dma_start(out_tok, x[:, :, :]).then_inc(s["stored"], 16)
                sp.wait_ge(s["stored"], 16)


_INS = ["x", "c", "positions", "w_ada", "b_ada", "norm1", "w_in", "q_norm", "k_norm", "conv_w", "conv_b",
        "conv_ln_g", "conv_ln_b", "conv_pw_w", "conv_pw_b", "pool_w", "pool_b", "pool_scale", "sgu_ln_g",
        "sgu_ln_b", "sgu_w", "sgu_b", "out_norm", "w_out", "norm2", "w_rg", "b_rg", "w_re", "b_re", "w_gate",
        "w_up", "w_down"]


def kernel(**inputs):
    import concourse.bacc as _bacc
    from concourse.bass_utils import run_bass_kernel_spmd as _run

    arrays = {name: np.ascontiguousarray(inputs[name]) for name in _INS}
    arrays["constants"] = constants()[0]
    nc = _bacc.Bacc("TRN2", target_bir_lowering=False, num_devices=1)
    A = {name: nc.dram_tensor(f"in_{name}", a.shape, mybir.dt.from_np(a.dtype), kind="ExternalInput").ap()
         for name, a in arrays.items()}
    out = nc.dram_tensor("out_0", (1, S, D), F32, kind="ExternalOutput").ap()
    build(nc, A, out)
    r = _run(nc, [{f"in_{name}": a for name, a in arrays.items()}], core_ids=[0])
    return r.results[0]["out_0"]
```

```python
from contextlib import ExitStack

import numpy as np

import concourse.bass as bass
from concourse import mybir

F32 = mybir.dt.float32
I32 = mybir.dt.int32
U32 = mybir.dt.uint32
ALU = mybir.AluOpType
ACT = mybir.ActivationFunctionType
AX = mybir.AxisListType

P = 128
D = 1024
S = 512
DEPTH = 2
T = S // P
K = D // P
G = D // 4
HEADS, HD = 4, 64
ROT = HD // 8
IH, ID = 4, 32
IROT = ID // 8
CHUNK = 64
TOPK = min(256, S // 4)
TAPS = 31
SGU_H = 4
NG, EPG = 4, 8
E = NG * EPG
FF = 512
EPS = 1e-6
THETA = 500000.0
D_IN = 8 * G + IH * ID + ID + IH

C_Q, C_V, C_CONV = 0, 2 * G, 3 * G + IH * ID + ID + IH
C_POOL, C_SGU = C_CONV + 2 * G, C_CONV + 3 * G
NA = C_CONV - C_V

R_MOD, R_N1, R_N2, R_ON, R_CB, R_LG, R_LB, R_PB, R_QB, R_QS = 0, 48, 56, 64, 72, 74, 76, 78, 80, 82
NROW = 84
SHIFT1, SCALE1, GATE1, SHIFT2, SCALE2, GATE2 = range(6)

RING = 6
ADA_COLS = 512
ADA_CHUNKS = 6 * D // ADA_COLS
N_IN, N_OUT = 5, 2
N_PRE = N_IN + N_OUT
N_CHUNKS = N_PRE + 3 * E

OVER_BLOCKS = 7
ROWS = 2 * S + P
NEG = -3.0e38
GONE = -3.4e38
MASK = -1.0e30
MAGIC = 12582912.0
TWO_PI = 2 * np.pi
PI1 = 6.28125
PI2 = float(np.float32(TWO_PI - PI1) - np.float32(TWO_PI - PI1) % np.float32(2.0 ** -20))
PI3 = float(TWO_PI - PI1 - PI2)


def constants():
    p = np.arange(P)[:, None]
    j = np.arange(P)[None, :]
    parts = {
        "ident": (p == j),
        "mean256": np.full((P, P), 1.0 / G),
        "mean64": (p // 64 == j // 64) / 64.0,
        "upto": (p <= j),
        "before": (p < j),
        "ones": np.ones((P, P)),
        "mask0": np.where((p < CHUNK) & (j >= CHUNK), MASK, 0.0),
        "iota": np.broadcast_to(np.arange(E), (P, E)),
        "invf": np.broadcast_to(np.concatenate([
            np.power(np.float32(THETA), (-2.0 * np.arange(ROT, dtype=np.float32) / np.float32(2 * ROT))),
            np.power(np.float32(THETA), (-2.0 * np.arange(IROT, dtype=np.float32) / np.float32(2 * IROT))),
        ]), (P, ROT + IROT)),
        "eps": np.full((P, 1), EPS),
    }
    win = np.array([2, 4, 8, 16])
    own = np.stack([win[0 + (p[:, 0] // 64)], win[2 + (p[:, 0] // 64)]], 1)
    parts["invw"] = 1.0 / own
    first = np.minimum(np.arange(1, 17)[None, None, :], own[:, :, None])
    parts["invc"] = (1.0 / first).reshape(P, 32)
    parts["blk"] = np.broadcast_to(np.arange(OVER_BLOCKS), (P, OVER_BLOCKS))
    where, at = {}, 0
    for name, a in parts.items():
        where[name] = (at, at + a.shape[1])
        at += a.shape[1]
    return np.concatenate([np.asarray(a, np.float32) for a in parts.values()], 1), where


def build(nc, A, out, debug=None):
    ctx = ExitStack()
    cw = constants()[1]
    NCONST = max(b for _, b in cw.values())

    def sb(name, shape, dt=F32):
        return ctx.enter_context(nc.sbuf_tensor(name, shape, dt))

    sems = []

    def sem(name, cleared=True):
        q = ctx.enter_context(nc.semaphore(name))
        if cleared:
            sems.append(q)
        return q

    mod_dram = nc.dram_tensor("mod_scratch", [DEPTH * 48, P], F32, kind="Internal").ap()
    xs_dram = nc.dram_tensor("sorted_tokens", [ROWS, D], F32, kind="Internal").ap()
    ys_dram = nc.dram_tensor("sorted_outputs", [ROWS, D], F32, kind="Internal").ap()
    x_tok = A["x"].rearrange("b (t p) d -> p (b t) d", p=P)
    out_tok = out.rearrange("b (t p) d -> p (b t) d", p=P)
    ada_v = A["w_ada"].rearrange("l (k p) n -> l p k n", p=P)
    win_v = A["w_in"].rearrange("l (k p) n -> l p k n", p=P)
    wout_v = A["w_out"].rearrange("l (k p) n -> l p k n", p=P)
    wg_v = A["w_gate"].rearrange("l e (k p) n -> l e p k n", p=P)
    wu_v = A["w_up"].rearrange("l e (k p) n -> l e p k n", p=P)
    wd_v = A["w_down"].rearrange("l e (k p) n -> l e p k n", p=P)

    with ctx:
        cst = sb("cst", [P, NCONST])

        def c(name):
            a, b = cw[name]
            return cst[:, a:b]

        ident = c("ident")
        x = sb("x_resident", [P, T, D])
        ring = sb("ring", [P, RING, 4096])
        work = sb("work", [P, 2 * 4096 + 4752])
        hT = work[:, 0:4096].rearrange("p (k s) -> p k s", k=K)
        mixT = work[:, 4096:8192].rearrange("p (k s) -> p k s", k=K)
        xn = work[:, 4096:8192].rearrange("p (t d) -> p t d", t=T)
        tokA = work[:, 8192:8192 + T * NA].rearrange("p (t n) -> p t n", t=T)
        tokB = work[:, 8192 + T * NA:8192 + T * (NA + 512)].rearrange("p (t n) -> p t n", t=T)
        dv = work[:, 8192 + T * (NA + 512):].rearrange("p (t n) -> p t n", t=T)
        prob = work[:, 0:2048].rearrange("p (h n) -> p h n", h=HEADS)
        probT = work[:, 2048:3072].rearrange("p (b n) -> p b n", b=2)
        xT = [work[:, i * 1024:(i + 1) * 1024].rearrange("p (k s) -> p k s", k=K) for i in range(2)]
        sgate = work[:, 2048:2560]
        hid = work[:, 2560:3072]
        hidT = work[:, 3072:3584].rearrange("p (k s) -> p k s", k=4)
        xs = [work[:, 4096 + i * 1024:5120 + i * 1024] for i in range(2)]
        ybuf = [work[:, 6144 + i * 1024:7168 + i * 1024] for i in range(2)]
        xn2 = work[:, 0:4096].rearrange("p (t d) -> p t d", t=T)
        h2T = mixT
        got = [[work[:, 4096 + (2 * t + j) * 1024:5120 + (2 * t + j) * 1024] for j in range(2)] for t in range(T)]
        mrow = work[0:1, 0:DEPTH * 6 * D]
        score = sb("score", [P, 1152])
        crow = score[0:K, 0:P]
        ccol = sb("ccol", [P, K])
        posi = sb("posi", [P, T], I32)
        posf = sb("posf", [P, T])
        ang = sb("ang", [P, T, ROT + IROT])
        turn = sb("turn", [P, T, ROT + IROT])
        sn = sb("sn", [P, T, ROT + IROT])
        cs = sb("cs", [P, T, ROT + IROT])
        prow = sb("prow", [NROW, P])
        cwrow = sb("cwrow", [2 * TAPS, P])
        pcol = sb("pcol", [P, NROW])
        cwcol = sb("cwcol", [P, 2 * TAPS])
        scl = sb("scl", [P, 2, K])
        qkn = sb("qkn", [P, 2, HD])
        sgn = sb("sgn", [P, 2, G])
        sgb = sb("sgb", [P, 2, P])
        sgw = sb("sgw", [P, SGU_H, P])
        sgwT = sb("sgwT", [P, SGU_H, P])
        pww = sb("pww", [P, 2, G])
        plw = sb("plw", [P, 2, P])
        wr = sb("wr", [P, K, NG + E])
        rb = sb("rb", [P, NG + E])
        convin = sb("convin", [P, 2, TAPS - 1 + S])
        c_last = sgw[:, 0, :]
        ada_sum = [convin[:, i, 0:ADA_COLS] for i in range(2)]
        acc = mixT[:, 2:4, :]
        uT = mixT[:, 6:8, :]
        sig = uT
        poolin = sb("poolin", [P, 2, 16 + S])
        qT = work[:, 3072:4096].rearrange("p (h n) -> p h n", h=2)
        kT = tokB[:, :, 0:2 * P]
        sums_tile = sb("window_sums", [P, 2 * 2 * (16 + S)])
        wsum = [sums_tile[:, i * 2 * (16 + S):(i + 1) * 2 * (16 + S)].rearrange("p (h n) -> p h n", h=2)
                for i in range(2)]
        tap_buf = [wsum[1][:, i, 0:S] for i in range(2)]
        iqT, ikT = wsum[0][:, 0, 0:S], wsum[0][:, 1, 0:S]
        tokB_flat = work[:, 8192 + T * NA:8192 + T * (NA + 512)]
        ik4 = tokB_flat[:, 0:S].rearrange("p (t n) -> p t n", t=T)
        sq = sb("sq", [P, 2, S])
        relu = [tokB_flat[:, (1 + i) * S:(2 + i) * S] for i in range(2)]
        SC = [0, 0, 256, 640]
        g1b = convin[:, :, :].rearrange("p h n -> p (h n)")[:, 0:D]
        g2b = work[:, 8192:8192 + D]
        small = sb("small", [P, 256])
        ss = small[:, 0:4]
        rs = small[:, 4:8]
        ssq = small[:, 8:40]
        rsq = small[:, 40:72]
        m8 = small[:, 72:80]
        mx = small[:, 80:84]
        nmx = small[:, 84:88]
        sums = small[:, 88:92]
        rsum = small[:, 92:96]
        bst = small[:, 96:120].rearrange("p (t n) -> p t n", t=T)
        bag = small[:, 120:128].rearrange("p (t n) -> p t n", t=T)
        rdv = small[:, 128:132]
        gidx = small[:, 132:136]
        gmax = small[:, 136:140]
        psel = small[:, 140:144]
        gates = small[:, 144:152].rearrange("p (j t) -> p j t", j=2)
        posr = small[:, 152:160].rearrange("p (j t) -> p j t", j=2)
        top8 = small[:, 160:192].rearrange("p (t n) -> p t n", t=T)
        topf = small[:, 192:224].rearrange("p (t n) -> p t n", t=T)
        ediff = small[:, 224:228]
        ropet = sq[:, :, :].rearrange("p h n -> p (h n)").rearrange("p (i t h r) -> p i t h r", i=4, t=T, h=8)
        sq_flat = sq[:, :, :].rearrange("p h n -> p (h n)")
        lgT = sq[0:NG + E, 0, :]
        taken = [0]

        def late(*shape):
            n = int(np.prod(shape))
            a = taken[0]
            taken[0] += n
            assert taken[0] <= 4 * (16 + S)
            flat = sums_tile[:, a:a + n]
            if len(shape) == 2:
                return flat.rearrange("p (a b) -> p a b", a=shape[0])
            return flat.rearrange("p (a b c) -> p a b c", a=shape[0], b=shape[1])

        lg = late(T, NG + E)
        r4 = late(3, T, NG)
        el = late(T, E)
        oh = late(3, T, E)
        rank = late(T, E)
        rtmp = late(T, E)
        tiles = rtmp
        cnt = late(9, E)
        exc = late(4, E)
        ovm = late(3, OVER_BLOCKS, E)
        topi = sb("topi", [P, T, 8], U32)
        ovf = sb("ovf", [P, 2, OVER_BLOCKS])
        posu = sb("posu", [P, 2, T], U32)
        starti = sb("starti", [1, E], I32)
        ovi = sb("ovi", [1, 16], I32)

        bank = [ctx.enter_context(nc.psum_tensor(f"bank{i}", [P, 512], F32)) for i in range(8)]

        GB, UB, HB = bank[0], bank[1], bank[2]
        YB, XP = bank[3:5], bank[5:7]
        conv_place = convin[:, :, 0:S]
        mix_sq_buf = {3: conv_place, 2: wsum[0][:, :, 16:], 1: wsum[1][:, :, 16:], 0: conv_place}
        rmix = small[:, 232:248].rearrange("p (g t) -> p g t", g=4)

        slot = [sem(f"slot{i}_loaded") for i in range(RING)]
        pe_done = sem("pe_done")
        act_evac = sem("act_evac")
        dve_evac = sem("dve_evac")
        act_step = sem("act_step")
        dve_step = sem("dve_step")
        pool_step = sem("pool_step")
        xs_in = [sem(f"xs_in{i}") for i in range(2)]
        zeroed = sem("zeroed", cleared=False)
        scattered = sem("scattered", cleared=False)
        got_in = [sem(f"got_in{t}", cleared=False) for t in range(T)]
        s = {name: sem(name) for name in (
            "consts_in", "x_in", "c_in", "pos_in", "bada_in", "mod_out", "rows_in", "taps_in",
            "norms_in", "sgu_in", "pw_in", "router_in", "gate1_in", "gate2_in", "y_written", "stored",
            "mod_done", "mod_evac", "c_silu", "turns_ready", "ada_summed", "ada_step",
            "rstd_done", "xn_done", "scl_ready", "conv_in", "idx_roped", "relu_free", "tap_ready", "tap_added", "conv_done",
            "qk_ss", "qk_rstd", "qk_roped", "sgu_var", "sgu_rstd", "sgu_normed", "pooled", "exp_in",
            "exp_done", "prob_ready", "centered", "centered_sq", "conv_normed", "swished", "mix_ready",
            "mix_sq", "wout_scaled", "x_added",
            "gexp_in", "gexp_out", "oh_ready", "rows_known", "routed",
            "gate_mm", "up_mm", "hid_tr", "down_mm", "xs_tr", "xt_ready", "silu_done", "hid_ready", "hidt_ready",
            "y_ready")}

        def clear_semaphores():
            nums = sorted(q.num for q in sems)
            kept = [q.num for q in (zeroed, scattered, *got_in)]
            nc.all_engine_barrier()
            nc.gpsimd.sem_clear(range(nums[0], kept[0]))
            nc.gpsimd.sem_clear(range(kept[-1] + 1, nums[-1] + 1))
            nc.all_engine_barrier()

        def stepper(eng, done):
            n = [0]

            def step(ins):
                n[0] += 1
                ins.then_inc(done, 1)
                eng.wait_ge(done, n[0])
            return step

        def root_mean_square(act, step, t):
            step(act.activation(score[:, 0:D], x[:, t, :], ACT.Square, accum_out=ss[:, t:t + 1]))
            return act.activation(rs[:, t:t + 1], ss[:, t:t + 1], ACT.Sqrt, bias=c("eps"), scale=1.0 / D)

        HALF = ADA_CHUNKS // RING
        with nc.Block() as block:
            @block.sync
            def _(sp):
                sp.dma_start(cst[:, :], A["constants"]).then_inc(s["consts_in"], 16)
                sp.dma_start(x[:, :, :], x_tok).then_inc(s["x_in"], 16)
                with sp.Fori(0, DEPTH) as l:
                    with sp.Fori(0, HALF) as i:
                        for j in range(RING):
                            src = ada_v[l, :, :, bass.ds((i * RING + j) * ADA_COLS, ADA_COLS)]
                            dst = ring[:, j, :].rearrange("p (k n) -> p k n", k=K)
                            sp.wait_ge(s["mod_evac"], (l * HALF + i) * RING + j + 1)
                            sp.dma_start(dst, src).then_inc(slot[j], 16)

            @block.scalar
            def _(act):
                act.sem_inc(s["mod_evac"], RING)
                act.dma_start(crow[:, :], A["c"].rearrange("b (k p) -> (b k) p", p=P)).then_inc(s["c_in"], 16)
                act.dma_start(posi[:, :], A["positions"].rearrange("b (t p) -> p (b t)", p=P),
                              allow_slow_non_contiguous=True).then_inc(s["pos_in"], 16)
                act.dma_start(mrow, A["b_ada"].rearrange("(a l) n -> a (l n)", a=1)).then_inc(s["bada_in"], 16)
                act.wait_ge(s["c_in"], 16)
                act.activation(crow[:, :], crow[:, :], ACT.Silu).then_inc(s["c_silu"], 1)
                act.wait_ge(s["turns_ready"], 1)
                act.activation(sn[:, :, :], ang[:, :, :], ACT.Sin)
                act.activation(cs[:, :, :], turn[:, :, :], ACT.Sin)
                step = stepper(act, act_step)
                act.wait_ge(s["x_in"], 16)
                act.wait_ge(pe_done, 1)
                for t in range(T):
                    root_mean_square(act, step, t)
                with act.Fori(0, DEPTH) as l:
                    with act.Fori(0, HALF) as i:
                        for j in range(RING):
                            at = act.snap(((l * HALF + i) * RING + j) * ADA_COLS)
                            act.wait_ge(s["mod_done"], (l * HALF + i) * RING + j + 1 + 2)
                            act.activation(mrow[:, bass.ds(at, ADA_COLS)], bank[j][0:1, :], ACT.Copy)\
                               .then_inc(s["mod_evac"], 1)
                act.wait_ge(s["mod_evac"], RING + DEPTH * ADA_CHUNKS)
                act.dma_start(mod_dram.rearrange("(a r) p -> a (r p)", a=1), mrow).then_inc(s["mod_out"], 16)
                act.wait_ge(s["mod_out"], 16)

            @block.vector
            def _(v):
                step = stepper(v, dve_step)
                v.memset(poolin[:, :, 0:16], 0.0)
                v.memset(plw[:, :, :], 0.0)
                v.wait_ge(s["consts_in"], 16)
                v.wait_ge(s["pos_in"], 16)
                nf = ROT + IROT
                step(v.tensor_copy(posf[:, :], posi[:, :]))
                step(v.tensor_tensor(ang[:, :, :], posf[:, :].unsqueeze(2).to_broadcast([P, T, nf]),
                                     c("invf").unsqueeze(1).to_broadcast([P, T, nf]), ALU.mult))
                step(v.tensor_scalar(turn[:, :, :], ang[:, :, :], 1.0 / TWO_PI, MAGIC, ALU.mult, ALU.add))
                step(v.tensor_scalar(turn[:, :, :], turn[:, :, :], MAGIC, None, ALU.subtract))
                for part in (PI1, PI2, PI3):
                    step(v.scalar_tensor_tensor(ang[:, :, :], turn[:, :, :], -part, ang[:, :, :],
                                                ALU.mult, ALU.add))
                step(v.tensor_scalar(ang[:, :, :], ang[:, :, :], 3.1415925, -3.1415925, ALU.min, ALU.max))
                step(v.tensor_scalar(turn[:, :, :], ang[:, :, :], -1.0, None, ALU.mult))
                step(v.tensor_tensor(turn[:, :, :], turn[:, :, :], ang[:, :, :], ALU.min))
                v.tensor_scalar(turn[:, :, :], turn[:, :, :], float(np.pi / 2), None, ALU.add)\
                    .then_inc(s["turns_ready"], 1)
                v.wait_ge(pe_done, 1)
                v.tensor_copy(c_last, bank[7][:, K - 1:K].to_broadcast([P, P]))
                v.tensor_copy(ccol[:, :], bank[7][:, 0:K]).then_inc(dve_evac, 1)
                v.wait_ge(dve_evac, 1)
                with v.Fori(0, DEPTH) as l:
                    with v.Fori(0, HALF) as i:
                        for j in range(RING):
                            w = ring[:, j, :].rearrange("p (k n) -> p k n", k=K)
                            dst = ada_sum[j % 2]
                            v.wait_ge(slot[j], (l * HALF + i + 1) * 16)
                            v.wait_ge(s["mod_done"], (l * HALF + i) * RING + j + 1)
                            for k in range(K - 1):
                                if k == 0:
                                    ins = v.tensor_scalar(dst, w[:, k, :], ccol[:, k:k + 1], None, ALU.mult)
                                else:
                                    ins = v.scalar_tensor_tensor(dst, w[:, k, :], ccol[:, k:k + 1], dst,
                                                                 ALU.mult, ALU.add)
                                if k < K - 2:
                                    ins.then_inc(s["ada_step"], 1)
                                    v.wait_ge(s["ada_step"], ((l * HALF + i) * RING + j) * (K - 2) + k + 1)
                            ins.then_inc(s["ada_summed"], 1)

            @block.gpsimd
            def _(pool):
                pool.memset(sq[:, :, :], 0.0).then_inc(pool_step, 1)
                pool.wait_ge(pool_step, 1)
                zero = sq[:, :, :].rearrange("p h n -> p (h n)")
                for b in range((ROWS - 2 * S) // P):
                    for scratch in (xs_dram, ys_dram):
                        pool.dma_start(scratch[2 * S + b * P:2 * S + (b + 1) * P, :], zero)\
                            .then_inc(zeroed, 16)
                pool.wait_ge(zeroed, 2 * 16 * ((ROWS - 2 * S) // P))

            @block.tensor
            def _(pe):
                pe.sem_inc(s["mod_done"], 2)
                pe.wait_ge(s["consts_in"], 16)
                pe.wait_ge(s["c_silu"], 1)
                pe.transpose(bank[7][:, 0:K], crow[:, :], ident[0:K, 0:K]).then_inc(pe_done, 1)
                pe.wait_ge(dve_evac, 1)
                pe.wait_ge(s["bada_in"], 16)
                with pe.Fori(0, DEPTH) as l:
                    with pe.Fori(0, HALF) as i:
                        for j in range(RING):
                            at = pe.snap(((l * HALF + i) * RING + j) * ADA_COLS)
                            pe.wait_ge(slot[j], (l * HALF + i + 1) * 16)
                            pe.wait_ge(s["mod_evac"], (l * HALF + i) * RING + j + 1)
                            pe.matmul(bank[j][:, :], c_last, ring[:, j, (K - 1) * ADA_COLS:K * ADA_COLS],
                                      start=True, stop=False)
                            pe.matmul(bank[j][:, :], c("ones")[0:1, :], mrow[:, bass.ds(at, ADA_COLS)],
                                      start=False, stop=False)
                            pe.wait_ge(s["ada_summed"], (l * HALF + i) * RING + j + 1)
                            pe.matmul(bank[j][:, :], c("ones"), ada_sum[j % 2], start=False, stop=True)\
                                .then_inc(s["mod_done"], 1)
        clear_semaphores()

        jobs = [(f"h{k}", "act") for k in range(K // 2)] + [("params", "dve"), ("taps", "dve")]
        jobs += [(f"h{k}", "dve") for k in range(K // 2, K)]
        jobs += [(f"A{t}", "act") for t in range(T)]
        jobs += [("cg0", "act"), ("ca0", "dve"), ("cg1", "act"), ("ca1", "dve"), ("iqT", "act"), ("ikT", "act")]
        jobs += [(f"idx{b}{h}", "act") for b in range(1, T) for h in range(IH)]
        jobs += [(f"B{t}", "act") for t in range(T)]
        jobs += [("pool0", "act"), ("pool1", "act"), ("u0", "act"), ("u1", "act")]
        jobs += [(f"E{t}", "act") for t in range(T)]
        jobs += [("qT0", "act"), ("qT1", "act"), ("kT0", "act"), ("kT1", "act")]

        def logit_jobs(b):
            return [(f"logit{b}{h}", "dve") for h in range(HEADS)]

        def value_jobs(b):
            out_ = []
            for pair in range(2):
                out_ += [(f"probT{b}{2 * pair}", "act"), (f"probT{b}{2 * pair + 1}", "act"), (f"pv{b}{pair}", "act")]
            return out_

        WARM = (14, 14, 12, 4)
        TN = [(t, n) for t in range(T) for n in range(N_OUT)]

        def out_jobs(g, tn):
            return [(f"out{g}{t}{n}", "dve") for t, n in tn]

        jobs += logit_jobs(0) + [("sgw", "dve")] + value_jobs(0) + [("sgu0", "dve"), ("sgu1", "dve")]
        jobs += logit_jobs(1) + [("cmean0", "dve"), ("cmean1", "dve")] + value_jobs(1)
        jobs += logit_jobs(2) + [("ms3", "act"), ("cvar0", "act"), ("cvar1", "act")] + out_jobs(3, TN[:4])
        jobs += value_jobs(2) + logit_jobs(3) + [("pl0", "dve"), ("pl1", "dve")] + out_jobs(3, TN[4:])
        jobs += [("pw0", "dve"), ("pw1", "dve"), ("ms2", "act")] + value_jobs(3) + out_jobs(2, TN)
        jobs += [("ms1", "act"), ("ms0", "act")] + out_jobs(1, TN) + out_jobs(0, TN)
        jobs += [(f"m{k}", "act") for k in range(K)]
        jobs += [("routeT", "act"), ("route", "dve"), ("rank", "dve")]
        index = {name: i for i, (name, _) in enumerate(jobs)}

        def done(name):
            return index[name] + 1

        def emptied(name):
            i = index[name]
            return sum(1 for _, e in jobs[:i + 1] if e == jobs[i][1])

        def bank_of(name):
            return bank[index[name] % 8]

        def await_bank(pe, name):
            i = index[name] - 8
            if i >= 0:
                pe.wait_ge(act_evac if jobs[i][1] == "act" else dve_evac, emptied(jobs[i][0]))

        IN_COLS = [(C_V, NA), (C_CONV, 2 * G), (C_Q, 2 * G), (C_POOL, 2 * G), (C_SGU + G, G)]
        IN_LAST = ["A3", "ca1", "B3", "u1", "E3", "out030", "out031"]

        def chunk_view(n, width):
            return ring[:, n % RING, 0:K * width].rearrange("p (k n) -> p k n", k=K)

        def loaded(n):
            return slot[n % RING], 16 * (n // RING + 1)

        with nc.Fori(0, DEPTH) as l:
            with nc.Block() as block:
                @block.sync
                def _(sp):
                    def expert_chunk(n, kind, e):
                        src = {"g": wg_v, "u": wu_v, "d": wd_v}[kind][l, e]
                        k = K if kind in "gu" else FF // P
                        sp.dma_start(ring[:, n % RING, :].rearrange("p (k n) -> p k n", k=k), src)\
                            .then_inc(slot[n % RING], 16)

                    def static_wait(n):
                        if n >= RING:
                            sp.wait_ge(pe_done, done(IN_LAST[n - RING]))

                    sp.dma_start(prow[R_MOD:R_MOD + 48, :], mod_dram[bass.ds(l * 48, 48), :])\
                      .then_inc(s["rows_in"], 16)
                    for r, name in ((R_N1, "norm1"), (R_N2, "norm2")):
                        sp.dma_start(prow[r:r + K, :], A[name][l].rearrange("(r p) -> r p", p=P))\
                          .then_inc(s["rows_in"], 16)
                    sp.dma_start(prow[R_QB:R_QB + 2, :], A["pool_b"][l].rearrange("(r a) c -> r (a c)", a=2))\
                      .then_inc(s["rows_in"], 16)
                    sp.dma_start(cwrow[:, :], A["conv_w"][l].rearrange("w (h p) -> (w h) p", p=P))\
                      .then_inc(s["taps_in"], 16)
                    for n, (a, w) in enumerate(IN_COLS):
                        sp.dma_start(chunk_view(n, w), win_v[l, :, :, a:a + w]).then_inc(slot[n], 16)
                        if n == 0:
                            sp.dma_start(g1b, mod_dram.rearrange("(m r) p -> m (r p)", r=K)
                                         [bass.ds(l * 6 + GATE1, 1), :].partition_broadcast(P))\
                              .then_inc(s["gate1_in"], 16)
                    for j, name in enumerate(("q_norm", "k_norm")):
                        sp.dma_start(qkn[:, j, :], A[name][l].partition_broadcast(P)).then_inc(s["norms_in"], 16)
                    for j, name in enumerate(("sgu_ln_g", "sgu_ln_b")):
                        sp.dma_start(sgn[:, j, :], A[name][l].partition_broadcast(P)).then_inc(s["sgu_in"], 16)
                    for h in range(SGU_H):
                        sp.dma_start(sgb[64 * (h % 2):64 * (h % 2) + 64, h // 2, :],
                                      A["sgu_b"][l, h].partition_broadcast(64)).then_inc(s["sgu_in"], 16)
                    sp.dma_start(sgw[:, :, :], A["sgu_w"][l].rearrange("h t s -> t h s")).then_inc(s["sgu_in"], 16)
                    sp.dma_start(pww[:, :, :], A["conv_pw_w"][l].rearrange("(i p) n -> p i n", p=P))\
                       .then_inc(s["pw_in"], 16)
                    for g in range(4):
                        o = 64 * (g % 2)
                        sp.dma_start(plw[o:o + 64, g // 2, o:o + 64], A["pool_w"][l, g]).then_inc(s["pw_in"], 16)
                    sp.dma_start(wr[:, :, 0:NG], A["w_rg"][l].rearrange("(k p) g -> p k g", p=P))\
                       .then_inc(s["router_in"], 16)
                    sp.dma_start(wr[:, :, NG:], A["w_re"][l].rearrange("(k p) g e -> p k (g e)", p=P))\
                       .then_inc(s["router_in"], 16)
                    sp.dma_start(rb[:, 0:NG], A["b_rg"][l].partition_broadcast(P)).then_inc(s["router_in"], 16)
                    sp.dma_start(rb[:, NG:], A["b_re"][l].rearrange("g e -> (g e)").partition_broadcast(P))\
                       .then_inc(s["router_in"], 16)
                    for j in range(N_OUT):
                        n = N_IN + j
                        static_wait(n)
                        sp.dma_start(chunk_view(n, 512), wout_v[l, :, :, j * 512:(j + 1) * 512])\
                            .then_inc(slot[n % RING], 16)
                    for n, (kind, e) in enumerate([("g", 0), ("u", 0), ("g", 1), ("u", 1), ("d", 0), ("g", 2)], N_PRE):
                        static_wait(n)
                        expert_chunk(n, kind, e)
                    sp.dma_start(g2b, mod_dram.rearrange("(m r) p -> m (r p)", r=K)
                                 [bass.ds(l * 6 + GATE2, 1), :].partition_broadcast(P)).then_inc(s["gate2_in"], 16)

                    def step_pair(i, first=False, last=False):
                        n = 13
                        sp.wait_ge(s["gate_mm"] if first else s["up_mm"], 1 if first else 2 * i + 1)
                        expert_chunk(n, "u", 2 * i + 2)
                        if first:
                            sp.wait_ge(s["up_mm"], 1)
                        else:
                            sp.wait_ge(s["down_mm"], 2 * i)
                        expert_chunk(n + 1, "d", 2 * i + 1)
                        sp.wait_ge(s["gate_mm"], 2 * i + 2)
                        expert_chunk(n + 2, "g", 2 * i + 3)
                        sp.wait_ge(s["up_mm"], 2 * i + 2)
                        expert_chunk(n + 3, "u", 2 * i + 3)
                        sp.wait_ge(s["down_mm"], 2 * i + 1)
                        expert_chunk(n + 4, "d", 2 * i + 2)
                        sp.wait_ge(s["gate_mm"], 2 * i + 3)
                        if last:
                            expert_chunk(n + 5, "d", E - 1)
                        else:
                            expert_chunk(n + 5, "g", 2 * i + 4)

                    step_pair(0, first=True)
                    with sp.Fori(1, E // 2 - 2) as i:
                        step_pair(i)
                    step_pair(E // 2 - 2, last=True)

                @block.scalar
                def _(act):
                    step = stepper(act, act_step)
                    for r, name, n in ((R_ON, "out_norm", K), (R_CB, "conv_b", 2), (R_LG, "conv_ln_g", 2),
                                       (R_LB, "conv_ln_b", 2), (R_PB, "conv_pw_b", 2), (R_QS, "pool_scale", 2)):
                        act.dma_start(prow[r:r + n, :], A[name][l].rearrange("(r p) -> r p", p=P))\
                           .then_inc(s["rows_in"], 16)
                    act.wait_ge(s["scl_ready"], 1)
                    for k in range(K // 2):
                        act.wait_ge(pe_done, done(f"h{k}"))
                        act.activation(hT[:, k, :], bank_of(f"h{k}")[:, :], ACT.Identity,
                                       bias=pcol[:, SHIFT1 * K + k:SHIFT1 * K + k + 1], scale=scl[:, 0, k:k + 1])\
                           .then_inc(act_evac, 1)
                    for t in range(T):
                        act.wait_ge(pe_done, done(f"A{t}"))
                        act.activation(tokA[:, t, :], bank_of(f"A{t}")[:, 0:NA], ACT.Copy).then_inc(act_evac, 1)
                    for h in range(2):
                        act.wait_ge(pe_done, done(f"cg{h}"))
                        act.activation(sig[:, h, :], bank_of(f"cg{h}")[:, :], ACT.Sigmoid).then_inc(act_evac, 1)
                    for name, dst in (("iqT", iqT), ("ikT", ikT)):
                        act.wait_ge(pe_done, done(name))
                        act.activation(dst[:, :], bank_of(name)[:, :], ACT.Copy).then_inc(act_evac, 1)
                    def taps(first, count):
                        for n in range(first, min(first + count, 2 * TAPS)):
                            h, w = divmod(n, TAPS)
                            src, weight = convin[:, h, w:w + S], cwcol[:, 2 * w + h:2 * w + h + 1]
                            if w == 0:
                                act.wait_ge(s["conv_in"], h + 1)
                                ins = act.activation(acc[:, h, :], src, ACT.Identity, scale=weight,
                                                     bias=pcol[:, R_CB + h:R_CB + h + 1])
                            else:
                                m = h * (TAPS - 1) + w - 1
                                if m >= 2:
                                    act.wait_ge(s["tap_added"], m - 1)
                                ins = act.activation(tap_buf[m % 2], src, ACT.Copy, scale=weight)
                            ins.then_inc(s["tap_ready"], 1)

                    n_relu = 0
                    for b in range(1, T):
                        for h in range(IH):
                            act.wait_ge(pe_done, done(f"idx{b}{h}"))
                            if n_relu >= 2:
                                act.wait_ge(s["relu_free"], n_relu - 1)
                            w = (b + 1) * P
                            act.activation(relu[n_relu % 2][:, 0:w], bank_of(f"idx{b}{h}")[:, 0:w], ACT.Relu,
                                           scale=float(ID ** -0.5 * IH ** -0.5)).then_inc(act_evac, 1)
                            taps(n_relu, 1)
                            n_relu += 1

                    act.wait_ge(s["relu_free"], n_relu)
                    for t in range(T):
                        act.wait_ge(pe_done, done(f"B{t}"))
                        act.activation(tokB[:, t, :], bank_of(f"B{t}")[:, :], ACT.Copy).then_inc(act_evac, 1)
                        taps(12 + 6 * t, 6)
                    for h in range(2):
                        act.wait_ge(pe_done, done(f"pool{h}"))
                        act.activation(poolin[:, h, 16:], bank_of(f"pool{h}")[:, :], ACT.Copy).then_inc(act_evac, 1)
                        taps(36 + 6 * h, 6)
                    act.wait_ge(s["qk_ss"], 1)
                    act.activation(rsq, ssq, ACT.Sqrt, bias=c("eps"), scale=1.0 / HD).then_inc(s["qk_rstd"], 1)
                    act.wait_ge(s["conv_in"], 2)
                    for h in range(2):
                        act.wait_ge(pe_done, done(f"u{h}"))
                        act.activation(uT[:, h, :], bank_of(f"u{h}")[:, :], ACT.Copy).then_inc(act_evac, 1)
                        taps(48 + 6 * h, 6)
                    for t in range(T):
                        act.wait_ge(pe_done, done(f"E{t}"))
                        act.activation(dv[:, t, :], bank_of(f"E{t}")[:, 0:G], ACT.Copy).then_inc(act_evac, 1)
                        taps(60 + t, 1)
                    for name, dst in (("qT0", qT[:, 0]), ("qT1", qT[:, 1]), ("kT0", kT[:, :, 0:P]), ("kT1", kT[:, :, P:2 * P])):
                        act.wait_ge(pe_done, done(name))
                        src = bank_of(name)[:, :]
                        if name[0] == "k":
                            src = src.rearrange("p (t n) -> p t n", t=T)
                        act.activation(dst, src, ACT.Copy).then_inc(act_evac, 1)

                    def exponentials(b):
                        w = (b + 1) * P
                        act.wait_ge(s["exp_in"], b + 1)
                        for h in range(HEADS):
                            ins = act.activation(prob[:, h, 0:w], prob[:, h, 0:w], ACT.Exp,
                                                 bias=nmx[:, h:h + 1], scale=float(HD ** -0.5),
                                                 accum_out=sums[:, h:h + 1])
                        ins.then_inc(s["exp_done"], 1)

                    def values(b):
                        w = (b + 1) * P
                        for pair in range(2):
                            before = f"pv{b}0" if pair else (f"pv{b - 1}1" if b else None)
                            if before:
                                act.wait_ge(pe_done, done(before))
                            for h in (2 * pair, 2 * pair + 1):
                                act.wait_ge(pe_done, done(f"probT{b}{h}"))
                                act.activation(probT[:, h % 2, 0:w], bank_of(f"probT{b}{h}")[:, 0:w], ACT.Copy)\
                                   .then_inc(act_evac, 1)
                            act.wait_ge(pe_done, done(f"pv{b}{pair}"))
                            act.activation(mixT[:, pair, b * P:(b + 1) * P], bank_of(f"pv{b}{pair}")[:, 0:P],
                                           ACT.Copy).then_inc(act_evac, 1)

                    def squares(g):
                        act.activation(mix_sq_buf[g], mixT[:, 2 * g:2 * g + 2, :], ACT.Square)\
                           .then_inc(s["mix_sq"], 1)

                    def mixer_root(g):
                        act.wait_ge(pe_done, done(f"ms{g}"))
                        act.activation(rmix[:, g, :], bank_of(f"ms{g}")[:, 0:T], ACT.Sqrt, bias=c("eps"))\
                           .then_inc(act_evac, 1)

                    act.wait_ge(s["sgu_var"], 1)
                    act.activation(rdv, bag[:, :, 1], ACT.Sqrt, bias=c("eps")).then_inc(s["sgu_rstd"], 1)
                    exponentials(0)
                    values(0)
                    exponentials(1)
                    act.wait_ge(s["mix_ready"], 1)
                    act.wait_ge(s["conv_done"], 1)
                    squares(3)
                    for h in range(2):
                        act.wait_ge(s["centered"], h + 1)
                        act.activation(sq[:, h, :], acc[:, h, :], ACT.Square).then_inc(s["centered_sq"], 1)
                    values(1)
                    exponentials(2)
                    mixer_root(3)
                    for h in range(2):
                        act.wait_ge(pe_done, done(f"cvar{h}"))
                        act.activation(sq[:, h, :], bank_of(f"cvar{h}")[:, :], ACT.Sqrt, bias=c("eps"))\
                           .then_inc(act_evac, 1)
                    values(2)
                    act.wait_ge(s["conv_normed"], 1)
                    for h in range(2):
                        act.activation(acc[:, h, :], acc[:, h, :], ACT.Silu,
                                       bias=pcol[:, R_LB + h:R_LB + h + 1], scale=pcol[:, R_LG + h:R_LG + h + 1])\
                           .then_inc(s["swished"], 1)
                    exponentials(3)
                    act.wait_ge(s["mix_ready"], 2)
                    squares(2)
                    mixer_root(2)
                    values(3)
                    act.wait_ge(s["mix_ready"], 3)
                    squares(1)
                    act.wait_ge(act_evac, emptied("pv31"))
                    squares(0)
                    mixer_root(1)
                    mixer_root(0)
                    for t in range(T):
                        act.wait_ge(s["x_added"], t + 1)
                        root_mean_square(act, step, t).then_inc(s["rstd_done"], 1)
                    for k in range(K):
                        act.wait_ge(pe_done, done(f"m{k}"))
                        act.activation(h2T[:, k, :], bank_of(f"m{k}")[:, :], ACT.Identity,
                                       bias=pcol[:, SHIFT2 * K + k:SHIFT2 * K + k + 1], scale=scl[:, 1, k:k + 1])\
                           .then_inc(act_evac, 1)
                    act.wait_ge(pe_done, done("routeT"))
                    act.activation(lgT, bank_of("routeT")[0:NG + E, :], ACT.Copy).then_inc(act_evac, 1)
                    act.wait_ge(s["gexp_in"], 1)
                    act.activation(r4[:, 0], r4[:, 0], ACT.Exp)
                    act.activation(ediff, ediff, ACT.Exp).then_inc(s["gexp_out"], 1)

                    act.wait_ge(s["routed"], 1)
                    act.wait_ge(scattered, (l + 1) * (16 * 2 * T))
                    act.sem_inc(act_step, 1)

                    def load_rows(e, b):
                        row = act.value_load(starti[0:1, bass.ds(e, 1)], min_val=0, max_val=2 * S)
                        act.dma_start(xs[b], xs_dram[bass.ds(row, P), :]).then_inc(xs_in[b], 16)

                    def evacuate_rows(count, b):
                        act.wait_ge(s["xs_tr"], count + 1)
                        for k in range(K):
                            ins = act.activation(xT[b][:, k, :], XP[k // 4][:, (k % 4) * P:(k % 4 + 1) * P],
                                                 ACT.Identity, scale=scl[:, 1, k:k + 1],
                                                 bias=pcol[:, SHIFT2 * K + k:SHIFT2 * K + k + 1])
                        ins.then_inc(s["xt_ready"], 1)

                    def silu(e):
                        act.wait_ge(s["gate_mm"], e + 1)
                        act.activation(sgate, GB[:, :], ACT.Silu).then_inc(s["silu_done"], 1)

                    def evacuate_hidden(e):
                        act.wait_ge(s["hid_tr"], e + 1)
                        act.activation(hidT, HB[:, :].rearrange("p (k s) -> p k s", k=4), ACT.Copy)\
                           .then_inc(s["hidt_ready"], 1)

                    def write_rows(e, b):
                        row = act.value_load(starti[0:1, bass.ds(e, 1)], min_val=0, max_val=2 * S)
                        act.wait_ge(s["y_written"], (e + 2) * 16)
                        act.sem_inc(act_step, 1)
                        act.wait_ge(s["y_ready"], e + 2)
                        act.dma_start(ys_dram[bass.ds(row, P), :], ybuf[b]).then_inc(s["y_written"], 16)

                    act.sem_inc(s["y_written"], 32)
                    load_rows(0, 0)
                    load_rows(1, 1)
                    evacuate_rows(0, 0)
                    load_rows(2, 0)
                    silu(0)
                    evacuate_rows(1, 1)
                    load_rows(3, 1)

                    def step_expert(e, b, more=True, rows=True):
                        act.wait_ge(s["hid_ready"], e)
                        silu(e)
                        evacuate_hidden(e - 1)
                        if rows:
                            evacuate_rows(e + 1, 1 - b)
                        if more:
                            load_rows(e + 3, 1 - b)
                        if rows:
                            write_rows(e - 1, 1 - b)

                    with act.Fori(0, E // 2 - 2) as i:
                        step_expert(2 * i + 1, 1)
                        step_expert(2 * i + 2, 0)
                    step_expert(E - 3, 1, more=False)
                    step_expert(E - 2, 0, more=False)
                    step_expert(E - 1, 1, more=False, rows=False)
                    evacuate_hidden(E - 1)
                    write_rows(E - 2, 0)
                    write_rows(E - 1, 1)
                    act.wait_ge(s["y_written"], 16 * (E + 2))

                @block.gpsimd
                def _(pool):
                    step = stepper(pool, pool_step)

                    for h in range(2):
                        for w in range(1, TAPS):
                            m = h * (TAPS - 1) + w - 1
                            pool.wait_ge(s["tap_ready"], h * TAPS + w + 1)
                            pool.tensor_tensor(acc[:, h, :], acc[:, h, :], tap_buf[m % 2], ALU.add)\
                                .then_inc(s["tap_added"], 1)
                            pool.wait_ge(s["tap_added"], m + 1)
                    pool.sem_inc(s["conv_done"], 1)
                    pool.wait_ge(act_evac, emptied("pool1"))
                    a, b = wsum
                    step(pool.tensor_tensor(a[:, :, 1:], poolin[:, :, 1:], poolin[:, :, 0:15 + S], ALU.add))
                    step(pool.tensor_tensor(b[:, :, 3:], a[:, :, 3:], a[:, :, 1:14 + S], ALU.add))
                    step(pool.tensor_tensor(a[:, 1, 7:], b[:, 1, 7:], b[:, 1, 3:12 + S], ALU.add))
                    step(pool.tensor_tensor(b[64:, 1, 15:], a[64:, 1, 15:], a[64:, 1, 7:8 + S], ALU.add))
                    invw, invc = c("invw"), c("invc").rearrange("p (h n) -> p h n", h=2)
                    for lo, src in ((0, a), (64, b)):
                        r = slice(lo, lo + 64)
                        step(pool.tensor_tensor(a[r, :, 16:32], src[r, :, 16:32], invc[r, :, :], ALU.mult))
                        step(pool.tensor_tensor(a[r, :, 16:32], a[r, :, 16:32], poolin[r, :, 16:32], ALU.subtract))
                        for h in range(2):
                            step(pool.tensor_scalar(a[r, h, 32:], src[r, h, 32:], invw[r, h:h + 1], None, ALU.mult))
                            step(pool.tensor_tensor(a[r, h, 32:], a[r, h, 32:], poolin[r, h, 32:], ALU.subtract))
                    pool.sem_inc(s["pooled"], 1)
                    pool.wait_ge(s["rows_known"], 1)
                    for t in range(T):
                        for j in range(2):
                            pool.indirect_dma_start(
                                xs_dram, bass.IndirectOffsetOnAxis(ap=posu[:, j, t:t + 1], axis=0),
                                xn2[:, t, :], None, bounds_check=ROWS - 1, oob_is_err=True)\
                                .then_inc(scattered, 16)

                @block.vector
                def _(v):
                    step = stepper(v, dve_step)
                    def normalise_tile(dst, t):
                        step(v.reciprocal(rs[:, t:t + 1], rs[:, t:t + 1]))
                        v.tensor_scalar(dst[:, t, :], x[:, t, :], rs[:, t:t + 1], None, ALU.mult)\
                         .then_inc(s["xn_done"], 1)

                    for t in range(T):
                        normalise_tile(xn, t)
                    v.wait_ge(pe_done, done("params"))
                    step(v.tensor_copy(pcol[:, :], bank_of("params")[:, 0:NROW]))
                    v.sem_inc(dve_evac, 1)
                    v.wait_ge(pe_done, done("taps"))
                    v.tensor_copy(cwcol[:, :], bank_of("taps")[:, 0:2 * TAPS]).then_inc(dve_evac, 1)
                    for j, (m, r) in enumerate(((SCALE1, R_N1), (SCALE2, R_N2))):
                        ins = v.scalar_tensor_tensor(scl[:, j, :], pcol[:, m * K:(m + 1) * K], 1.0,
                                                     pcol[:, r:r + K], ALU.add, ALU.mult)
                    step(ins)
                    v.sem_inc(s["scl_ready"], 1)
                    for k in range(K // 2, K):
                        v.wait_ge(pe_done, done(f"h{k}"))
                        v.tensor_scalar(hT[:, k, :], bank_of(f"h{k}")[:, :], scl[:, 0, k:k + 1],
                                        pcol[:, SHIFT1 * K + k:SHIFT1 * K + k + 1], ALU.mult, ALU.add)\
                         .then_inc(dve_evac, 1)

                    def scale_w_out(n):
                        w = chunk_view(N_IN + n, 512)
                        v.wait_ge(*loaded(N_IN + n))
                        for k in range(K):
                            ins = v.scalar_tensor_tensor(w[:, k, :], w[:, k, :], pcol[:, R_ON + k:R_ON + k + 1],
                                                         g1b[:, n * 512:(n + 1) * 512], ALU.mult, ALU.mult)
                        step(ins)
                        v.sem_inc(s["wout_scaled"], 1)

                    v.wait_ge(s["gate1_in"], 16)
                    scale_w_out(0)

                    def rope(tiles, heads, half, table):
                        cos = cs[:, :, table:table + half].unsqueeze(2).to_broadcast([P, T, heads, half])
                        sin = sn[:, :, table:table + half].unsqueeze(2).to_broadcast([P, T, heads, half])
                        a, b = tiles[:, :, :, 0:half], tiles[:, :, :, half:2 * half]
                        tmp = [ropet[:, i, :, 0:heads, 0:half] for i in range(4)]
                        v.tensor_tensor(tmp[0], a, cos, ALU.mult)
                        v.tensor_tensor(tmp[1], b, sin, ALU.mult)
                        v.tensor_tensor(tmp[2], b, cos, ALU.mult)
                        step(v.tensor_tensor(tmp[3], a, sin, ALU.mult))
                        v.tensor_tensor(a, tmp[0], tmp[1], ALU.subtract)
                        return v.tensor_tensor(b, tmp[2], tmp[3], ALU.add)

                    v.wait_ge(act_evac, emptied("A3"))
                    step(rope(tokA[:, :, G:G + (IH + 1) * ID].rearrange("p t (h d) -> p t h d", d=ID),
                              IH + 1, IROT, ROT))
                    v.tensor_copy(ik4[:, :, :].rearrange("p t (r d) -> p t r d", r=4),
                                  tokA[:, :, G + IH * ID:G + (IH + 1) * ID].unsqueeze(2)
                                  .to_broadcast([P, T, 4, ID])).then_inc(s["idx_roped"], 1)
                    scale_w_out(1)
                    v.memset(convin[:, :, 0:TAPS - 1], 0.0)
                    for h in range(2):
                        v.wait_ge(act_evac, emptied(f"cg{h}"))
                        v.wait_ge(pe_done, done(f"ca{h}"))
                        step(v.tensor_tensor(convin[:, h, TAPS - 1:], bank_of(f"ca{h}")[:, :], sig[:, h, :],
                                             ALU.mult))
                        v.sem_inc(dve_evac, 1)
                        v.sem_inc(s["conv_in"], 1)
                    n = 0
                    for b in range(1, T):
                        w = (b + 1) * P
                        dst = score[:, SC[b]:SC[b] + w]
                        for h in range(IH):
                            iw = tokA[:, b, NA - IH + h:NA - IH + h + 1]
                            v.wait_ge(act_evac, emptied(f"idx{b}{h}"))
                            if h == 0:
                                ins = v.tensor_scalar(dst, relu[n % 2][:, 0:w], iw, None, ALU.mult)
                            else:
                                ins = v.scalar_tensor_tensor(dst, relu[n % 2][:, 0:w], iw, dst, ALU.mult, ALU.add)
                            n += 1
                            step(ins)
                            v.sem_inc(s["relu_free"], 1)
                        step(v.memset(score[0:CHUNK, SC[b] + w - CHUNK:SC[b] + w], NEG))

                    def select(b, rounds=range(TOPK // 8)):
                        w = (b + 1) * P
                        sc = score[:, SC[b]:SC[b] + w]
                        for n in rounds:
                            step(v.max(m8, sc))
                            step(v.match_replace(sc, m8, sc, GONE))
                        if rounds.stop == TOPK // 8:
                            step(v.tensor_scalar(sc, sc, float(0.5 * (NEG + GONE)), MASK, ALU.is_gt, ALU.mult))

                    select(1)
                    select(2)
                    v.wait_ge(act_evac, emptied("B3"))
                    for t in range(T):
                        for h in range(2 * HEADS):
                            src = tokB[:, t, h * HD:(h + 1) * HD]
                            n = (t * 8 + h) % 16
                            ins = v.tensor_tensor_reduce(sq_flat[:, n * HD:(n + 1) * HD], src, src, 1.0, 0.0,
                                                         ALU.mult, ALU.add, ssq[:, t * 8 + h:t * 8 + h + 1])
                        if t == 1:
                            step(ins)
                    ins.then_inc(s["qk_ss"], 1)
                    select(3, range(0, 9))
                    v.wait_ge(s["qk_rstd"], 1)
                    step(v.reciprocal(rsq, rsq))
                    v.wait_ge(s["norms_in"], 32)
                    qk = tokB[:, :, :].rearrange("p t (h d) -> p t h d", d=HD)
                    step(v.tensor_tensor(qk, qk, rsq.rearrange("p (t h) -> p t h", t=T).unsqueeze(3)
                                         .to_broadcast([P, T, 2 * HEADS, HD]), ALU.mult))
                    for j in range(2):
                        for t in range(T):
                            part = qk[:, t, j * HEADS:(j + 1) * HEADS, :]
                            ins = v.tensor_tensor(part, part, qkn[:, j, :].unsqueeze(1)
                                                  .to_broadcast([P, HEADS, HD]), ALU.mult)
                    step(ins)
                    rope(qk, 2 * HEADS, ROT, 0).then_inc(s["qk_roped"], 1)
                    select(3, range(9, TOPK // 8))
                    v.wait_ge(act_evac, emptied("E3"))
                    for t in range(T):
                        step(v.bn_stats(bst[:, t, :], dv[:, t, :]))
                    for t in range(T):
                        ins = v.bn_aggr(bag[:, t, :], bst[:, t, :])
                    ins.then_inc(s["sgu_var"], 1)

                    def logits(b):
                        w = (b + 1) * P
                        bias = score[:, SC[b]:SC[b] + w] if b else c("mask0")
                        v.wait_ge(pe_done, done(f"probT{b - 1}3" if b else "E3"))
                        for h in range(HEADS):
                            v.wait_ge(pe_done, done(f"logit{b}{h}"))
                            ins = v.tensor_tensor_reduce(prob[:, h, 0:w], bank_of(f"logit{b}{h}")[:, 0:w], bias,
                                                         1.0, NEG, ALU.add, ALU.max, mx[:, h:h + 1])
                            if h < HEADS - 1:
                                ins.then_inc(dve_evac, 1)
                        step(ins)
                        v.sem_inc(dve_evac, 1)
                        v.tensor_scalar(nmx, mx, -float(HD ** -0.5), None, ALU.mult).then_inc(s["exp_in"], 1)

                    def probabilities(b):
                        w = (b + 1) * P
                        v.wait_ge(s["exp_done"], b + 1)
                        step(v.reciprocal(rsum, sums))
                        for h in range(HEADS):
                            ins = v.tensor_scalar(prob[:, h, 0:w], prob[:, h, 0:w], rsum[:, h:h + 1], None, ALU.mult)
                        ins.then_inc(s["prob_ready"], 1)

                    def mixer_reciprocal(g):
                        v.wait_ge(act_evac, emptied(f"ms{g}"))
                        step(v.reciprocal(rmix[:, g, :], rmix[:, g, :]))

                    def add_out(g, t, n):
                        part = x[:, t, n * 512:(n + 1) * 512]
                        v.wait_ge(pe_done, done(f"out{g}{t}{n}"))
                        step(v.scalar_tensor_tensor(part, bank_of(f"out{g}{t}{n}")[:, :], rmix[:, g, t:t + 1], part,
                                                    ALU.mult, ALU.add))
                        v.sem_inc(dve_evac, 1)

                    def normalise_conv():
                        v.wait_ge(act_evac, emptied("cvar1"))
                        step(v.reciprocal(sq[:, :, :], sq[:, :, :]))
                        step(v.tensor_tensor(acc[:, :, :], acc[:, :, :], sq[:, :, :], ALU.mult))
                        v.sem_inc(s["conv_normed"], 1)

                    def conv_outputs():
                        v.wait_ge(pe_done, done("pw1"))
                        for co in range(2):
                            ins = v.tensor_scalar(mixT[:, 2 + co, :], bank_of(f"pw{co}")[:, :],
                                                  pcol[:, R_PB + co:R_PB + co + 1], None, ALU.add)
                            if co == 0:
                                ins.then_inc(dve_evac, 1)
                        step(ins)
                        v.sem_inc(dve_evac, 1)
                        v.sem_inc(s["mix_ready"], 1)

                    logits(0)
                    v.wait_ge(s["sgu_rstd"], 1)
                    step(v.reciprocal(rdv, rdv))
                    v.wait_ge(s["sgu_in"], 16 * 7)
                    for t in range(T):
                        ins = v.tensor_scalar(dv[:, t, :], dv[:, t, :], bag[:, t, 0:1], rdv[:, t:t + 1],
                                              ALU.subtract, ALU.mult)
                    step(ins)
                    probabilities(0)
                    step(v.tensor_tensor(dv, dv, sgn[:, 0, :].unsqueeze(1).to_broadcast([P, T, G]), ALU.mult))
                    v.tensor_tensor(dv, dv, sgn[:, 1, :].unsqueeze(1).to_broadcast([P, T, G]), ALU.add)\
                        .then_inc(s["sgu_normed"], 1)
                    v.wait_ge(pe_done, done("sgw"))
                    v.tensor_tensor(sgwT[:, :, :], bank_of("sgw")[:, :].rearrange("p (h t) -> p h t", h=SGU_H),
                                    c("upto").unsqueeze(1).to_broadcast([P, SGU_H, P]), ALU.mult)\
                        .then_inc(dve_evac, 1)
                    v.wait_ge(act_evac, emptied("u1"))
                    for p in range(2):
                        v.wait_ge(pe_done, done(f"sgu{p}"))
                        mixed = sq[:, p, :]
                        step(v.tensor_tensor(mixed.rearrange("p (n t) -> p n t", n=T),
                                             bank_of(f"sgu{p}")[:, :].rearrange("p (n t) -> p n t", n=T),
                                             sgb[:, p, :].unsqueeze(1).to_broadcast([P, T, P]), ALU.add))
                        v.sem_inc(dve_evac, 1)
                        ins = v.tensor_tensor(uT[:, p, :], mixed, uT[:, p, :], ALU.mult)
                    step(ins)
                    v.sem_inc(s["mix_ready"], 1)
                    logits(1)
                    for h in range(2):
                        v.wait_ge(pe_done, done(f"cmean{h}"))
                        step(v.tensor_tensor(acc[:, h, :], acc[:, h, :], bank_of(f"cmean{h}")[:, :], ALU.subtract))
                        v.sem_inc(dve_evac, 1)
                        v.sem_inc(s["centered"], 1)
                    probabilities(1)
                    logits(2)
                    mixer_reciprocal(3)
                    for t, n in TN[:4]:
                        add_out(3, t, n)
                    probabilities(2)
                    normalise_conv()
                    logits(3)
                    for h in range(2):
                        v.wait_ge(pe_done, done(f"pl{h}"))
                        ins = v.tensor_scalar(mixT[:, 4 + h, :], bank_of(f"pl{h}")[:, :],
                                              pcol[:, R_QB + h:R_QB + h + 1], pcol[:, R_QS + h:R_QS + h + 1],
                                              ALU.add, ALU.mult)
                        if h == 0:
                            ins.then_inc(dve_evac, 1)
                    step(ins)
                    v.sem_inc(dve_evac, 1)
                    v.sem_inc(s["mix_ready"], 1)
                    for t, n in TN[4:]:
                        add_out(3, t, n)
                    conv_outputs()
                    probabilities(3)
                    mixer_reciprocal(2)
                    for t, n in TN:
                        add_out(2, t, n)
                    mixer_reciprocal(1)
                    for t, n in TN:
                        add_out(1, t, n)
                    mixer_reciprocal(0)
                    for t in range(T):
                        add_out(0, t, 0)
                        add_out(0, t, 1)
                        v.sem_inc(s["x_added"], 1)
                        if t:
                            v.wait_ge(s["rstd_done"], t)
                            normalise_tile(xn2, t - 1)
                    v.wait_ge(s["rstd_done"], T)
                    normalise_tile(xn2, T - 1)

                    v.wait_ge(s["router_in"], 64)
                    v.wait_ge(pe_done, done("route"))
                    step(v.tensor_tensor(lg[:, :, :], bank_of("route")[:, 0:T * (NG + E)]
                                         .rearrange("p (t n) -> p t n", t=T),
                                         rb[:, :].unsqueeze(1).to_broadcast([P, T, NG + E]), ALU.add))
                    v.sem_inc(dve_evac, 1)
                    grp = lg[:, :, 0:NG]
                    io4 = c("iota")[:, 0:NG].unsqueeze(1).to_broadcast([P, T, NG])
                    step(v.tensor_reduce(gmax, grp, AX.X, ALU.max))
                    gm = gmax.unsqueeze(2).to_broadcast([P, T, NG])
                    v.tensor_tensor(r4[:, 0], grp, gm, ALU.subtract)
                    step(v.tensor_tensor(r4[:, 1], grp, gm, ALU.is_lt))
                    step(v.scalar_tensor_tensor(r4[:, 1], r4[:, 1], float(NG), io4, ALU.mult, ALU.add))
                    step(v.tensor_reduce(gidx, r4[:, 1], AX.X, ALU.min))
                    step(v.tensor_tensor(r4[:, 2], io4, gidx.unsqueeze(2).to_broadcast([P, T, NG]), ALU.is_equal))
                    step(v.tensor_scalar(r4[:, 2], r4[:, 2], 1.0, -MASK, ALU.subtract, ALU.mult))
                    for t in range(T):
                        ins = v.tensor_tensor(el[:, t, :].rearrange("p (g e) -> p g e", g=NG),
                                              lg[:, t, NG:].rearrange("p (g e) -> p g e", g=NG),
                                              r4[:, 2, t, :].unsqueeze(2).to_broadcast([P, NG, EPG]), ALU.add)
                    step(ins)
                    for t in range(T):
                        ins = v.max(top8[:, t, :], el[:, t, :])
                    step(ins)
                    for t in range(T):
                        v.max_index(topi[:, t, :], top8[:, t, :], el[:, t, :])
                    step(v.tensor_tensor(ediff, top8[:, :, 1], top8[:, :, 0], ALU.subtract))
                    v.sem_inc(s["gexp_in"], 1)
                    step(v.tensor_copy(topf, topi[:, :, :]))
                    io = c("iota").unsqueeze(1).to_broadcast([P, T, E])
                    for j in range(2):
                        ins = v.tensor_tensor(oh[:, j], topf[:, :, j:j + 1].to_broadcast([P, T, E]), io, ALU.is_equal)
                    step(ins)
                    v.tensor_tensor(oh[:, 2], oh[:, 0], oh[:, 1], ALU.add).then_inc(s["oh_ready"], 1)
                    v.wait_ge(s["gexp_out"], 1)
                    step(v.reduce_sum(psel, r4[:, 0], AX.X))
                    step(v.tensor_scalar(rsum, ediff, 1.0, None, ALU.add))
                    step(v.tensor_tensor(psel, psel, rsum, ALU.mult))
                    step(v.reciprocal(gates[:, 0, :], psel))
                    v.tensor_tensor(gates[:, 1, :], gates[:, 0, :], ediff, ALU.mult)
                    v.wait_ge(pe_done, done("rank"))
                    own, inc = cnt[:, 0:3, :], [cnt[:, 3:6, :], cnt[:, 6:9, :]]
                    v.tensor_copy(rank[:, :, :], bank_of("rank")[:, 0:T * E].rearrange("p (t e) -> p t e", t=T))
                    step(v.tensor_copy(tiles[:, :, :], bank_of("rank")[:, T * E:2 * T * E]
                                       .rearrange("p (t e) -> p t e", t=T)))
                    for t in range(1, T):
                        step(v.tensor_tensor(tiles[:, t, :], tiles[:, t, :], tiles[:, t - 1, :], ALU.add))
                    v.tensor_tensor(rank[:, 1:, :], rank[:, 1:, :], tiles[:, 0:T - 1, :], ALU.add)
                    total = tiles[:, T - 1, :]
                    step(v.tensor_scalar(own[:, 0, :], total, float(P), None, ALU.min))
                    step(v.tensor_tensor(own[:, 1, :], total, own[:, 0, :], ALU.subtract))
                    v.sem_inc(dve_evac, 1)
                    step(v.tensor_scalar(own[:, 2, :], own[:, 1, :], 0.0, None, ALU.is_gt))
                    for n in range(1, S // P - 1):
                        step(v.scalar_tensor_tensor(own[:, 2, :], own[:, 1, :], float(n * P), own[:, 2, :],
                                                    ALU.is_gt, ALU.add))
                    src, m = own, 0
                    for d in (1, 2, 4, 8, 16):
                        dst = inc[m % 2]
                        v.tensor_copy(dst[:, :, 0:d], src[:, :, 0:d])
                        step(v.tensor_tensor(dst[:, :, d:], src[:, :, d:], src[:, :, 0:E - d], ALU.add))
                        src, m = dst, m + 1
                    step(v.tensor_tensor(exc[:, 0:3, :], src, own, ALU.subtract))
                    start0, start1, nbx, far = (exc[:, i, :] for i in range(4))
                    step(v.tensor_scalar(start1, start1, src[:, 0, E - 1:E], None, ALU.add))
                    step(v.scalar_tensor_tensor(far, start1, -float(P), start0, ALU.add, ALU.subtract))
                    every = [P, T, E]
                    v.scalar_tensor_tensor(rtmp[:, :, :], rank[:, :, :], float(P),
                                           far.unsqueeze(1).to_broadcast(every), ALU.is_ge, ALU.mult)
                    step(v.tensor_tensor(rank[:, :, :], rank[:, :, :], start0.unsqueeze(1).to_broadcast(every),
                                         ALU.add))
                    step(v.tensor_tensor(rank[:, :, :], rank[:, :, :], rtmp[:, :, :], ALU.add))
                    for j in range(2):
                        step(v.tensor_tensor(oh[:, j], oh[:, j], rank[:, :, :], ALU.mult))
                        step(v.tensor_reduce(posr[:, j, :], oh[:, j], AX.X, ALU.add))
                    v.tensor_copy(posu[:, :, :], posr).then_inc(s["rows_known"], 1)
                    one, many = slice(0, 1), [1, OVER_BLOCKS, E]
                    rel, inside, row = (ovm[one, i] for i in range(3))
                    step(v.tensor_tensor(rel, c("blk")[one].unsqueeze(2).to_broadcast(many),
                                         nbx[one].unsqueeze(1).to_broadcast(many), ALU.subtract))
                    v.tensor_tensor(inside, rel, own[one, 2].unsqueeze(1).to_broadcast(many), ALU.is_lt)
                    step(v.scalar_tensor_tensor(row, rel, float(P), start1[one].unsqueeze(1).to_broadcast(many),
                                                ALU.mult, ALU.add))
                    step(v.scalar_tensor_tensor(inside, rel, 0.0, inside, ALU.is_ge, ALU.mult))
                    v.tensor_tensor(row, row, inside, ALU.mult)
                    step(v.tensor_tensor(inside, inside, c("iota")[one].unsqueeze(1).to_broadcast(many), ALU.mult))
                    v.tensor_reduce(ovf[one, 0], inside, AX.X, ALU.add)
                    step(v.tensor_reduce(ovf[one, 1], row, AX.X, ALU.add))
                    v.tensor_copy(ovi[one, 0:2 * OVER_BLOCKS], ovf[one].rearrange("p a b -> p (a b)"))
                    v.tensor_copy(ovi[one, 2 * OVER_BLOCKS:2 * OVER_BLOCKS + 1], src[one, 2, E - 1:E])
                    v.tensor_copy(starti[:, :], start0[one]).then_inc(s["routed"], 1)

                    v.sem_inc(s["y_ready"], 1)

                    def multiply(e):
                        v.wait_ge(s["silu_done"], e + 1)
                        v.wait_ge(s["up_mm"], e + 1)
                        v.tensor_tensor(hid, UB[:, :], sgate, ALU.mult).then_inc(s["hid_ready"], 1)

                    def evacuate_y(e, b):
                        v.wait_ge(s["y_written"], (e + 1) * 16)
                        v.wait_ge(s["down_mm"], e + 1)
                        v.tensor_tensor(ybuf[b][:, 0:512], YB[0][:, :], g2b[:, 0:512], ALU.mult)
                        v.tensor_tensor(ybuf[b][:, 512:D], YB[1][:, :], g2b[:, 512:D], ALU.mult)\
                         .then_inc(s["y_ready"], 1)

                    multiply(0)
                    v.wait_ge(s["gate2_in"], 16)
                    with v.Fori(0, E // 2 - 1) as i:
                        for b, e in ((1, 2 * i + 1), (0, 2 * i + 2)):
                            multiply(e)
                            evacuate_y(e - 1, 1 - b)
                    multiply(E - 1)
                    evacuate_y(E - 2, 0)
                    evacuate_y(E - 1, 1)

                @block.tensor
                def _(pe):
                    def turn_tokens(prefix, tokens, tiles=range(K)):
                        for k in tiles:
                            await_bank(pe, f"{prefix}{k}")
                            for t in range(T):
                                mm = pe.transpose(bank_of(f"{prefix}{k}")[:, t * P:(t + 1) * P],
                                                  tokens[:, t, k * P:(k + 1) * P], ident)
                            mm.then_inc(pe_done, 1)

                    def by_token(names, n, width):
                        w = chunk_view(n, width)
                        pe.wait_ge(*loaded(n))
                        for t in range(T):
                            await_bank(pe, f"{names}{t}")
                            for k in range(K):
                                mm = pe.matmul(bank_of(f"{names}{t}")[:, 0:width], hT[:, k, t * P:(t + 1) * P],
                                               w[:, k, :], start=(k == 0), stop=(k == K - 1))
                            mm.then_inc(pe_done, 1)

                    def by_channel(name, n, at):
                        w = chunk_view(n, 512)
                        await_bank(pe, name)
                        for k in range(K):
                            mm = pe.matmul(bank_of(name)[:, :], w[:, k, at:at + P], hT[:, k, :],
                                           start=(k == 0), stop=(k == K - 1))
                        mm.then_inc(pe_done, 1)

                    pe.wait_ge(s["xn_done"], T)
                    turn_tokens("h", xn, range(K // 2))
                    pe.wait_ge(s["rows_in"], 16 * 10)
                    pe.transpose(bank_of("params")[:, 0:NROW], prow[:, :], ident[0:NROW, 0:NROW]).then_inc(pe_done, 1)
                    pe.wait_ge(s["taps_in"], 16)
                    pe.transpose(bank_of("taps")[:, 0:2 * TAPS], cwrow[:, :], ident[0:2 * TAPS, 0:2 * TAPS])\
                        .then_inc(pe_done, 1)
                    turn_tokens("h", xn, range(K // 2, K))
                    pe.wait_ge(act_evac, emptied(f"h{K // 2 - 1}"))
                    pe.wait_ge(dve_evac, emptied(f"h{K - 1}"))
                    by_token("A", 0, NA)
                    pe.wait_ge(*loaded(1))
                    for h in range(2):
                        by_channel(f"cg{h}", 1, G + h * P)
                        by_channel(f"ca{h}", 1, h * P)
                    pe.wait_ge(s["idx_roped"], 1)
                    for name, src in (("iqT", tokA[:, :, G:G + P]), ("ikT", ik4[:, :, :])):
                        await_bank(pe, name)
                        for t in range(T):
                            mm = pe.transpose(bank_of(name)[:, t * P:(t + 1) * P], src[:, t, :], ident)
                        mm.then_inc(pe_done, 1)
                    pe.wait_ge(act_evac, emptied("ikT"))
                    for b in range(1, T):
                        for h in range(IH):
                            name, r, w = f"idx{b}{h}", slice(h * ID, (h + 1) * ID), (b + 1) * P
                            await_bank(pe, name)
                            pe.matmul(bank_of(name)[:, 0:w], iqT[r, b * P:(b + 1) * P], ikT[r, 0:w],
                                      start=True, stop=True).then_inc(pe_done, 1)
                    by_token("B", 2, 512)
                    pe.wait_ge(*loaded(3))
                    for h in range(2):
                        by_channel(f"pool{h}", 3, h * P)
                    for h in range(2):
                        by_channel(f"u{h}", 3, G + h * P)
                    by_token("E", 4, G)
                    pe.wait_ge(s["qk_roped"], 1)
                    for j, head in ((0, "qT"), (1, "kT")):
                        for pair in range(2):
                            name, a = f"{head}{pair}", (2 * j + pair) * P
                            await_bank(pe, name)
                            for t in range(T):
                                mm = pe.transpose(bank_of(name)[:, t * P:(t + 1) * P], tokB[:, t, a:a + P], ident)
                            mm.then_inc(pe_done, 1)

                    def logits(b):
                        w = (b + 1) * P
                        if b == 0:
                            pe.wait_ge(act_evac, emptied("kT1"))
                        for h in range(HEADS):
                            name, r = f"logit{b}{h}", slice(64 * (h % 2), 64 * (h % 2) + 64)
                            await_bank(pe, name)
                            pe.matmul(bank_of(name)[:, 0:w].rearrange("p (t n) -> p t n", n=P),
                                      qT[r, h // 2, b * P:(b + 1) * P],
                                      kT[r, 0:b + 1, (h // 2) * P:(h // 2 + 1) * P],
                                      start=True, stop=True).then_inc(pe_done, 1)

                    def keep_warm(name, n):
                        await_bank(pe, name)
                        for _ in range(n):
                            pe.matmul(bank_of(name)[:, 0:P], ident, ident, start=True, stop=True)

                    def values(b):
                        keep_warm(f"probT{b}0", WARM[b])
                        pe.wait_ge(s["prob_ready"], b + 1)
                        for pair in range(2):
                            for h in (2 * pair, 2 * pair + 1):
                                name = f"probT{b}{h}"
                                await_bank(pe, name)
                                for kt in range(b + 1):
                                    mm = pe.transpose(bank_of(name)[:, kt * P:(kt + 1) * P],
                                                      prob[:, h, kt * P:(kt + 1) * P], ident)
                                mm.then_inc(pe_done, 1)
                            name = f"pv{b}{pair}"
                            await_bank(pe, name)
                            pe.wait_ge(act_evac, emptied(f"probT{b}{2 * pair + 1}"))
                            for h in (2 * pair, 2 * pair + 1):
                                o = 64 * (h % 2)
                                for kt in range(b + 1):
                                    mm = pe.matmul(bank_of(name)[o:o + 64, 0:P], tokA[:, kt, h * HD:(h + 1) * HD],
                                                   probT[:, h % 2, kt * P:(kt + 1) * P],
                                                   start=(kt == 0), stop=(kt == b))
                            mm.then_inc(pe_done, 1)

                    def mean_square(g, count):
                        pe.wait_ge(s["mix_sq"], count)
                        await_bank(pe, f"ms{g}")
                        for t in range(T):
                            for i in range(2):
                                mm = pe.matmul(bank_of(f"ms{g}")[:, t:t + 1], mix_sq_buf[g][:, i, t * P:(t + 1) * P],
                                               c("mean256")[:, 0:1], start=(i == 0), stop=(i == 1))
                        mm.then_inc(pe_done, 1)

                    def project_out(g, tn):
                        for t, n in tn:
                            name = f"out{g}{t}{n}"
                            w = chunk_view(N_IN + n, 512)
                            await_bank(pe, name)
                            for i in range(2):
                                mm = pe.matmul(bank_of(name)[:, :], mixT[:, 2 * g + i, t * P:(t + 1) * P],
                                               w[:, 2 * g + i, :], start=(i == 0), stop=(i == 1))
                            mm.then_inc(pe_done, 1)

                    logits(0)
                    pe.wait_ge(s["sgu_in"], 16 * 7)
                    await_bank(pe, "sgw")
                    for h in range(SGU_H):
                        mm = pe.transpose(bank_of("sgw")[:, h * P:(h + 1) * P], sgw[:, h, :], ident)
                    mm.then_inc(pe_done, 1)
                    values(0)
                    pe.wait_ge(s["sgu_normed"], 1)
                    pe.wait_ge(dve_evac, emptied("sgw"))
                    for pair in range(2):
                        name = f"sgu{pair}"
                        await_bank(pe, name)
                        for n in range(T):
                            for h in (2 * pair, 2 * pair + 1):
                                o = 64 * (h % 2)
                                mm = pe.matmul(bank_of(name)[o:o + 64, n * P:(n + 1) * P],
                                               dv[:, n, h * 64:(h + 1) * 64], sgwT[:, h, :], start=True, stop=True)
                        mm.then_inc(pe_done, 1)
                    logits(1)
                    pe.wait_ge(s["conv_done"], 1)
                    for h in range(2):
                        await_bank(pe, f"cmean{h}")
                        pe.matmul(bank_of(f"cmean{h}")[:, :], c("mean64"), acc[:, h, :], start=True, stop=True)\
                            .then_inc(pe_done, 1)
                    values(1)
                    logits(2)
                    mean_square(3, 1)
                    for h in range(2):
                        pe.wait_ge(s["centered_sq"], h + 1)
                        await_bank(pe, f"cvar{h}")
                        pe.matmul(bank_of(f"cvar{h}")[:, :], c("mean64"), sq[:, h, :], start=True, stop=True)\
                            .then_inc(pe_done, 1)
                    pe.wait_ge(s["wout_scaled"], N_OUT)
                    project_out(3, TN[:4])
                    values(2)
                    logits(3)
                    pe.wait_ge(s["pooled"], 1)
                    pe.wait_ge(s["pw_in"], 16 * 5)
                    for h in range(2):
                        await_bank(pe, f"pl{h}")
                        pe.matmul(bank_of(f"pl{h}")[:, :], plw[:, h, :], wsum[0][:, h, 16:], start=True, stop=True)\
                            .then_inc(pe_done, 1)
                    project_out(3, TN[4:])
                    pe.wait_ge(s["swished"], 2)
                    for co in range(2):
                        await_bank(pe, f"pw{co}")
                        for ci in range(2):
                            mm = pe.matmul(bank_of(f"pw{co}")[:, :], pww[:, ci, co * P:(co + 1) * P], acc[:, ci, :],
                                           start=(ci == 0), stop=(ci == 1))
                        mm.then_inc(pe_done, 1)
                    mean_square(2, 2)
                    values(3)
                    project_out(2, TN)
                    mean_square(1, 3)
                    mean_square(0, 4)
                    project_out(1, TN)
                    project_out(0, TN)
                    pe.wait_ge(s["xn_done"], 2 * T)
                    turn_tokens("m", xn2)
                    pe.wait_ge(act_evac, emptied(f"m{K - 1}"))
                    pe.wait_ge(s["router_in"], 64)
                    await_bank(pe, "routeT")
                    for k in range(K):
                        mm = pe.matmul(bank_of("routeT")[0:NG + E, :], wr[:, k, :], h2T[:, k, :],
                                       start=(k == 0), stop=(k == K - 1))
                    mm.then_inc(pe_done, 1)
                    await_bank(pe, "route")
                    pe.wait_ge(act_evac, emptied("routeT"))
                    for t in range(T):
                        mm = pe.transpose(bank_of("route")[:, t * (NG + E):(t + 1) * (NG + E)],
                                          lgT[:, t * P:(t + 1) * P], ident[0:NG + E, 0:NG + E])
                    mm.then_inc(pe_done, 1)
                    pe.wait_ge(s["oh_ready"], 1)
                    await_bank(pe, "rank")
                    marks = oh[:, 2].rearrange("p t e -> p (t e)")
                    pe.matmul(bank_of("rank")[:, 0:T * E], c("before"), marks, start=True, stop=True)
                    mm = pe.matmul(bank_of("rank")[:, T * E:2 * T * E], c("ones"), marks, start=True, stop=True)
                    mm.then_inc(pe_done, 1)

                    def expert_matrix(j, k):
                        return ring[:, j % RING, :].rearrange("p (k n) -> p k n", k=k)

                    def turn_rows(count, b, times):
                        pe.wait_ge(xs_in[b], 16 * times)
                        for k in range(K):
                            mm = pe.transpose(XP[k // 4][:, (k % 4) * P:(k % 4 + 1) * P],
                                              xs[b][:, k * P:(k + 1) * P], ident)
                        mm.then_inc(s["xs_tr"], 1)

                    def first_product(n, fill, out_bank, b, signal):
                        w = expert_matrix(n, K)
                        pe.wait_ge(slot[n % RING], 16 * fill)
                        for k in range(K):
                            mm = pe.matmul(out_bank[:, :], xT[b][:, k, :], w[:, k, :],
                                           start=(k == 0), stop=(k == K - 1))
                        mm.then_inc(signal, 1)

                    def turn_hidden(e):
                        pe.wait_ge(s["hid_ready"], e + 1)
                        for k in range(4):
                            mm = pe.transpose(HB[:, k * P:(k + 1) * P], hid[:, k * P:(k + 1) * P], ident)
                        mm.then_inc(s["hid_tr"], 1)

                    def down(e, n, fill):
                        w = expert_matrix(n, 4)
                        pe.wait_ge(slot[n % RING], 16 * fill)
                        pe.wait_ge(s["hidt_ready"], e + 1)
                        pe.wait_ge(s["y_ready"], e + 1)
                        for half in range(2):
                            for k in range(4):
                                mm = pe.matmul(YB[half][:, :], hidT[:, k, :], w[:, k, half * 512:(half + 1) * 512],
                                               start=(k == 0), stop=(k == 3))
                        mm.then_inc(s["down_mm"], 1)

                    pe.wait_ge(s["routed"], 1)
                    turn_rows(0, 0, 1)
                    pe.wait_ge(s["xt_ready"], 1)
                    first_product(N_PRE, (N_PRE // RING) + 1, GB, 0, s["gate_mm"])
                    first_product(N_PRE + 1, (N_PRE + 1) // RING + 1, UB, 0, s["up_mm"])
                    turn_rows(1, 1, 1)

                    def step_expert(e, b, n, fill, times, rows=True):
                        pe.wait_ge(s["xt_ready"], e + 1)
                        pe.wait_ge(s["silu_done"], e)
                        first_product(n, fill, GB, b, s["gate_mm"])
                        turn_hidden(e - 1)
                        first_product(n + 1, fill, UB, b, s["up_mm"])
                        if rows:
                            turn_rows(e + 1, 1 - b, times)
                        down(e - 1, n + 2, fill)

                    with pe.Fori(0, E // 2 - 1) as i:
                        step_expert(2 * i + 1, 1, 9, i + 2, i + 2)
                        step_expert(2 * i + 2, 0, 12, i + 3, i + 2)
                    step_expert(E - 1, 1, 9, E // 2 + 1, 0, rows=False)
                    turn_hidden(E - 1)
                    n = N_CHUNKS - 1
                    down(E - 1, n, n // RING + 1)

            clear_semaphores()

            n_over = nc.values_load(ovi[0:1, 2 * OVER_BLOCKS:2 * OVER_BLOCKS + 1], min_val=0, max_val=OVER_BLOCKS)
            with nc.If(n_over > 0):
                with nc.Fori(0, OVER_BLOCKS) as i:
                    with nc.If(n_over > i):
                        with nc.Block() as block:
                            @block.sync
                            def _(sp):
                                e = sp.value_load(ovi[0:1, bass.ds(i, 1)], min_val=0, max_val=E - 1)
                                row = sp.value_load(ovi[0:1, bass.ds(i + OVER_BLOCKS, 1)], min_val=0, max_val=ROWS - P)
                                for j, (src, k) in enumerate(((wg_v, K), (wu_v, K), (wd_v, 4))):
                                    sp.dma_start(ring[:, j, :].rearrange("p (k n) -> p k n", k=k),
                                                 src[l, bass.ds(e, 1)].rearrange("e p k n -> (e p) k n"))\
                                        .then_inc(slot[j], 16)
                                sp.dma_start(xs[0], xs_dram[bass.ds(row, P), :]).then_inc(xs_in[0], 16)
                                sp.wait_ge(s["y_ready"], 1)
                                sp.dma_start(ys_dram[bass.ds(row, P), :], ybuf[0]).then_inc(s["y_written"], 16)
                                sp.wait_ge(s["y_written"], 16)

                            @block.gpsimd
                            def _(pool):
                                pool.memset(small[:, 228:229], 0.0)

                            @block.scalar
                            def _(act):
                                act.wait_ge(s["xs_tr"], 1)
                                for k in range(K):
                                    ins = act.activation(xT[0][:, k, :], XP[k // 4][:, (k % 4) * P:(k % 4 + 1) * P],
                                                         ACT.Identity, scale=scl[:, 1, k:k + 1],
                                                         bias=pcol[:, SHIFT2 * K + k:SHIFT2 * K + k + 1])
                                ins.then_inc(s["xt_ready"], 1)
                                act.wait_ge(s["gate_mm"], 1)
                                act.activation(sgate, GB[:, :], ACT.Silu).then_inc(s["silu_done"], 1)
                                act.wait_ge(s["hid_tr"], 1)
                                act.activation(hidT, HB[:, :].rearrange("p (k s) -> p k s", k=4), ACT.Copy)\
                                   .then_inc(s["hidt_ready"], 1)

                            @block.vector
                            def _(v):
                                v.wait_ge(s["silu_done"], 1)
                                v.wait_ge(s["up_mm"], 1)
                                v.tensor_tensor(hid, UB[:, :], sgate, ALU.mult).then_inc(s["hid_ready"], 1)
                                v.wait_ge(s["down_mm"], 1)
                                v.tensor_tensor(ybuf[0][:, 0:512], YB[0][:, :], g2b[:, 0:512], ALU.mult)
                                v.tensor_tensor(ybuf[0][:, 512:D], YB[1][:, :], g2b[:, 512:D], ALU.mult)\
                                 .then_inc(s["y_ready"], 1)

                            @block.tensor
                            def _(pe):
                                pe.wait_ge(xs_in[0], 16)
                                for k in range(K):
                                    mm = pe.transpose(XP[k // 4][:, (k % 4) * P:(k % 4 + 1) * P],
                                                      xs[0][:, k * P:(k + 1) * P], ident)
                                mm.then_inc(s["xs_tr"], 1)
                                pe.wait_ge(s["xt_ready"], 1)
                                for j, (dst, signal) in enumerate(((GB, s["gate_mm"]), (UB, s["up_mm"]))):
                                    w = ring[:, j, :].rearrange("p (k n) -> p k n", k=K)
                                    pe.wait_ge(slot[j], 16)
                                    for k in range(K):
                                        mm = pe.matmul(dst[:, :], xT[0][:, k, :], w[:, k, :],
                                                       start=(k == 0), stop=(k == K - 1))
                                    mm.then_inc(signal, 1)
                                pe.wait_ge(s["hid_ready"], 1)
                                for k in range(4):
                                    mm = pe.transpose(HB[:, k * P:(k + 1) * P], hid[:, k * P:(k + 1) * P], ident)
                                mm.then_inc(s["hid_tr"], 1)
                                pe.wait_ge(s["hidt_ready"], 1)
                                pe.wait_ge(slot[2], 16)
                                w = ring[:, 2, :].rearrange("p (k n) -> p k n", k=4)
                                for half in range(2):
                                    for k in range(4):
                                        mm = pe.matmul(YB[half][:, :], hidT[:, k, :],
                                                       w[:, k, half * 512:(half + 1) * 512],
                                                       start=(k == 0), stop=(k == 3))
                                mm.then_inc(s["down_mm"], 1)
                        clear_semaphores()

            with nc.Block() as block:
                @block.gpsimd
                def _(pool):
                    for t in range(T):
                        for j in range(2):
                            pool.indirect_dma_start(
                                got[t][j], None, ys_dram,
                                bass.IndirectOffsetOnAxis(ap=posu[:, j, t:t + 1], axis=0),
                                bounds_check=ROWS - 1, oob_is_err=True).then_inc(got_in[t], 16)

                @block.vector
                def _(v):
                    step = stepper(v, dve_step)
                    for t in range(T):
                        v.wait_ge(got_in[t], l * 32 + 32)
                        for j in range(2):
                            step(v.scalar_tensor_tensor(x[:, t, :], got[t][j], gates[:, j, t:t + 1], x[:, t, :],
                                                        ALU.mult, ALU.add))
                        v.sem_inc(s["x_added"], 1)

                @block.scalar
                def _(act):
                    step = stepper(act, act_step)
                    for t in range(T):
                        act.wait_ge(s["x_added"], t + 1)
                        root_mean_square(act, step, t)
            clear_semaphores()

        with nc.Block() as block:
            @block.sync
            def _(sp):
                sp.dma_start(out_tok, x[:, :, :]).then_inc(s["stored"], 16)
                sp.wait_ge(s["stored"], 16)


_INS = ["x", "c", "positions", "w_ada", "b_ada", "norm1", "w_in", "q_norm", "k_norm", "conv_w", "conv_b",
        "conv_ln_g", "conv_ln_b", "conv_pw_w", "conv_pw_b", "pool_w", "pool_b", "pool_scale", "sgu_ln_g",
        "sgu_ln_b", "sgu_w", "sgu_b", "out_norm", "w_out", "norm2", "w_rg", "b_rg", "w_re", "b_re", "w_gate",
        "w_up", "w_down"]


def kernel(**inputs):
    import concourse.bacc as _bacc
    from concourse.bass_utils import run_bass_kernel_spmd as _run

    arrays = {name: np.ascontiguousarray(inputs[name]) for name in _INS}
    arrays["constants"] = constants()[0]
    nc = _bacc.Bacc("TRN2", target_bir_lowering=False, num_devices=1)
    A = {name: nc.dram_tensor(f"in_{name}", a.shape, mybir.dt.from_np(a.dtype), kind="ExternalInput").ap()
         for name, a in arrays.items()}
    out = nc.dram_tensor("out_0", (1, S, D), F32, kind="ExternalOutput").ap()
    build(nc, A, out)
    r = _run(nc, [{f"in_{name}": a for name, a in arrays.items()}], core_ids=[0])
    return r.results[0]["out_0"]
```
